# Optimizing a Trainium2 kernel written in Bass

```python
import math
import jax, jax.numpy as jnp
from jax import lax
import numpy as np

D_MODEL = 1024
BATCH = 1
SEQ = 256
DEPTH = 2

N_MEM = 256
CONV_WIDTH = D_MODEL
CONV_KERNEL = 31
DIFF_HEADS = 8
DIFF_HEAD_DIM = D_MODEL // DIFF_HEADS // 2
ATTN_WIDTH = DIFF_HEADS * 2 * DIFF_HEAD_DIM
IN_COLS = 2 * CONV_WIDTH + 3 * ATTN_WIDTH + 2 * D_MODEL
Q_BLOCK = 128
ROPE_THETA = 10000.0
X_HEADS = 4
X_HEAD_DIM = D_MODEL // X_HEADS
N_GROUPS = 4
EXPERTS_PER_GROUP = 8
N_EXPERTS = N_GROUPS * EXPERTS_PER_GROUP
TOP_K = 2
EXPERT_FF = D_MODEL // 2
MOE_BLOCK = 128
RMS_EPS = 1e-6
LN_EPS = 1e-5

kernel_name = 'hybrid_conformer_diffattn_hmoe_encoder'

def rmsnorm(x, g, eps=RMS_EPS):
    xf = x.astype(jnp.float32)
    y = xf * lax.rsqrt(jnp.mean(xf * xf, axis=-1, keepdims=True) + eps)
    return (y * g.astype(jnp.float32)).astype(x.dtype)

def layernorm(x, g, b, eps=LN_EPS):
    xf = x.astype(jnp.float32)
    mu = jnp.mean(xf, axis=-1, keepdims=True)
    xc = xf - mu
    y = xc * lax.rsqrt(jnp.mean(xc * xc, axis=-1, keepdims=True) + eps)
    return (y * g.astype(jnp.float32) + b.astype(jnp.float32)).astype(x.dtype)

def rope(x, pos):
    d = x.shape[-1]
    half = d // 2
    inv_freq = jnp.exp(-math.log(ROPE_THETA) * jnp.arange(half, dtype=jnp.float32) / half)
    ang = pos.astype(jnp.float32)[..., None] * inv_freq
    cos = jnp.cos(ang)[:, :, None, :]
    sin = jnp.sin(ang)[:, :, None, :]
    xf = x.astype(jnp.float32)
    x1, x2 = xf[..., :half], xf[..., half:]
    return jnp.concatenate([x1 * cos - x2 * sin, x2 * cos + x1 * sin], axis=-1).astype(x.dtype)

def conformer_conv(a, dw, db, ln_g, ln_b, w_proj):
    c = a.shape[-1] // 2
    y = a[..., :c] * jax.nn.sigmoid(a[..., c:])
    y = lax.conv_general_dilated(
        y, dw[:, None, :].astype(y.dtype), window_strides=(1,),
        padding=[(CONV_KERNEL // 2, CONV_KERNEL // 2)],
        dimension_numbers=('NWC', 'WIO', 'NWC'),
        feature_group_count=c) + db
    y = jax.nn.silu(layernorm(y, ln_g, ln_b))
    return y @ w_proj

def diff_attention(q, k, v, pos, lam, lam_init, subln_g):
    B, S, _ = q.shape
    H, d = DIFF_HEADS, DIFF_HEAD_DIM
    q = rope(q.reshape(B, S, 2 * H, d), pos).reshape(B, S, H, 2, d)
    k = rope(k.reshape(B, S, 2 * H, d), pos).reshape(B, S, H, 2, d)
    v = v.reshape(B, S, H, 2 * d)
    scale = d ** -0.5
    nb = S // Q_BLOCK
    qb = q.reshape(B, nb, Q_BLOCK, H, 2, d).transpose(1, 0, 2, 3, 4, 5)

    def block(q_blk):
        s = jnp.einsum('bqhcd,bkhcd->bhcqk', q_blk, k).astype(jnp.float32) * scale
        p = jax.nn.softmax(s, axis=-1)
        a = p[:, :, 0] - lam * p[:, :, 1]
        return jnp.einsum('bhqk,bkhe->bqhe', a.astype(v.dtype), v)

    o = lax.map(block, qb)
    o = o.transpose(1, 0, 2, 3, 4).reshape(B, S, H, 2 * d)
    o = rmsnorm(o, subln_g, LN_EPS) * (1.0 - lam_init)
    return o.reshape(B, S, H * 2 * d)

def cross_attention(u, m, w_q, w_kv, w_o):
    B, S, D = u.shape
    q = (u @ w_q).reshape(B, S, X_HEADS, X_HEAD_DIM)
    kv = m @ w_kv
    k = kv[..., :D].reshape(B, -1, X_HEADS, X_HEAD_DIM)
    v = kv[..., D:].reshape(B, -1, X_HEADS, X_HEAD_DIM)
    s = jnp.einsum('bqhd,bkhd->bhqk', q, k).astype(jnp.float32) * (X_HEAD_DIM ** -0.5)
    p = jax.nn.softmax(s, axis=-1)
    o = jnp.einsum('bhqk,bkhd->bqhd', p.astype(v.dtype), v).reshape(B, S, D)
    return o @ w_o

def grouped_swiglu(xf, expert, w1, w3, w2):
    N, K = expert.shape
    D = xf.shape[-1]
    A = N * K
    flat_e = expert.reshape(A)
    order = jnp.argsort(flat_e).astype(jnp.int32)
    sorted_e = flat_e[order]
    counts = jnp.zeros((N_EXPERTS,), jnp.int32).at[flat_e].add(1)
    padded = ((counts + MOE_BLOCK - 1) // MOE_BLOCK) * MOE_BLOCK
    start = jnp.cumsum(counts) - counts
    pstart = jnp.cumsum(padded) - padded
    rank = jnp.arange(A, dtype=jnp.int32) - start[sorted_e]
    dest = pstart[sorted_e] + rank
    P = A + N_EXPERTS * MOE_BLOCK
    row_src = jnp.full((P,), A, jnp.int32).at[dest].set(order)
    x_pad = jnp.concatenate([xf, jnp.zeros((1, D), xf.dtype)], axis=0)
    x_rows = x_pad[row_src // K]
    nb = P // MOE_BLOCK
    block_start = jnp.arange(nb, dtype=jnp.int32) * MOE_BLOCK
    pend = pstart + padded
    block_e = jnp.minimum(jnp.searchsorted(pend, block_start, side='right'), N_EXPERTS - 1).astype(jnp.int32)

    def expert_block(args):
        xb, e = args
        hdn = jax.nn.silu(xb @ w1[e]) * (xb @ w3[e])
        return hdn @ w2[e]

    y_rows = lax.map(expert_block, (x_rows.reshape(nb, MOE_BLOCK, D), block_e)).reshape(P, D)
    y = jnp.zeros((A, D), y_rows.dtype).at[row_src].set(y_rows, mode='drop')
    return y.reshape(N, K, D)

def hier_moe(u, w_group, b_group, w_router, b_router, w1, w3, w2):
    B, S, D = u.shape
    N = B * S
    xf = u.reshape(N, D)
    g_prob = jax.nn.softmax((xf @ w_group).astype(jnp.float32) + b_group.astype(jnp.float32), axis=-1)
    g_w, g_sel = lax.top_k(g_prob, 1)
    e_logits = ((xf @ w_router).astype(jnp.float32) + b_router.astype(jnp.float32)).reshape(N, N_GROUPS, EXPERTS_PER_GROUP)
    e_logits = jnp.take_along_axis(e_logits, g_sel[:, :, None], axis=1)[:, 0]
    top_v, top_i = lax.top_k(e_logits, TOP_K)
    weights = g_w * jax.nn.softmax(top_v, axis=-1)
    expert = (g_sel * EXPERTS_PER_GROUP + top_i).astype(jnp.int32)
    y = grouped_swiglu(xf, expert, w1, w3, w2)
    out = jnp.einsum('nkd,nk->nd', y, weights.astype(y.dtype))
    return out.reshape(B, S, D)

def setup_inputs(seed: int = 0) -> dict:
    key = jax.random.key(seed)
    ks = iter(jax.random.split(key, 40))

    def w(shape, fan_in):
        return jax.random.normal(next(ks), shape, jnp.float32) * (fan_in ** -0.5)

    def gain(shape):
        return 1.0 + 0.02 * jax.random.normal(next(ks), shape, jnp.float32)

    def small(shape, s):
        return s * jax.random.normal(next(ks), shape, jnp.float32)

    L, D = DEPTH, D_MODEL
    return {
        'x': jax.random.normal(next(ks), (BATCH, SEQ, D), jnp.float32),
        'mem': jax.random.normal(next(ks), (BATCH, N_MEM, D), jnp.float32),
        'positions': jnp.broadcast_to(jnp.arange(SEQ, dtype=jnp.int32), (BATCH, SEQ)),
        'norm_mix_g': gain((L, D)),
        'w_in': w((L, D, IN_COLS), D),
        'conv_dw': w((L, CONV_KERNEL, CONV_WIDTH), CONV_KERNEL),
        'conv_db': small((L, CONV_WIDTH), 0.02),
        'conv_ln_g': gain((L, CONV_WIDTH)),
        'conv_ln_b': small((L, CONV_WIDTH), 0.02),
        'w_conv_out': w((L, CONV_WIDTH, D), CONV_WIDTH),
        'lam_q1': small((L, DIFF_HEAD_DIM), 0.1),
        'lam_k1': small((L, DIFF_HEAD_DIM), 0.1),
        'lam_q2': small((L, DIFF_HEAD_DIM), 0.1),
        'lam_k2': small((L, DIFF_HEAD_DIM), 0.1),
        'subln_g': gain((L, 2 * DIFF_HEAD_DIM)),
        'w_attn_out': w((L, ATTN_WIDTH, D), ATTN_WIDTH),
        'w_out': w((L, D, D), D),
        'norm_mem_g': gain((L, D)),
        'norm_x_g': gain((L, D)),
        'w_xq': w((L, D, D), D),
        'w_xkv': w((L, D, 2 * D), D),
        'w_xo': w((L, D, D), D),
        'norm_ffn_g': gain((L, D)),
        'w_group': w((L, D, N_GROUPS), D),
        'b_group': small((L, N_GROUPS), 0.01),
        'w_router': w((L, D, N_EXPERTS), D),
        'b_router': small((L, N_EXPERTS), 0.01),
        'w1': w((L, N_EXPERTS, D, EXPERT_FF), D),
        'w3': w((L, N_EXPERTS, D, EXPERT_FF), D),
        'w2': w((L, N_EXPERTS, EXPERT_FF, D), EXPERT_FF),
        'final_norm_g': gain((D,)),
    }

def reference(x, mem, positions, norm_mix_g, w_in, conv_dw, conv_db, conv_ln_g, conv_ln_b,
              w_conv_out, lam_q1, lam_k1, lam_q2, lam_k2, subln_g, w_attn_out, w_out,
              norm_mem_g, norm_x_g, w_xq, w_xkv, w_xo, norm_ffn_g, w_group, b_group,
              w_router, b_router, w1, w3, w2, final_norm_g):
    h = x
    c0 = 2 * CONV_WIDTH
    c1 = c0 + ATTN_WIDTH
    c2 = c1 + ATTN_WIDTH
    c3 = c2 + ATTN_WIDTH
    for i in range(DEPTH):
        u = rmsnorm(h, norm_mix_g[i])
        proj = u @ w_in[i]
        y_conv = conformer_conv(proj[..., :c0], conv_dw[i], conv_db[i],
                                conv_ln_g[i], conv_ln_b[i], w_conv_out[i])
        lam_init = 0.8 - 0.6 * math.exp(-0.3 * i)
        lam = (jnp.exp(jnp.sum(lam_q1[i].astype(jnp.float32) * lam_k1[i].astype(jnp.float32)))
               - jnp.exp(jnp.sum(lam_q2[i].astype(jnp.float32) * lam_k2[i].astype(jnp.float32)))
               + lam_init)
        y_attn = diff_attention(proj[..., c0:c1], proj[..., c1:c2], proj[..., c2:c3],
                                positions, lam, lam_init, subln_g[i]) @ w_attn_out[i]
        gates = jax.nn.sigmoid(proj[..., c3:])
        merged = gates[..., :D_MODEL] * y_conv + gates[..., D_MODEL:] * y_attn
        h = h + merged @ w_out[i]
        m = rmsnorm(mem, norm_mem_g[i])
        h = h + cross_attention(rmsnorm(h, norm_x_g[i]), m, w_xq[i], w_xkv[i], w_xo[i])
        h = h + hier_moe(rmsnorm(h, norm_ffn_g[i]), w_group[i], b_group[i], w_router[i],
                         b_router[i], w1[i], w3[i], w2[i])
    return rmsnorm(h, final_norm_g)


_drawn_inputs = setup_inputs


def setup_inputs(seed=0):
    import zlib

    import numpy as np

    out = dict(_drawn_inputs(seed))
    spreads = {}
    factors = {'norm_x_g': 5.616, 'b_group': 3.303, 'final_norm_g': 2.925}
    for name, (base, spread) in spreads.items():
        noise = np.random.default_rng([zlib.crc32(name.encode()), seed]).standard_normal(out[name].shape)
        drawn = base * np.exp(spread * noise) if base else spread * noise
        out[name] = __import__('jax').numpy.asarray(drawn.astype(out[name].dtype))
    for name, factor in factors.items():
        out[name] = (out[name] * factor).astype(out[name].dtype)
    return out
```

```python
import math
from contextlib import ExitStack

import numpy as np

import concourse.bass as bass
from concourse import mybir

P = 128
F32 = mybir.dt.float32
I32 = mybir.dt.int32
ALU = mybir.AluOpType
ACT = mybir.ActivationFunctionType
AX = mybir.AxisListType

LAYERS = 2
T = 256
TT = T // P
D = 1024
DC = D // P
KERN = 31
PAD = KERN // 2
HEADS = 8
HALF = 32
XHEADS = 4
GROUPS = 4
PER_GROUP = 8
EXPERTS = GROUPS * PER_GROUP
FF = D // 2
FC = FF // P
SLAB = 512
RING = 6
PAIRS = EXPERTS // 2
CAP = 32
MAX_PASSES = T // CAP
HALVES = D // SLAB

R_DB, R_LNG, R_LNB, R_MIX, R_MEM, R_X, R_FFN = range(KERN, KERN + 7)
ROWS = KERN + 7
NR = GROUPS + EXPERTS
K_WR = DC * ROWS
K_RB = K_WR + DC * NR
K_SUB = K_RB + NR
K_LAM = K_SUB + 1
NPK = K_LAM + 1

C_ID = 0
C_ROT = C_ID + P
C_TRI = C_ROT + P
C_MEAN = C_TRI + P
C_IOTA = C_MEAN + P
C_THR = C_IOTA + CAP
C_DESC = C_THR + MAX_PASSES - 1
C_INVF = C_DESC + EXPERTS
C_MLO = C_INVF + 1
C_MHI = C_MLO + 1
C_LAM = C_MHI + 1
C_OML = C_LAM + LAYERS
NCON = C_OML + LAYERS

RMS_EPS = 1e-6
LN_EPS = 1e-5
TWO_PI = (6.28125, 0.0019350051879882812, 3.019916e-07)
MAGIC = 12582912.0
SIN_MAX = 3.1415925

SLABS = ["a0", "g0", "a1", "g1", "q0", "q1", "k0", "k1", "v0", "v1", "gc0", "gc1", "ga0", "ga1",
         "xk0", "xk1", "ao0", "ao1", "co0", "co1", "xv0", "wo0", "wo1", "xv1", "xq0", "xq1", "xo0", "xo1"]
DENSE_ROUNDS = -(-len(SLABS) // RING)

TURN = 4


def pairs(name):
    return [f"{name}{j}" for j in range(4)]


ATTN_STEPS = HEADS * TT
JOBS = (pairs("nm") + ["a.0", "a.1", "g.0", "g.1", "a.2", "a.3", "g.2", "g.3"] + pairs("q.") + pairs("k.")
        + pairs("v."))
for _j in range(ATTN_STEPS // 2):
    JOBS += [f"gate.{_j}"]
    if _j == 0:
        JOBS += ["mean"]
    if _j == 3:
        JOBS += ["var"]
JOBS += ["xk.0", "xk.1"] + pairs("oT") + ["xk.2", "xk.3"] + pairs("ao.") + pairs("co.") + ["xv.0", "xv.1"]
JOBS += pairs("wo.") + ["xv.2", "xv.3"] + pairs("nx") + pairs("xq.") + pairs("px") + pairs("xo.") + pairs("nf")
JOBS += ["router", "rank"]


def banks_of_jobs():
    where, used, last = {}, [0] * TURN, -1
    for job in JOBS:
        n = TURN // 2 if job.startswith(("gate", "mean", "var")) else TURN
        last = (last + 1) % n
        used[last] += 1
        where[job] = (last, used[last])
    return where


WHERE = banks_of_jobs()


def bank(job):
    return WHERE[job][0]


def turn(job):
    return WHERE[job][1]


def score_banks(s):
    return 2 + 2 * (s % 2)


ROPE_BANK = 5
VALUE_BANK = 6
MIX_BANK = 7


class Chain:

    def __init__(self, eng, sem):
        self.eng, self.sem, self.n = eng, sem, 0

    def note(self, ins):
        ins.then_inc(self.sem, 1)
        self.n += 1
        return self.n

    def after(self, n):
        self.eng.wait_ge(self.sem, n)

    def link(self, ins):
        self.after(self.note(ins))


def constants():
    c = np.zeros((P, NCON), np.float32)
    p = np.arange(P)
    c[:, C_ID:C_ID + P] = np.eye(P)
    for b in range(0, P, 2 * HALF):
        for d in range(HALF):
            c[b + HALF + d, C_ROT + b + d] = -1.0
            c[b + d, C_ROT + b + HALF + d] = 1.0
    c[:, C_TRI:C_TRI + P] = (p[:, None] < p[None, :]) / D
    c[:, C_MEAN:C_MEAN + P] = 1.0 / D
    c[:, C_IOTA:C_IOTA + CAP] = np.arange(CAP)
    c[:, C_THR:C_THR + MAX_PASSES - 1] = CAP * np.arange(1, MAX_PASSES)
    c[:, C_DESC:C_DESC + EXPERTS] = EXPERTS - np.arange(EXPERTS)
    step = np.float32(-math.log(10000.0))
    c[:, C_INVF] = np.exp(step * (p % HALF).astype(np.float32) / np.float32(HALF))
    c[:, C_MLO] = (p // CAP) % 2 == 0
    c[:, C_MHI] = (p // CAP) % 2 == 1
    for i in range(LAYERS):
        c[:, C_LAM + i] = 0.8 - 0.6 * math.exp(-0.3 * i)
        c[:, C_OML + i] = 1.0 - (0.8 - 0.6 * math.exp(-0.3 * i))
    return c


def encoder(nc, consts, x, mem, positions, norm_mix_g, w_in, conv_dw, conv_db, conv_ln_g, conv_ln_b, w_conv_out,
            lam_q1, lam_k1, lam_q2, lam_k2, subln_g, w_attn_out, w_out, norm_mem_g, norm_x_g, w_xq, w_xkv, w_xo,
            norm_ffn_g, w_group, b_group, w_router, b_router, w1, w3, w2, final_norm_g, out):
    mem_t_dram = nc.dram_tensor("mem_t_scratch", (LAYERS, P, DC * T), F32, kind="Internal").ap()

    with ExitStack() as ctx:
        def sb(name, shape, dt=F32):
            return ctx.enter_context(nc.sbuf_tensor(name, shape, dt))

        def sem(name):
            return ctx.enter_context(nc.semaphore(name))

        ring = sb("ring", [P, RING, DC * SLAB])
        h = sb("h", [P, TT, D])
        uT = sb("uT", [P, DC, T])
        glu_pad = sb("glu_pad", [P, DC, T + 2 * PAD + 2])
        big = sb("big", [P, 7, DC * T])
        memT = sb("memT", [P, DC, T])
        cst = sb("cst", [P, NCON])
        pk = sb("pk", [P, LAYERS, NPK])
        cur = sb("cur", [P, NPK])
        rope_cs = sb("rope_cs", [P, 2, T])
        work = sb("work", [P, 2304])
        small = sb("small", [P, 224])
        rs_ln = sb("rs_ln", [P, T])
        npass_i = sb("npass_i", [P, 1], I32)
        ps = ctx.enter_context(nc.psum_tensor("ps", [P, 8, SLAB], F32))

        def chunks(i):
            return big[:, i, :].rearrange("p (c t) -> p c t", c=DC)

        def rows(i):
            return big[:, i, :].rearrange("p (s d) -> p s d", s=TT)

        glu = glu_pad[:, :, PAD:PAD + T]
        sq = glu
        xkT = glu
        conv = chunks(0)
        xT = chunks(0)
        qT = chunks(1)
        oT = chunks(1)
        kT = chunks(2)
        merged = chunks(2)
        v = rows(3)
        xv = rows(3)
        gate_c = chunks(4)
        xqT = chunks(4)
        gate_a = chunks(5)
        xoT = chunks(5)
        o_all = big[:, 6, :].rearrange("p (s e) -> p s e", s=ATTN_STEPS)
        uN = rows(6)
        memN = rows(6)

        ident = cst[:, C_ID:C_ID + P]
        rot = cst[:, C_ROT:C_ROT + P]
        tri = cst[:, C_TRI:C_TRI + P]
        mean_m = cst[:, C_MEAN:C_MEAN + P]
        iota = cst[:, C_IOTA:C_IOTA + CAP]
        par = cur[:, 0:K_WR].rearrange("p (c r) -> p c r", c=DC)
        wr = cur[:, K_WR:K_RB].rearrange("p (c n) -> p c n", c=DC)
        rb = cur[:, K_RB:K_SUB]
        sub_col = cur[:, K_SUB:K_SUB + 1]
        neglam = cur[:, K_LAM:K_LAM + 1]

        def wk(at, *shape):
            n = int(np.prod(shape))
            a = work[:, at:at + n]
            if len(shape) == 1:
                return a
            names = "abcd"[:len(shape)]
            return a.rearrange(f"p ({' '.join(names)}) -> p {' '.join(names)}",
                               **{k: s for k, s in zip(names[:-1], shape[:-1])})

        sg = wk(0, 2, 2, T)
        qraw = wk(0, 2, 2, T)
        rt1 = wk(1024, 2, T)
        rt2 = wk(1536, 2, T)
        E = wk(0, 2, 2, T)
        amix = wk(1024, 2, T)
        aTs = wk(1536, 2, T)
        etmp = wk(2048, T)
        pT = wk(1024, 2, 2 * T)
        nmx = small[:, 0:32].rearrange("p (s c) -> p s c", s=ATTN_STEPS)
        sm = small[:, 32:64].rearrange("p (s c) -> p s c", s=ATTN_STEPS)
        ssq = small[:, 66:82]
        ss = small[:, 82:84]
        xnm = small[:, 84:92].rearrange("p (s c) -> p s c", s=XHEADS)
        xsm = small[:, 92:100].rearrange("p (s c) -> p s c", s=XHEADS)
        cnt1 = small[:, 100:101]
        thr7 = small[:, 101:108]

        rbuf = big[:, 2, :]
        roff = [0]

        def rt(*shape):
            n = int(np.prod(shape))
            a = rbuf[:, roff[0]:roff[0] + n]
            roff[0] += n
            if len(shape) == 1:
                return a
            names = "abcd"[:len(shape)]
            return a.rearrange(f"p ({' '.join(names)}) -> p {' '.join(names)}",
                               **{k: s for k, s in zip(names[:-1], shape[:-1])})

        logit = rt(TT, NR)
        m_g = rt(TT)
        d_g = rt(TT, GROUPS)
        e_g = rt(TT, GROUPS)
        g_w = rt(TT)
        eq_g = rt(TT, GROUPS)
        oh_g = rt(TT, GROUPS)
        mx_g = rt(TT)
        masked = rt(TT, EXPERTS)
        top1 = rt(TT)
        top2 = rt(TT)
        first = rt(TT, EXPERTS)
        mx_e = rt(TT)
        oh1 = rt(TT, EXPERTS)
        oh2 = rt(TT, EXPERTS)
        gap = rt(TT)
        e_gap = rt(TT)
        w_1 = rt(TT)
        w_2 = rt(TT)
        tok_w = rt(TT, EXPERTS)
        tok_w2 = rt(TT, EXPERTS)
        picked = rt(TT, EXPERTS)
        rank = rt(TT, EXPERTS)
        roff[0] = 0
        rbuf = big[:, 3, :]
        sel = rt(TT, 2, CAP)
        spread = rt(TT, 2, 2, CAP)
        xe = rt(DC, 2 * CAP)
        up_t = rt(FC, 2, CAP)
        rbuf = big[:, 4, :]
        roff[0] = 0
        y_sb = rt(SLAB)
        scat = rt(2, T)
        up_sb = rt(SLAB)
        silu_t = rt(FC, 2, CAP)

        landed = [sem(f"slab_landed_{i}") for i in range(RING)]
        freed = sem("slab_freed")
        cst_in, x_in, par_in, pos_in, mem_in = (sem(n) for n in ("consts_in", "x_in", "params_in", "pos_in", "mem_in"))
        st_rows, st_pk, st_mss, st_mvar, st_msq, st_mn, st_mt, st_mg, st_msto = (sem("setup_" + n) for n in (
            "rows_turned", "params_packed", "mem_squares", "mem_variance", "mem_root", "mem_normed", "mem_turned",
            "mem_scaled", "mem_stored"))
        st_ang, st_cs, st_dot, st_exp, st_ch = (sem("setup_" + n) for n in (
            "angles", "sincos", "lambda_dots", "lambda_exps", "vector_chain"))
        mt_in = sem("mem_t_in")
        layer_end, layer_go = sem("layer_end"), sem("layer_go")
        np_ready, np_seen = sem("passes_ready"), sem("passes_seen")
        layer_clear = sem("layer_clear")
        sel_ready, spread_ready, xg_done, gt_done, xe_ready, scat_ready, up_done, up_out, upt_done, silu_ready, \
            upt_ready, y_done, y_out, added = (sem("moe_" + n) for n in (
                "select_ready", "spread_ready", "gathered", "spread_turned", "tokens_ready", "scatter_ready",
                "up_done", "up_out", "up_turned", "silu_ready", "hidden_ready", "down_done", "down_out", "added"))
        h_back = sem("moe_residual_back")
        fin_g, fin_ss, fin_var, fin_sq, fin_ch, fin_out, out_done = (sem("final_" + n) for n in (
            "gain_in", "squares", "variance", "root", "chain", "rows_ready", "stored"))

        first_sem = sem("bank_full_0")
        full = [first_sem] + [sem(f"bank_full_{b}") for b in range(1, TURN)]
        free = [sem(f"bank_free_{b}") for b in range(TURN)]
        dch, ach = sem("vector_chain"), sem("scalar_chain")
        cur_ready = sem("layer_params_ready")
        n_ss, n_var, n_root, n_ready, n_turned = (sem("norm_" + n) for n in (
            "squares", "variance", "root", "rows_ready", "columns_ready"))
        sig_ready, glu_ready = sem("glu_sigmoid_ready"), sem("glu_ready")
        conv_ready, ln_xc, ln_sq, ln_var, ln_root, ln_y, ln_out = (sem(n) for n in (
            "conv_ready", "ln_centred", "ln_squared", "ln_variance", "ln_root", "ln_scaled", "ln_silu_ready"))
        qraw_ready, rope_full, rope_ready = sem("rope_raw_ready"), sem("rope_turned"), sem("rope_ready")
        v_ready = sem("v_ready")
        s_full, nm_ready, exp_ready, a_ready, at_full, at_ready, pv_full, o_ready = (sem("attn_" + n) for n in (
            "scores", "max_ready", "exp_ready", "mix_ready", "mix_turned", "mix_columns", "values", "rows_out"))
        gate_raw, gate_ready, o_var, o_root, o_norm, oT_ready = (sem(n) for n in (
            "gates_raw", "gates_ready", "subln_variance", "subln_root", "subln_ready", "attn_columns_ready"))
        xk_ready, xv_ready, merged_ready, h_ready, xq_ready = (sem(n) for n in (
            "xk_ready", "xv_ready", "merged_ready", "h_ready", "xq_ready"))
        xs_full, xnm_ready, xexp_ready, xp_ready, xt_full, xt_ready, xo_ready = (sem("cross_" + n) for n in (
            "scores", "max_ready", "exp_ready", "probs_ready", "probs_turned", "probs_columns", "columns_ready"))
        r_diff, r_exp, r_gap, r_gexp, r_mask, rank_ready = (sem("router_" + n) for n in (
            "group_diff", "group_exp", "gap", "gap_exp", "picked", "rank_ready"))
        last_sem = rank_ready
        cleared = range(first_sem.num, last_sem.num + 1)

        block = ctx.enter_context(nc.Block())

        def slab_source(name, L):
            kind, half = name[:-1], int(name[-1])
            c = {"a": 0, "g": D, "q": 2 * D, "k": 3 * D, "v": 4 * D, "gc": 5 * D, "ga": 6 * D}
            if kind in c:
                w, c0 = w_in, c[kind]
            elif kind in ("xk", "xv"):
                w, c0 = w_xkv, D * (kind == "xv")
            else:
                w, c0 = {"co": w_conv_out, "ao": w_attn_out, "wo": w_out, "xq": w_xq, "xo": w_xo}[kind], 0
            c0 += half * SLAB
            return w[L, :, c0:c0 + SLAB].rearrange("(c p) n -> p c n", p=P)

        def slot(j):
            return ring[:, j, :].rearrange("p (c n) -> p c n", c=DC)

        @block.sync
        def _(sp):
            rnd = sp.alloc_register("sp_round")
            sp.reg_mov(rnd, 0)

            def experts(L, i):
                r = sp.snap(rnd)
                srcs = [w1[L, 2 * i], w3[L, 2 * i], w1[L, 2 * i + 1], w3[L, 2 * i + 1], w2[L, 2 * i], w2[L, 2 * i + 1]]
                for j, s in enumerate(srcs):
                    sp.wait_ge(freed, r * RING + (j + 1))
                    sp.dma_start(ring[:, j, :].rearrange("p (c n) -> p c n", c=DC if j < 4 else FC),
                                 s.rearrange("(c p) n -> p c n", p=P)).then_inc(landed[j], 16)
                sp.reg_add(rnd, rnd, 1)

            with sp.Fori(0, LAYERS) as L:
                r = sp.snap(rnd)
                for n, name in enumerate(SLABS):
                    sp.wait_ge(freed, r * RING + (n + 1))
                    sp.dma_start(slot(n % RING), slab_source(name, L)).then_inc(landed[n % RING], 16)
                for n in range(len(SLABS), DENSE_ROUNDS * RING):
                    sp.wait_ge(freed, r * RING + (n + 1))
                    sp.sem_inc(landed[n % RING], 16)
                sp.reg_add(rnd, rnd, DENSE_ROUNDS)
                with sp.Fori(0, PAIRS) as i:
                    experts(L, i)
                sp.wait_ge(np_ready, L + 1)
                sp.sem_inc(np_seen, 1)
                passes = sp.value_load(npass_i[0:1, 0:1], min_val=1, max_val=MAX_PASSES)
                with sp.If(passes > 1):
                    with sp.Fori(1, passes) as _p:
                        with sp.Fori(0, PAIRS) as i:
                            experts(L, i)
                    sp.nop()
                sp.nop()
            for s in range(TT):
                sp.wait_ge(fin_out, s + 1)
                sp.dma_start(out[0, s * P:(s + 1) * P, :], uN[:, s, :]).then_inc(out_done, 16)
            sp.wait_ge(out_done, 16 * TT)

        @block.gpsimd
        def _(pool):
            pool.dma_start(memN, mem[0].rearrange("(s p) d -> p s d", p=P)).then_inc(mem_in, 16)
            with pool.Fori(0, LAYERS) as L:
                pool.wait_ge(st_msto, 16)
                pool.dma_start(memT[:], mem_t_dram[L].rearrange("p (c t) -> p c t", c=DC)).then_inc(mt_in, 16)
                pool.wait_ge(mt_in, L * 16 + 16)
                pool.sem_inc(layer_end, 1)
                pool.wait_ge(layer_go, L + 1)
            pool.dma_start(memT[:, 0:FC, :].rearrange("p c t -> p (c t)"),
                           final_norm_g.partition_broadcast(P)).then_inc(fin_g, 16)
            pool.wait_ge(fin_g, 16)

        @block.scalar
        def _(act):
            act.dma_start(cst[:], consts).then_inc(cst_in, 16)
            act.dma_start(work[:, 0:T].bitcast(I32), positions[0].partition_broadcast(P)).then_inc(pos_in, 16)
            prow = big[:, 0, :].rearrange("p (l d) -> p l d", l=LAYERS)
            n_par = 0
            for src, r0, r1 in ((conv_dw.rearrange("l k d -> k l d"), 0, KERN), (conv_db, R_DB, R_DB + 1),
                                (conv_ln_g, R_LNG, R_LNG + 1), (conv_ln_b, R_LNB, R_LNB + 1),
                                (norm_mix_g, R_MIX, R_MIX + 1), (norm_mem_g, R_MEM, R_MEM + 1),
                                (norm_x_g, R_X, R_X + 1), (norm_ffn_g, R_FFN, R_FFN + 1)):
                s = src if r1 - r0 > 1 else src.rearrange("(o l) d -> o l d", o=1)
                act.dma_start(prow[r0:r1], s).then_inc(par_in, 16)
                n_par += 1
            act.dma_start(h[:], x[0].rearrange("(s p) d -> p s d", p=P)).then_inc(x_in, 16)
            for i in range(LAYERS):
                wrl = pk[:, i, K_WR:K_RB].rearrange("p (c n) -> p c n", c=DC)
                act.dma_start(wrl[:, :, 0:GROUPS], w_group[i].rearrange("(c p) n -> p c n", p=P)).then_inc(par_in, 16)
                act.dma_start(wrl[:, :, GROUPS:NR], w_router[i].rearrange("(c p) n -> p c n", p=P)).then_inc(par_in, 16)
                act.dma_start(pk[:, i, K_RB:K_RB + GROUPS], b_group[i].partition_broadcast(P)).then_inc(par_in, 16)
                act.dma_start(pk[:, i, K_RB + GROUPS:K_SUB], b_router[i].partition_broadcast(P)).then_inc(par_in, 16)
                act.dma_start(pk[:, i, K_SUB:K_SUB + 1], subln_g[i].rearrange("(p o) -> p o", o=1)).then_inc(par_in, 16)
                for j, lv in enumerate((lam_q1, lam_k1, lam_q2, lam_k2)):
                    act.dma_start(work[:, 1024 + (i * 4 + j) * 64:1024 + (i * 4 + j + 1) * 64],
                                  lv[i].partition_broadcast(P)).then_inc(par_in, 16)
            act.wait_ge(mem_in, 16)
            for s in range(TT):
                act.activation(uT[:, s * FC:(s + 1) * FC, :].rearrange("p c t -> p (c t)"), memN[:, s, :], ACT.Square,
                               accum_out=ss[:, s:s + 1]).then_inc(st_mss, 1)
            act.wait_ge(st_mvar, 1)
            act.activation(ss, ss, ACT.Sqrt).then_inc(st_msq, 1)
            act.wait_ge(st_ang, 1)
            act.activation(rope_cs[:], wk(512, 2, T), ACT.Sin).then_inc(st_cs, 1)
            act.wait_ge(st_dot, 1)
            act.activation(small[:, 108:112], small[:, 104:108], ACT.Exp).then_inc(st_exp, 1)
            act.wait_ge(st_mg, 4)
            act.dma_start(mem_t_dram.rearrange("l p f -> p l f"), big[:, 1:3, :]).then_inc(st_msto, 16)

            q = act.alloc_register("act_pass")
            act.reg_mov(q, 0)
            u = act.alloc_register("act_unit")
            act.reg_mov(u, 0)

            def evac(job, dst, func=ACT.Copy, scale=1.0):
                b = bank(job)
                act.wait_ge(full[b], turn(job))
                src = ps[:, b, :]
                if len(dst.shape) == 3:
                    src = src.rearrange("p (c t) -> p c t", c=2)
                return act.activation(dst, src, func, scale=scale)

            act.wait_ge(x_in, 16)
            with act.Fori(0, LAYERS) as L:
                ch = Chain(act, ach)

                def squares(n):
                    for s in range(TT):
                        if n > 0:
                            act.wait_ge(h_ready, 4 * (n - 1) + 2 * (s + 1))
                        act.activation(uN[:, s, :], h[:, s, :], ACT.Square,
                                       accum_out=ss[:, s:s + 1]).then_inc(n_ss, 1)
                    act.wait_ge(n_var, n + 1)
                    act.activation(ss, ss, ACT.Sqrt).then_inc(n_root, 1)

                def turned(kind, dst, row):
                    for j in (1, 3):
                        b = bank(f"{kind}{j}")
                        act.wait_ge(full[b], turn(f"{kind}{j}"))
                        for c in range(2):
                            ins = act.activation(dst[:, 2 * j + c, :], ps[:, b, c * T:(c + 1) * T], ACT.Copy,
                                                 scale=par[:, 2 * j + c, row:row + 1])
                            if c == 0:
                                ins.then_inc(n_turned, 1)
                            else:
                                ins.then_inc(free[b], 1)

                def out(job, dst, ready, n, func=ACT.Copy, scale=1.0):
                    evac(job, dst, func, scale).then_inc(ready, 1)
                    act.wait_ge(ready, n)
                    act.sem_inc(free[bank(job)], 1)

                squares(0)
                act.wait_ge(cur_ready, 1)
                turned("nm", uT, R_MIX)
                for j in range(4):
                    if j >= 2:
                        act.wait_ge(glu_ready, j - 1)
                    out(f"g.{j}", sg[:, j % 2].rearrange("p c t -> p (c t)"), sig_ready, j + 1, ACT.Sigmoid)
                for j in range(8):
                    if j >= 2:
                        act.wait_ge(rope_ready, j - 1)
                    else:
                        act.wait_ge(glu_ready, 4)
                    job = f"q.{j}" if j < 4 else f"k.{j - 4}"
                    out(job, qraw[:, j % 2].rearrange("p c t -> p (c t)"), qraw_ready, j + 1,
                        scale=0.125 if j < 4 else 1.0)
                for j in range(4):
                    out(f"v.{j}", v[:, j % 2, (j // 2) * SLAB:(j // 2 + 1) * SLAB], v_ready, j + 1)
                act.wait_ge(rope_ready, 8)
                for s in range(ATTN_STEPS + 1):
                    if s < ATTN_STEPS:
                        act.wait_ge(nm_ready, s + 1)
                        if s >= 2:
                            act.wait_ge(a_ready, s - 1)
                        for c in range(2):
                            ins = act.activation(E[:, s % 2, c, :], ps[:, score_banks(s) + c, 0:T], ACT.Exp,
                                                 bias=nmx[:, s, c:c + 1], accum_out=sm[:, s, c:c + 1])
                            ins.then_inc(exp_ready, 1)
                    if s >= 1:
                        act.wait_ge(at_full, s)
                        act.activation(aTs[:, (s - 1) % 2, :], ps[:, MIX_BANK, 0:T], ACT.Copy).then_inc(at_ready, 1)
                    if s >= 5 and s % 4 == 1 or s == ATTN_STEPS:
                        if s == ATTN_STEPS:
                            g = ATTN_STEPS // 4 - 1
                        else:
                            g = (s - 5) // 4
                        act.wait_ge(pv_full, g + 1)
                        act.activation(o_all[:, 4 * g:4 * g + 4, :].rearrange("p s e -> p (s e)"), ps[:, VALUE_BANK, :],
                                       ACT.Copy).then_inc(o_ready, 1)
                    if s == 6:
                        act.wait_ge(ln_xc, 1)
                        act.activation(sq, conv, ACT.Square).then_inc(ln_sq, 1)
                act.wait_ge(ln_var, 1)
                act.activation(rs_ln[:], rs_ln[:], ACT.Sqrt).then_inc(ln_root, 1)
                act.wait_ge(o_var, 1)
                act.activation(ssq, ssq, ACT.Sqrt).then_inc(o_root, 1)
                for j, g in enumerate((gate_c, gate_a)):
                    act.wait_ge(gate_raw, 4 * (j + 1))
                    act.activation(g, g, ACT.Sigmoid).then_inc(gate_ready, 1)
                for j in range(2):
                    out(f"xk.{j}", xkT[:, 2 * j:2 * j + 2, :], xk_ready, j + 1)
                act.wait_ge(ln_y, 1)
                for c in range(DC):
                    act.activation(conv[:, c, :], conv[:, c, :], ACT.Silu, bias=par[:, c, R_LNB:R_LNB + 1],
                                   scale=par[:, c, R_LNG:R_LNG + 1]).then_inc(ln_out, 1)
                for j in range(2, 4):
                    out(f"xk.{j}", xkT[:, 2 * j:2 * j + 2, :], xk_ready, j + 1)
                for j in range(2):
                    out(f"xv.{j}", xv[:, j % 2, 0:SLAB], xv_ready, j + 1)
                squares(1)
                for j in range(2, 4):
                    out(f"xv.{j}", xv[:, j % 2, SLAB:2 * SLAB], xv_ready, j + 1)
                turned("nx", xT, R_X)

                def xexp(hd):
                    act.wait_ge(xnm_ready, hd + 1)
                    for s in range(TT):
                        act.activation(E[:, hd % 2, s, :], ps[:, 4 + hd % 2, s * T:(s + 1) * T], ACT.Exp,
                                       bias=xnm[:, hd, s:s + 1], accum_out=xsm[:, hd, s:s + 1]).then_inc(xexp_ready, 1)

                def xturn(hd):
                    act.wait_ge(xt_full, hd + 1)
                    act.activation(pT[:, hd % 2, :], ps[:, 6 + hd % 2, :], ACT.Copy).then_inc(xt_ready, 1)

                def xq_out(j):
                    out(f"xq.{j}", xqT[:, 2 * j:2 * j + 2, :].rearrange("p c t -> p (c t)"), xq_ready, j + 1,
                        scale=1.0 / 16)

                xq_out(0)
                xq_out(1)
                xq_out(2)
                xexp(0)
                xq_out(3)
                xexp(1)
                xturn(0)
                xexp(2)
                xturn(1)
                xexp(3)
                xturn(2)
                xturn(3)
                squares(2)
                turned("nf", uT, R_FFN)
                act.wait_ge(r_diff, 1)
                act.activation(e_g, d_g, ACT.Exp).then_inc(r_exp, 1)
                act.wait_ge(r_gap, 1)
                act.activation(e_gap, gap, ACT.Exp).then_inc(r_gexp, 1)

                act.wait_ge(rank_ready, 1)
                passes = act.value_load(npass_i[0:1, 0:1], min_val=1, max_val=MAX_PASSES)
                with act.Fori(0, passes) as _p:
                    with act.Fori(0, PAIRS) as _i:
                        n = act.snap(u)
                        act.wait_ge(gt_done, n + 1)
                        act.activation(scat[:, 0, :], ps[:, 2, 0:T], ACT.Copy, scale=cst[:, C_MLO:C_MLO + 1])
                        act.activation(scat[:, 1, :], ps[:, 2, 0:T], ACT.Copy,
                                       scale=cst[:, C_MHI:C_MHI + 1]).then_inc(scat_ready, 1)
                        act.wait_ge(up_done, n + 1)
                        act.activation(up_sb, ps[:, 1, :], ACT.Copy).then_inc(up_out, 1)
                        act.wait_ge(upt_done, n + 1)
                        a4 = ps[:, 2, :].rearrange("p (f e w s) -> p f e w s", f=FC, e=2, w=2)
                        act.activation(silu_t, a4[:, :, :, 0, :], ACT.Silu).then_inc(silu_ready, 1)
                        act.reg_add(u, u, 1)
                    n = act.snap(u)
                    k = act.snap(q)
                    act.wait_ge(added, n)
                    act.activation(h[:, 1, :], ps[:, 6:8, :].rearrange("p b n -> p (b n)"), ACT.Copy).then_inc(h_back, 1)
                    act.wait_ge(h_back, k * 2 + 2)
                    act.reg_add(q, q, 1)
                act.drain().then_inc(layer_end, 1)
                act.wait_ge(layer_go, L + 1)
            for s in range(TT):
                act.activation(uT[:, s * FC:(s + 1) * FC, :].rearrange("p c t -> p (c t)"), h[:, s, :], ACT.Square,
                               accum_out=ss[:, s:s + 1]).then_inc(fin_ss, 1)
            act.wait_ge(fin_var, 1)
            act.activation(ss, ss, ACT.Sqrt).then_inc(fin_sq, 1)

        @block.vector
        def _(dve):
            sc = Chain(dve, st_ch)
            prow_n = 8 + LAYERS * 9
            dve.memset(glu_pad[:], 0.0)
            dve.wait_ge(st_mss, TT)
            dve.tensor_scalar(ss, ss, 1.0 / D, RMS_EPS, ALU.mult, ALU.add).then_inc(st_mvar, 1)
            dve.wait_ge(pos_in, 16)
            dve.wait_ge(cst_in, 16)
            posf = wk(256, T)
            ang, turns, red = posf, wk(512, 2, T), wk(512, 2, T)
            sc.link(dve.tensor_copy(posf, work[:, 0:T].bitcast(I32)))
            sc.link(dve.tensor_scalar(ang, posf, cst[:, C_INVF:C_INVF + 1], None, ALU.mult))
            kk = rt2
            sc.link(dve.tensor_scalar(kk[:, 1, :], ang, 1.0 / (2 * math.pi), 0.0, ALU.mult, ALU.add))
            sc.link(dve.tensor_scalar(kk[:, 0, :], ang, 1.0 / (2 * math.pi), 0.25, ALU.mult, ALU.add))
            sc.link(dve.tensor_scalar(kk, kk, MAGIC, None, ALU.add))
            sc.link(dve.tensor_scalar(kk, kk, MAGIC, None, ALU.subtract))
            prev = ang.unsqueeze(1).to_broadcast([P, 2, T])
            for part in TWO_PI:
                sc.link(dve.scalar_tensor_tensor(red, kk, -part, prev, ALU.mult, ALU.add))
                prev = red
            sc.link(dve.tensor_scalar(red[:, 0, :], red[:, 0, :], math.pi / 2, None, ALU.add))
            ins = dve.tensor_scalar(red, red, SIN_MAX, -SIN_MAX, ALU.min, ALU.max)
            ins.then_inc(st_ang, 1)
            dve.wait_ge(par_in, 16 * prow_n)
            dve.wait_ge(st_ang, 1)
            lv = work[:, 1024:1024 + LAYERS * 256].rearrange("p (l w d) -> p l w d", l=2 * LAYERS, w=2)
            lp = wk(1024 + LAYERS * 256, 2 * LAYERS, 64)
            sc.link(dve.tensor_tensor(lp, lv[:, :, 0, :], lv[:, :, 1, :], ALU.mult))
            dve.tensor_reduce(small[:, 104:108], lp, AX.X, ALU.add).then_inc(st_dot, 1)
            dve.wait_ge(st_rows, 1)
            for i in range(LAYERS):
                sc.link(dve.tensor_copy(pk[:, i, 0:K_WR], ps[:, 4 + i, 0:K_WR]))
                sc.link(dve.tensor_scalar(pk[:, i, K_SUB:K_SUB + 1], pk[:, i, K_SUB:K_SUB + 1],
                                          cst[:, C_OML + i:C_OML + i + 1], None, ALU.mult))
            dve.wait_ge(st_exp, 1)
            for i in range(LAYERS):
                lam = pk[:, i, K_LAM:K_LAM + 1]
                sc.link(dve.tensor_tensor(lam, small[:, 109 + 2 * i:110 + 2 * i], small[:, 108 + 2 * i:109 + 2 * i],
                                          ALU.subtract))
                sc.link(dve.tensor_tensor(lam, lam, cst[:, C_LAM + i:C_LAM + i + 1], ALU.subtract))
            dve.wait_ge(st_msq, 1)
            sc.link(dve.reciprocal(ss, ss))
            for s in range(TT):
                dve.tensor_scalar(memN[:, s, :], memN[:, s, :], ss[:, s:s + 1], None, ALU.mult).then_inc(st_mn, 1)
            dve.wait_ge(st_mt, 1)
            for j in range(4):
                for i in range(LAYERS):
                    gain = pk[:, i, 0:K_WR].rearrange("p (c r) -> p c r", c=DC)[:, 2 * j:2 * j + 2, R_MEM]
                    ins = dve.tensor_tensor(chunks(1 + i)[:, 2 * j:2 * j + 2, :],
                                            ps[:, j, :].rearrange("p (c t) -> p c t", c=2),
                                            gain.unsqueeze(2).to_broadcast([P, 2, T]), ALU.mult)
                ins.then_inc(st_mg, 1)

            q = dve.alloc_register("dve_pass")
            dve.reg_mov(q, 0)
            u = dve.alloc_register("dve_unit")
            dve.reg_mov(u, 0)
            dve.wait_ge(st_msto, 16)

            with dve.Fori(0, LAYERS) as L:
                ch = Chain(dve, dch)

                def both(job):
                    return ps[:, bank(job), :].rearrange("p (c t) -> p c t", c=2)

                def bcast(job, n, row):
                    return par[:, n:n + 2, row].unsqueeze(2).to_broadcast([P, 2, T])

                def norm(n):
                    dve.wait_ge(n_ss, TT * (n + 1))
                    dve.tensor_scalar(ss, ss, 1.0 / D, RMS_EPS, ALU.mult, ALU.add).then_inc(n_var, 1)
                    dve.wait_ge(n_root, n + 1)
                    ch.link(dve.reciprocal(ss, ss))
                    for s in range(TT):
                        dve.tensor_scalar(uN[:, s, :], h[:, s, :], ss[:, s:s + 1], None, ALU.mult).then_inc(n_ready, 1)

                def turned(kind, dst, row):
                    for j in (0, 2):
                        job = f"{kind}{j}"
                        dve.wait_ge(full[bank(job)], turn(job))
                        dve.tensor_tensor(dst[:, 2 * j:2 * j + 2, :], both(job), bcast(job, 2 * j, row),
                                          ALU.mult).then_inc(free[bank(job)], 1)

                dve.tensor_copy(cur[:], pk[:, L, :]).then_inc(cur_ready, 1)
                dve.wait_ge(cur_ready, 1)
                norm(0)
                turned("nm", uT, R_MIX)

                conv_last = {}
                taps = [(c0, t) for c0 in range(0, DC, 2) for t in range(KERN)]

                def conv_taps(n, have):
                    for _ in range(n):
                        if not taps or taps[0][0] // 2 >= have:
                            return
                        c0, t = taps.pop(0)
                        for c in (c0, c0 + 1):
                            src, wt = glu_pad[:, c, t:t + T], par[:, c, t:t + 1]
                            if t == 0:
                                dve.wait_ge(glu_ready, c0 // 2 + 1)
                                ins = dve.tensor_scalar(conv[:, c, :], src, wt, par[:, c, R_DB:R_DB + 1], ALU.mult, ALU.add)
                            else:
                                ch.after(conv_last[c])
                                ins = dve.scalar_tensor_tensor(conv[:, c, :], src, wt, conv[:, c, :], ALU.mult, ALU.add)
                            if not taps and c == c0 + 1:
                                ins.then_inc(conv_ready, 1)
                            else:
                                conv_last[c] = ch.note(ins)

                for j in range(4):
                    dve.wait_ge(sig_ready, j + 1)
                    dve.wait_ge(full[bank(f"a.{j}")], turn(f"a.{j}"))
                    dve.tensor_tensor(glu[:, 2 * j:2 * j + 2, :], both(f"a.{j}"), sg[:, j % 2], ALU.mult).then_inc(glu_ready, 1)
                    dve.wait_ge(glu_ready, j + 1)
                    dve.sem_inc(free[bank(f"a.{j}")], 1)
                    conv_taps((8, 26, 8, 8)[j], j + 1)
                cos2 = rope_cs[:, 0:1, :].to_broadcast([P, 2, T])
                sin2 = rope_cs[:, 1:2, :].to_broadcast([P, 2, T])
                for j in range(8):
                    job = f"q.{j}" if j < 4 else f"k.{j - 4}"
                    dst = (qT if j < 4 else kT)[:, 2 * (j % 4):2 * (j % 4) + 2, :]
                    dve.wait_ge(qraw_ready, j + 1)
                    k1 = ch.note(dve.tensor_tensor(rt1, qraw[:, j % 2], cos2, ALU.mult))
                    conv_taps(4, 4)
                    dve.wait_ge(rope_full, j + 1)
                    k2 = ch.note(dve.tensor_tensor(rt2, ps[:, ROPE_BANK, :].rearrange("p (c t) -> p c t", c=2), sin2, ALU.mult))
                    conv_taps(1, 4)
                    ch.after(k2)
                    dve.tensor_tensor(dst, rt1, rt2, ALU.add).then_inc(rope_ready, 1)
                    conv_taps(3, 4)
                conv_taps(len(taps), 4)

                def row_max(s):
                    dve.wait_ge(s_full, s + 1)
                    dve.tensor_reduce(nmx[:, s, :], ps[:, score_banks(s):score_banks(s) + 2, 0:T], AX.X, ALU.max,
                                      negate=True).then_inc(nm_ready, 1)

                dve.wait_ge(rope_ready, 8)
                row_max(0)
                for s in range(ATTN_STEPS):
                    if s + 1 < ATTN_STEPS:
                        row_max(s + 1)
                    dve.wait_ge(exp_ready, 2 * (s + 1))
                    rc = sm[:, s, :]
                    if s >= 1:
                        dve.wait_ge(a_ready, s)
                    ch.link(dve.reciprocal(rc, rc))
                    ch.link(dve.tensor_scalar(rc[:, 1:2], rc[:, 1:2], neglam, None, ALU.mult))
                    ch.link(dve.tensor_scalar(etmp, E[:, s % 2, 1, :], rc[:, 1:2], None, ALU.mult))
                    if s >= 2:
                        dve.wait_ge(at_full, s - 1)
                    dve.scalar_tensor_tensor(amix[:, s % 2, :], E[:, s % 2, 0, :], rc[:, 0:1], etmp, ALU.mult,
                                             ALU.add).then_inc(a_ready, 1)
                    if s % 2 == 1:
                        job = f"gate.{s // 2}"
                        g, j = ((gate_c, s // 2) if s < 8 else (gate_a, s // 2 - 4))
                        dve.wait_ge(full[bank(job)], turn(job))
                        dve.tensor_copy(g[:, 2 * j:2 * j + 2, :], both(job)).then_inc(gate_raw, 1)
                        dve.wait_ge(gate_raw, s // 2 + 1)
                        dve.sem_inc(free[bank(job)], 1)
                    if s == 3:
                        dve.wait_ge(full[bank("mean")], turn("mean"))
                        dve.wait_ge(conv_ready, 1)
                        mu = ps[:, bank("mean"), 0:T].unsqueeze(1).to_broadcast([P, DC, T])
                        dve.tensor_tensor(conv, conv, mu, ALU.subtract).then_inc(ln_xc, 1)
                        dve.wait_ge(ln_xc, 1)
                        dve.sem_inc(free[bank("mean")], 1)
                    if s == 9:
                        dve.wait_ge(full[bank("var")], turn("var"))
                        dve.tensor_scalar(rs_ln[:], ps[:, bank("var"), 0:T], LN_EPS, None, ALU.add).then_inc(ln_var, 1)
                        dve.wait_ge(ln_var, 1)
                        dve.sem_inc(free[bank("var")], 1)
                dve.wait_ge(o_ready, 4)
                sqo = uT[:].rearrange("p c t -> p (c t)").rearrange("p (s e) -> p s e", s=ATTN_STEPS)
                ch.link(dve.tensor_tensor(sqo, o_all, o_all, ALU.mult))
                ch.link(dve.tensor_reduce(ssq, sqo, AX.X, ALU.add))
                dve.tensor_scalar(ssq, ssq, 1.0 / P, LN_EPS, ALU.mult, ALU.add).then_inc(o_var, 1)
                dve.wait_ge(o_root, 1)
                ch.link(dve.reciprocal(ssq, ssq))
                dve.tensor_tensor(o_all, o_all, ssq.unsqueeze(2).to_broadcast([P, ATTN_STEPS, P]),
                                  ALU.mult).then_inc(o_norm, 1)
                dve.wait_ge(ln_root, 1)
                ch.link(dve.reciprocal(rs_ln[:], rs_ln[:]))
                dve.tensor_tensor(conv, conv, rs_ln[:].unsqueeze(1).to_broadcast([P, DC, T]), ALU.mult).then_inc(ln_y, 1)
                for j in range(4):
                    job = f"oT{j}"
                    dve.wait_ge(full[bank(job)], turn(job))
                    dve.tensor_scalar(oT[:, 2 * j:2 * j + 2, :], both(job), sub_col, None, ALU.mult).then_inc(oT_ready, 1)
                    dve.wait_ge(oT_ready, j + 1)
                    dve.sem_inc(free[bank(job)], 1)
                dve.wait_ge(gate_ready, 2)
                mg = {}
                for j in range(4):
                    job = f"ao.{j}"
                    dve.wait_ge(full[bank(job)], turn(job))
                    mg[j] = ch.note(dve.tensor_tensor(merged[:, 2 * j:2 * j + 2, :], both(job),
                                                      gate_a[:, 2 * j:2 * j + 2, :], ALU.mult))
                    ch.after(mg[j])
                    dve.sem_inc(free[bank(job)], 1)
                for j in range(4):
                    job = f"co.{j}"
                    dve.wait_ge(full[bank(job)], turn(job))
                    g = gate_c[:, 2 * j:2 * j + 2, :]
                    ch.link(dve.tensor_tensor(g, both(job), g, ALU.mult))
                    dve.sem_inc(free[bank(job)], 1)
                    m = merged[:, 2 * j:2 * j + 2, :]
                    dve.tensor_tensor(m, m, g, ALU.add).then_inc(merged_ready, 1)

                def add_to_h(kind, base):
                    for j in range(4):
                        job, s, half = f"{kind}{j}", j // 2, j % 2
                        dve.wait_ge(full[bank(job)], turn(job))
                        hs = h[:, s, half * SLAB:(half + 1) * SLAB]
                        dve.tensor_tensor(hs, hs, ps[:, bank(job), :], ALU.add).then_inc(h_ready, 1)
                        dve.wait_ge(h_ready, base + j + 1)
                        dve.sem_inc(free[bank(job)], 1)

                add_to_h("wo.", 0)
                norm(1)
                turned("nx", xT, R_X)

                def xmax(hd):
                    dve.wait_ge(xs_full, hd + 1)
                    dve.tensor_reduce(xnm[:, hd, :], ps[:, 4 + hd % 2, :].rearrange("p (s k) -> p s k", s=TT), AX.X,
                                      ALU.max, negate=True).then_inc(xnm_ready, 1)

                def xscale(hd):
                    dve.wait_ge(xexp_ready, TT * (hd + 1))
                    ch.link(dve.reciprocal(xsm[:, hd, :], xsm[:, hd, :]))
                    for s in range(TT):
                        dve.tensor_scalar(E[:, hd % 2, s, :], E[:, hd % 2, s, :], xsm[:, hd, s:s + 1], None,
                                          ALU.mult).then_inc(xp_ready, 1)

                def px_out(hd):
                    job = f"px{hd}"
                    dve.wait_ge(full[bank(job)], turn(job))
                    dve.tensor_copy(xoT[:, 2 * hd:2 * hd + 2, :], both(job)).then_inc(xo_ready, 1)
                    dve.wait_ge(xo_ready, hd + 1)
                    dve.sem_inc(free[bank(job)], 1)

                xmax(0)
                xscale(0)
                for hd in range(1, XHEADS):
                    xmax(hd)
                    xscale(hd)
                    if hd >= 2:
                        px_out(hd - 2)
                px_out(2)
                px_out(3)
                add_to_h("xo.", 4)
                norm(2)
                turned("nf", uT, R_FFN)

                def over(a, n):
                    return a.unsqueeze(2).to_broadcast([P, TT, n])

                def desc(n):
                    return cst[:, C_DESC + EXPERTS - n:C_DESC + EXPERTS].unsqueeze(1).to_broadcast([P, TT, n])

                dve.wait_ge(full[bank("router")], turn("router"))
                ch.link(dve.tensor_tensor(logit, ps[:, bank("router"), 0:TT * NR].rearrange("p (s n) -> p s n", s=TT),
                                          rb.unsqueeze(1).to_broadcast([P, TT, NR]), ALU.add))
                lg = logit[:, :, 0:GROUPS]
                ch.link(dve.tensor_reduce(m_g, lg, AX.X, ALU.max))
                dve.tensor_tensor(d_g, lg, over(m_g, GROUPS), ALU.subtract).then_inc(r_diff, 1)
                ch.link(dve.tensor_tensor(eq_g, lg, over(m_g, GROUPS), ALU.is_equal))
                ch.link(dve.tensor_tensor(eq_g, eq_g, desc(GROUPS), ALU.mult))
                ch.link(dve.tensor_reduce(mx_g, eq_g, AX.X, ALU.max))
                ch.link(dve.tensor_tensor(oh_g, eq_g, over(mx_g, GROUPS), ALU.is_equal))
                ch.link(dve.tensor_scalar(oh_g, oh_g, -1.0, 1e30, ALU.add, ALU.mult))
                for s in range(TT):
                    ch.link(dve.tensor_tensor(masked[:, s, :].rearrange("p (g e) -> p g e", g=GROUPS),
                                              logit[:, s, GROUPS:NR].rearrange("p (g e) -> p g e", g=GROUPS),
                                              oh_g[:, s, :].unsqueeze(2).to_broadcast([P, GROUPS, PER_GROUP]), ALU.add))
                for top, oh in ((top1, oh1), (top2, oh2)):
                    ch.link(dve.tensor_reduce(top, masked, AX.X, ALU.max))
                    ch.link(dve.tensor_tensor(first, masked, over(top, EXPERTS), ALU.is_equal))
                    ch.link(dve.tensor_tensor(first, first, desc(EXPERTS), ALU.mult))
                    ch.link(dve.tensor_reduce(mx_e, first, AX.X, ALU.max))
                    ch.link(dve.tensor_tensor(oh, first, over(mx_e, EXPERTS), ALU.is_equal))
                    if oh is oh1:
                        ch.link(dve.scalar_tensor_tensor(masked, oh1, -3e30, masked, ALU.mult, ALU.add))
                dve.tensor_tensor(gap, top2, top1, ALU.subtract).then_inc(r_gap, 1)
                dve.tensor_tensor(picked, oh1, oh2, ALU.add).then_inc(r_mask, 1)
                dve.wait_ge(r_exp, 1)
                ch.link(dve.tensor_reduce(g_w, e_g, AX.X, ALU.add))
                ch.link(dve.reciprocal(g_w, g_w))
                dve.wait_ge(r_gexp, 1)
                ch.link(dve.tensor_scalar(w_1, e_gap, 1.0, None, ALU.add))
                ch.link(dve.reciprocal(w_1, w_1))
                ch.link(dve.tensor_tensor(w_1, w_1, g_w, ALU.mult))
                ch.link(dve.tensor_tensor(w_2, w_1, e_gap, ALU.mult))
                ch.link(dve.tensor_tensor(tok_w, oh1, over(w_1, EXPERTS), ALU.mult))
                ch.link(dve.tensor_tensor(tok_w2, oh2, over(w_2, EXPERTS), ALU.mult))
                ch.link(dve.tensor_tensor(tok_w, tok_w, tok_w2, ALU.add))
                rkb = ps[:, bank("rank"), :]
                dve.wait_ge(full[bank("rank")], turn("rank"))
                ch.link(dve.tensor_scalar(rank, rkb[:, 0:TT * EXPERTS].rearrange("p (s e) -> p s e", s=TT), float(D), 1.0,
                                          ALU.mult, ALU.add))
                ch.link(dve.tensor_tensor(rank, rank, picked, ALU.mult))
                ch.link(dve.tensor_scalar(rank, rank, -1.0, None, ALU.add))
                ch.link(dve.tensor_reduce(cnt1, rkb[:, TT * EXPERTS:(TT + 1) * EXPERTS], AX.X, ALU.max))
                ch.link(dve.tensor_scalar(cnt1, cnt1, float(D), None, ALU.mult))
                ch.link(dve.tensor_tensor(thr7, cst[:, C_THR:C_THR + MAX_PASSES - 1],
                                          cnt1.to_broadcast([P, MAX_PASSES - 1]), ALU.is_lt))
                ch.link(dve.tensor_reduce(cnt1, thr7, AX.X, ALU.add))
                dve.tensor_scalar(npass_i[:], cnt1, 1.0, None, ALU.add).then_inc(rank_ready, 1)
                dve.wait_ge(rank_ready, 1)
                dve.sem_inc(np_ready, 1)

                passes = dve.value_load(npass_i[0:1, 0:1], min_val=1, max_val=MAX_PASSES)
                with dve.Fori(0, passes) as _p:
                    with dve.Fori(0, PAIRS) as i:
                        n = dve.snap(u)
                        dve.tensor_tensor(sel, rank[:, :, bass.ds(i * 2, 2)].unsqueeze(3).to_broadcast([P, TT, 2, CAP]),
                                          iota.unsqueeze(1).unsqueeze(1).to_broadcast([P, TT, 2, CAP]),
                                          ALU.is_equal).then_inc(sel_ready, 1)
                        dve.wait_ge(sel_ready, n + 1)
                        for dup in range(2):
                            dve.tensor_tensor(spread[:, :, :, dup, :], sel,
                                              tok_w[:, :, bass.ds(i * 2, 2)].unsqueeze(3).to_broadcast([P, TT, 2, CAP]),
                                              ALU.mult).then_inc(spread_ready, 1)
                        dve.wait_ge(xg_done, n + 1)
                        dve.tensor_tensor(xe, ps[:, 0, :].rearrange("p (c s) -> p c s", c=DC),
                                          par[:, :, R_FFN].unsqueeze(2).to_broadcast([P, DC, 2 * CAP]),
                                          ALU.mult).then_inc(xe_ready, 1)
                        dve.wait_ge(silu_ready, n + 1)
                        a4 = ps[:, 2, :].rearrange("p (f e w s) -> p f e w s", f=FC, e=2, w=2)
                        dve.tensor_tensor(up_t, silu_t, a4[:, :, :, 1, :], ALU.mult).then_inc(upt_ready, 1)
                        dve.wait_ge(y_done, n + 1)
                        dve.tensor_copy(y_sb, ps[:, 3, :]).then_inc(y_out, 1)
                        dve.reg_add(u, u, 1)
                    n = dve.snap(u)
                    k = dve.snap(q)
                    dve.wait_ge(added, n)
                    dve.tensor_copy(h[:, 0, :], ps[:, 4:6, :].rearrange("p b n -> p (b n)")).then_inc(h_back, 1)
                    dve.wait_ge(h_back, k * 2 + 2)
                    dve.tensor_scalar(rank, rank, -float(CAP), None, ALU.add)
                    dve.drain()
                    dve.reg_add(q, q, 1)
                dve.drain()
                dve.wait_ge(layer_end, 3 * L + 3)
                dve.sem_inc(layer_clear, 1)
                dve.sem_clear(cleared)
                dve.sem_inc(layer_go, 1)

            fc = Chain(dve, fin_ch)
            dve.wait_ge(fin_ss, TT)
            dve.tensor_scalar(ss, ss, 1.0 / D, RMS_EPS, ALU.mult, ALU.add).then_inc(fin_var, 1)
            dve.wait_ge(fin_sq, 1)
            fc.link(dve.reciprocal(ss, ss))
            dve.wait_ge(fin_g, 16)
            for s in range(TT):
                dve.scalar_tensor_tensor(uN[:, s, :], h[:, s, :], ss[:, s:s + 1],
                                         memT[:, 0:FC, :].rearrange("p c t -> p (c t)"), ALU.mult,
                                         ALU.mult).then_inc(fin_out, 1)

        @block.tensor
        def _(pe):
            prow = big[:, 0, :].rearrange("p (l d) -> p l d", l=LAYERS)
            pe.sem_inc(freed, RING)
            pe.wait_ge(cst_in, 16)
            pe.wait_ge(par_in, 16 * (8 + LAYERS * 9))
            for i in range(LAYERS):
                for c in range(DC):
                    last = pe.transpose(ps[:, 4 + i, c * ROWS:(c + 1) * ROWS], prow[0:ROWS, i, c * P:(c + 1) * P],
                                        ident[0:ROWS, 0:ROWS])
            last.then_inc(st_rows, 1)

            def turn_rows(dst, src, j):
                for c in range(2):
                    for s in range(TT):
                        last = pe.transpose(dst[:, c * T + s * P:c * T + (s + 1) * P],
                                            src[:, s, (2 * j + c) * P:(2 * j + c + 1) * P], ident)
                return last

            pe.wait_ge(st_mn, TT)
            for j in range(4):
                last = turn_rows(ps[:, j, :], memN, j)
            last.then_inc(st_mt, 1)
            pe.wait_ge(st_mg, 4)

            rnd = pe.alloc_register("pe_round")
            pe.reg_mov(rnd, 0)
            u = pe.alloc_register("pe_unit")
            pe.reg_mov(u, 0)
            q = pe.alloc_register("pe_pass")
            pe.reg_mov(q, 0)
            with pe.Fori(0, LAYERS) as L:
                r = pe.snap(rnd)

                def take(name):
                    n = SLABS.index(name)
                    pe.wait_ge(landed[n % RING], (r + (n // RING + 1)) * 16)
                    return slot(n % RING)

                def begin(job):
                    if turn(job) > 1:
                        pe.wait_ge(free[bank(job)], turn(job) - 1)
                    return ps[:, bank(job), :]

                def columns(dst, w, c, xs):
                    for k in range(DC):
                        last = pe.matmul(dst, w[:, k, c * P:(c + 1) * P], xs[:, k, :], start=(k == 0), stop=(k == DC - 1))
                    return last

                def col_jobs(kind, slab, jobs, xs, after=None):
                    w = take(slab)
                    for n, j in enumerate(jobs):
                        job = f"{kind}{j}"
                        dst = begin(job)
                        for c in range(2):
                            last = columns(dst[:, c * T:(c + 1) * T], w, 2 * n + c, xs)
                        last.then_inc(full[bank(job)], 1)
                        if n == 1:
                            pe.wait_ge(full[bank(job)], turn(job))
                            pe.sem_inc(freed, 1)
                        if after:
                            after(j)

                def row_job(job, w, xs, s):
                    dst = begin(job)
                    for k in range(DC):
                        last = pe.matmul(dst, xs[:, k, s * P:(s + 1) * P], w[:, k, :], start=(k == 0), stop=(k == DC - 1))
                    last.then_inc(full[bank(job)], 1)

                def release(job):
                    pe.wait_ge(full[bank(job)], turn(job))
                    pe.sem_inc(freed, 1)

                def turn_norm(kind, n):
                    pe.wait_ge(n_ready, TT * (n + 1))
                    for j in range(4):
                        job = f"{kind}{j}"
                        turn_rows(begin(job), uN, j).then_inc(full[bank(job)], 1)
                    for j in range(4):
                        pe.wait_ge(free[bank(f"{kind}{j}")], turn(f"{kind}{j}"))
                    pe.wait_ge(n_turned, 2 * (n + 1))

                turn_norm("nm", 0)
                col_jobs("a.", "a0", (0, 1), uT)
                col_jobs("g.", "g0", (0, 1), uT)
                col_jobs("a.", "a1", (2, 3), uT)
                col_jobs("g.", "g1", (2, 3), uT)

                def rotate(j):
                    pe.wait_ge(qraw_ready, j + 1)
                    if j >= 1:
                        pe.wait_ge(rope_ready, j)
                    pe.matmul(ps[:, ROPE_BANK, :], rot, qraw[:, j % 2].rearrange("p c t -> p (c t)"), start=True,
                              stop=True).then_inc(rope_full, 1)

                col_jobs("q.", "q0", (0, 1), uT, lambda j: rotate(j - 1) if j else None)
                col_jobs("q.", "q1", (2, 3), uT, lambda j: rotate(j - 1))
                col_jobs("k.", "k0", (0, 1), uT, lambda j: rotate(j + 3))
                col_jobs("k.", "k1", (2, 3), uT, lambda j: rotate(j + 3))
                for n in range(2):
                    w = take(f"v{n}")
                    for s in range(TT):
                        row_job(f"v.{2 * n + s}", w, uT, s)
                        if n == 0 and s == 0:
                            rotate(7)
                    release(f"v.{2 * n + 1}")

                def scores(s):
                    hd, t = s // TT, s % TT
                    if s >= 2:
                        pe.wait_ge(exp_ready, 2 * (s - 1))
                    for c in range(2):
                        lo = 2 * HALF * c
                        last = pe.matmul(ps[:, score_banks(s) + c, 0:T], qT[lo:lo + 2 * HALF, hd, t * P:(t + 1) * P],
                                         kT[lo:lo + 2 * HALF, hd, :], start=True, stop=True)
                    last.then_inc(s_full, 1)

                def turn_mix(s):
                    pe.wait_ge(a_ready, s + 1)
                    if s >= 1:
                        pe.wait_ge(at_ready, s)
                    for k in range(2):
                        last = pe.transpose(ps[:, MIX_BANK, k * P:(k + 1) * P], amix[:, s % 2, k * P:(k + 1) * P], ident)
                    last.then_inc(at_full, 1)

                def values(s):
                    hd = s // TT
                    pe.wait_ge(at_ready, s + 1)
                    if s % 4 == 0 and s >= 4:
                        pe.wait_ge(o_ready, s // 4)
                    for k in range(2):
                        last = pe.matmul(ps[:, VALUE_BANK, (s % 4) * P:(s % 4 + 1) * P], aTs[:, s % 2, k * P:(k + 1) * P],
                                         v[:, k, hd * P:(hd + 1) * P], start=(k == 0), stop=(k == 1))
                    if s % 4 == 3:
                        last.then_inc(pv_full, 1)

                pe.wait_ge(rope_ready, 8)
                pe.wait_ge(v_ready, 4)
                scores(0)
                for s in range(ATTN_STEPS):
                    if s + 1 < ATTN_STEPS:
                        scores(s + 1)
                    if s % 4 == 0:
                        w = take(("gc0", "gc1", "ga0", "ga1")[s // 4])
                    job = f"gate.{s // 2}"
                    if s % 2 == 0:
                        gdst = begin(job)
                    last = columns(gdst[:, (s % 2) * T:(s % 2 + 1) * T], w, s % 4, uT)
                    if s % 2 == 1:
                        last.then_inc(full[bank(job)], 1)
                    if s % 4 == 3:
                        release(job)
                    if s == 1:
                        pe.wait_ge(conv_ready, 1)
                        dst = begin("mean")
                        for c in range(DC):
                            last = pe.matmul(dst[:, 0:T], mean_m, conv[:, c, :], start=(c == 0), stop=(c == DC - 1))
                        last.then_inc(full[bank("mean")], 1)
                    if s == 7:
                        pe.wait_ge(ln_sq, 1)
                        dst = begin("var")
                        for c in range(DC):
                            last = pe.matmul(dst[:, 0:T], mean_m, sq[:, c, :], start=(c == 0), stop=(c == DC - 1))
                        last.then_inc(full[bank("var")], 1)
                    if s >= 1:
                        values(s - 1)
                    turn_mix(s)
                values(ATTN_STEPS - 1)

                pe.wait_ge(mt_in, L * 16 + 16)
                col_jobs("xk.", "xk0", (0, 1), memT)
                pe.wait_ge(o_norm, 1)
                for j in range(4):
                    dst = begin(f"oT{j}")
                    for c in range(2):
                        for s in range(TT):
                            last = pe.transpose(dst[:, c * T + s * P:c * T + (s + 1) * P],
                                                o_all[:, (2 * j + c) * TT + s, :], ident)
                    last.then_inc(full[bank(f"oT{j}")], 1)
                col_jobs("xk.", "xk1", (2, 3), memT)
                pe.wait_ge(oT_ready, 4)
                col_jobs("ao.", "ao0", (0, 1), oT)
                col_jobs("ao.", "ao1", (2, 3), oT)
                pe.wait_ge(ln_out, DC)
                col_jobs("co.", "co0", (0, 1), conv)
                col_jobs("co.", "co1", (2, 3), conv)
                w = take("xv0")
                for s in range(TT):
                    row_job(f"xv.{s}", w, memT, s)
                release("xv.1")
                pe.wait_ge(merged_ready, 4)
                ws = [take("wo0"), take("wo1")]
                for s in range(TT):
                    for half in range(HALVES):
                        row_job(f"wo.{2 * s + half}", ws[half], merged, s)
                release("wo.3")
                pe.sem_inc(freed, 1)
                w = take("xv1")
                for s in range(TT):
                    row_job(f"xv.{2 + s}", w, memT, s)
                release("xv.3")
                turn_norm("nx", 1)

                def xscores(hd):
                    pe.wait_ge(xq_ready, hd + 1)
                    if hd == 0:
                        pe.wait_ge(xk_ready, 4)
                    if hd >= 2:
                        pe.wait_ge(xexp_ready, TT * (hd - 1))
                    for s in range(TT):
                        for c in range(2):
                            last = pe.matmul(ps[:, 4 + hd % 2, s * T:(s + 1) * T], xqT[:, 2 * hd + c, s * P:(s + 1) * P],
                                             xkT[:, 2 * hd + c, :], start=(c == 0), stop=(c == 1))
                    last.then_inc(xs_full, 1)

                def xturn(hd):
                    pe.wait_ge(xp_ready, TT * (hd + 1))
                    if hd >= 2:
                        pe.wait_ge(xt_ready, hd - 1)
                    for k in range(2):
                        for s in range(TT):
                            last = pe.transpose(ps[:, 6 + hd % 2, k * T + s * P:k * T + (s + 1) * P],
                                                E[:, hd % 2, s, k * P:(k + 1) * P], ident)
                    last.then_inc(xt_full, 1)

                def xvalues(hd):
                    pe.wait_ge(xt_ready, hd + 1)
                    if hd == 0:
                        pe.wait_ge(xv_ready, 4)
                    dst = begin(f"px{hd}")
                    for c in range(2):
                        for k in range(2):
                            last = pe.matmul(dst[:, c * T:(c + 1) * T], xv[:, k, (2 * hd + c) * P:(2 * hd + c + 1) * P],
                                             pT[:, hd % 2, k * T:(k + 1) * T], start=(k == 0), stop=(k == 1))
                    last.then_inc(full[bank(f"px{hd}")], 1)

                col_jobs("xq.", "xq0", (0, 1), xT)
                w = take("xq1")
                dst = begin("xq.2")
                for c in range(2):
                    last = columns(dst[:, c * T:(c + 1) * T], w, c, xT)
                last.then_inc(full[bank("xq.2")], 1)
                xscores(0)
                dst = begin("xq.3")
                for c in range(2):
                    last = columns(dst[:, c * T:(c + 1) * T], w, 2 + c, xT)
                last.then_inc(full[bank("xq.3")], 1)
                release("xq.3")
                xscores(1)
                xturn(0)
                for hd in range(2, XHEADS + 2):
                    if hd < XHEADS:
                        xscores(hd)
                    if hd - 1 < XHEADS:
                        xturn(hd - 1)
                    xvalues(hd - 2)
                pe.wait_ge(xo_ready, 4)
                ws = [take("xo0"), take("xo1")]
                for s in range(TT):
                    for half in range(HALVES):
                        row_job(f"xo.{2 * s + half}", ws[half], xoT, s)
                release("xo.3")
                pe.sem_inc(freed, 1 + DENSE_ROUNDS * RING - len(SLABS))
                turn_norm("nf", 2)

                dst = begin("router")
                for s in range(TT):
                    for k in range(DC):
                        last = pe.matmul(dst[:, s * NR:(s + 1) * NR], uT[:, k, s * P:(s + 1) * P], wr[:, k, :],
                                         start=(k == 0), stop=(k == DC - 1))
                last.then_inc(full[bank("router")], 1)
                pe.wait_ge(r_mask, 1)
                dst = ps[:, bank("rank"), :]
                pe.matmul(dst[:, 0:EXPERTS], tri, picked[:, 0, :], start=True, stop=True)
                pe.matmul(dst[:, EXPERTS:2 * EXPERTS], tri, picked[:, 1, :], start=True, stop=False)
                pe.matmul(dst[:, EXPERTS:2 * EXPERTS], mean_m, picked[:, 0, :], start=False, stop=True)
                pe.matmul(dst[:, 2 * EXPERTS:3 * EXPERTS], mean_m, picked[:, 0, :], start=True, stop=False)
                pe.matmul(dst[:, 2 * EXPERTS:3 * EXPERTS], mean_m, picked[:, 1, :], start=False,
                          stop=True).then_inc(full[bank("rank")], 1)
                pe.reg_add(rnd, rnd, DENSE_ROUNDS)

                pe.wait_ge(rank_ready, 1)
                passes = pe.value_load(npass_i[0:1, 0:1], min_val=1, max_val=MAX_PASSES)
                with pe.Fori(0, passes) as _p:
                    for s in range(TT):
                        for half in range(HALVES):
                            pe.matmul(ps[:, 4 + 2 * s + half, :], ident, h[:, s, half * SLAB:(half + 1) * SLAB],
                                      start=True, stop=True)
                    with pe.Fori(0, PAIRS) as _i:
                        n = pe.snap(u)
                        rr = pe.snap(rnd)
                        pe.wait_ge(sel_ready, n + 1)
                        for c in range(DC):
                            for s in range(TT):
                                last = pe.matmul(ps[:, 0, c * 2 * CAP:(c + 1) * 2 * CAP], uN[:, s, c * P:(c + 1) * P],
                                                 sel[:, s].rearrange("p e s -> p (e s)"), start=(s == 0), stop=(s == TT - 1))
                        last.then_inc(xg_done, 1)
                        pe.wait_ge(spread_ready, n * 2 + 2)
                        for s in range(TT):
                            last = pe.transpose(ps[:, 2, s * P:(s + 1) * P],
                                                spread[:, s].rearrange("p e w s -> p (e w s)"), ident)
                        last.then_inc(gt_done, 1)
                        pe.wait_ge(xe_ready, n + 1)
                        for j in range(4):
                            pe.wait_ge(landed[j], rr * 16 + 16)
                        for k in range(DC):
                            for j in range(4):
                                e = j // 2
                                last = pe.matmul(ps[CAP * j:CAP * (j + 1), 1, :], xe[:, k, e * CAP:(e + 1) * CAP],
                                                 slot(j)[:, k, :], start=(k == 0), stop=(k == DC - 1),
                                                 skip_group_check=True)
                        last.then_inc(up_done, 1)
                        pe.wait_ge(up_done, n + 1)
                        pe.sem_inc(freed, 4)
                        pe.wait_ge(up_out, n + 1)
                        pe.wait_ge(scat_ready, n + 1)
                        for f in range(FC):
                            last = pe.transpose(ps[:, 2, f * P:(f + 1) * P], up_sb[:, f * P:(f + 1) * P], ident)
                        last.then_inc(upt_done, 1)
                        pe.wait_ge(upt_ready, n + 1)
                        for j in range(4, RING):
                            pe.wait_ge(landed[j], rr * 16 + 16)
                        for f in range(FC):
                            for j in range(4):
                                e, half = j // 2, j % 2
                                w = ring[:, 4 + e, :].rearrange("p (c n) -> p c n", c=FC)
                                last = pe.matmul(ps[CAP * j:CAP * (j + 1), 3, :], up_t[:, f, e, :],
                                                 w[:, f, half * SLAB:(half + 1) * SLAB], start=(f == 0),
                                                 stop=(f == FC - 1), skip_group_check=True)
                        last.then_inc(y_done, 1)
                        pe.wait_ge(y_done, n + 1)
                        pe.sem_inc(freed, 2)
                        pe.wait_ge(y_out, n + 1)
                        for s in range(TT):
                            for half in range(HALVES):
                                last = pe.matmul(ps[:, 4 + 2 * s + half, :], scat[:, half, s * P:(s + 1) * P], y_sb,
                                                 start=False, stop=True, skip_group_check=True)
                        last.then_inc(added, 1)
                        pe.reg_add(u, u, 1)
                        pe.reg_add(rnd, rnd, 1)
                    k = pe.snap(q)
                    pe.wait_ge(h_back, k * 2 + 2)
                    pe.reg_add(q, q, 1)
                pe.drain().then_inc(layer_end, 1)
                pe.wait_ge(layer_go, L + 1)


_INS = ["x", "mem", "positions", "norm_mix_g", "w_in", "conv_dw", "conv_db", "conv_ln_g", "conv_ln_b", "w_conv_out",
        "lam_q1", "lam_k1", "lam_q2", "lam_k2", "subln_g", "w_attn_out", "w_out", "norm_mem_g", "norm_x_g", "w_xq",
        "w_xkv", "w_xo", "norm_ffn_g", "w_group", "b_group", "w_router", "b_router", "w1", "w3", "w2", "final_norm_g"]


def kernel(**inputs):
    import concourse.bacc as _bacc
    from concourse.bass_utils import run_bass_kernel_spmd as _run

    nc = _bacc.Bacc("TRN2", target_bir_lowering=False, num_devices=1)
    arrays, args = {}, []
    for name in ["consts"] + _INS:
        a = constants() if name == "consts" else np.ascontiguousarray(inputs[name])
        arrays[f"in_{name}_dram"] = a
        args.append(nc.dram_tensor(f"in_{name}_dram", a.shape, mybir.dt.from_np(a.dtype), kind="ExternalInput").ap())
    o = nc.dram_tensor("out_0_dram", (1, T, D), F32, kind="ExternalOutput").ap()
    encoder(nc, *args, o)
    r = _run(nc, [arrays], core_ids=[0])
    return r.results[0]["out_0_dram"]
```

```python
import math
from contextlib import ExitStack

import numpy as np

import concourse.bass as bass
from concourse import mybir

P = 128
F32 = mybir.dt.float32
F32R = mybir.dt.float32r
I32 = mybir.dt.int32
ALU = mybir.AluOpType
ACT = mybir.ActivationFunctionType
AX = mybir.AxisListType

LAYERS = 2
T = 256
TT = T // P
D = 1024
DC = D // P
KERN = 31
PAD = KERN // 2
HEADS = 8
HALF = 32
XHEADS = 4
GROUPS = 4
PER_GROUP = 8
EXPERTS = GROUPS * PER_GROUP
FF = D // 2
FC = FF // P
SLAB = 512
RING = 6
PAIRS = EXPERTS // 2
CAP = 32
MAX_PASSES = T // CAP
HALVES = D // SLAB

R_DB, R_LNG, R_LNB, R_MIX, R_MEM, R_X, R_FFN = range(KERN, KERN + 7)
ROWS = KERN + 7
NR = GROUPS + EXPERTS
K_WR = DC * ROWS
K_RB = K_WR + DC * NR
K_SUB = K_RB + NR
K_LAM = K_SUB + 1
NPK = K_LAM + 1

C_ID = 0
C_ROT = C_ID + P
C_TRI = C_ROT + P
C_MEAN = C_TRI + P
C_IOTA = C_MEAN + P
C_THR = C_IOTA + CAP
C_DESC = C_THR + MAX_PASSES - 1
C_INVF = C_DESC + EXPERTS
C_MLO = C_INVF + 1
C_MHI = C_MLO + 1
C_LAM = C_MHI + 1
C_OML = C_LAM + LAYERS
NCON = C_OML + LAYERS

RMS_EPS = 1e-6
LN_EPS = 1e-5
TWO_PI = (6.28125, 0.0019350051879882812, 3.019916e-07)
MAGIC = 12582912.0
SIN_MAX = 3.1415925

SLABS = ["a0", "g0", "a1", "g1", "q0", "q1", "k0", "k1", "v0", "v1", "gc0", "gc1", "ga0", "ga1",
         "xk0", "xk1", "ao0", "ao1", "co0", "co1", "xv0", "wo0", "wo1", "xv1", "xq0", "xq1", "xo0", "xo1"]

LAND = 2
QUARTERS = 4
SPLITS = 4
NQ = QUARTERS * len(SLABS)

TURN = 4


def pairs(name):
    return [f"{name}{j}" for j in range(4)]


ATTN_STEPS = HEADS * TT
JOBS = (pairs("nm") + ["a.0", "a.1", "g.0", "g.1", "a.2", "a.3", "g.2", "g.3"] + pairs("q.") + pairs("k.")
        + pairs("v."))
for _j in range(ATTN_STEPS // 2):
    JOBS += [f"gate.{_j}"]
    if _j == 0:
        JOBS += ["mean"]
    if _j == 3:
        JOBS += ["var"]
JOBS += ["xk.0", "xk.1"] + pairs("oT") + ["xk.2", "xk.3"] + pairs("ao.") + pairs("co.") + ["xv.0", "xv.1"]
JOBS += pairs("wo.") + ["xv.2", "xv.3"] + pairs("nx") + pairs("xq.") + pairs("px") + pairs("xo.") + pairs("nf")
JOBS += ["router", "rank"]


def banks_of_jobs():
    where, used, last = {}, [0] * TURN, -1
    for job in JOBS:
        n = TURN // 2 if job.startswith(("gate", "mean", "var")) else TURN
        last = (last + 1) % n
        used[last] += 1
        where[job] = (last, used[last])
    return where


WHERE = banks_of_jobs()


def last_quarters():
    at = {}
    for kind in ("a", "g", "q", "k", "xk", "ao", "co", "xq"):
        for j in range(4):
            at[f"{kind}.{j}"] = QUARTERS * SLABS.index(f"{kind}{j // 2}") + (1, 3)[j % 2]
    for kind in ("v", "xv", "wo", "xo"):
        for j in range(4):
            at[f"{kind}.{j}"] = QUARTERS * SLABS.index(f"{kind}{j // 2}") + 3
    return at


LAST_QUARTER = last_quarters()


def bank(job):
    return WHERE[job][0]


def turn(job):
    return WHERE[job][1]


def score_banks(s):
    return 2 + 2 * (s % 2)


ROPE_BANK = 5
VALUE_BANK = 6
MIX_BANK = 7


class Chain:

    def __init__(self, eng, sem):
        self.eng, self.sem, self.n = eng, sem, 0

    def note(self, ins):
        ins.then_inc(self.sem, 1)
        self.n += 1
        return self.n

    def after(self, n):
        self.eng.wait_ge(self.sem, n)

    def link(self, ins):
        self.after(self.note(ins))


def constants():
    c = np.zeros((P, NCON), np.float32)
    p = np.arange(P)
    c[:, C_ID:C_ID + P] = np.eye(P)
    for b in range(0, P, 2 * HALF):
        for d in range(HALF):
            c[b + HALF + d, C_ROT + b + d] = -1.0
            c[b + d, C_ROT + b + HALF + d] = 1.0
    c[:, C_TRI:C_TRI + P] = (p[:, None] < p[None, :]) / D
    c[:, C_MEAN:C_MEAN + P] = 1.0 / D
    c[:, C_IOTA:C_IOTA + CAP] = np.arange(CAP)
    c[:, C_THR:C_THR + MAX_PASSES - 1] = CAP * np.arange(1, MAX_PASSES)
    c[:, C_DESC:C_DESC + EXPERTS] = EXPERTS - np.arange(EXPERTS)
    step = np.float32(-math.log(10000.0))
    c[:, C_INVF] = np.exp(step * (p % HALF).astype(np.float32) / np.float32(HALF))
    c[:, C_MLO] = (p // CAP) % 2 == 0
    c[:, C_MHI] = (p // CAP) % 2 == 1
    for i in range(LAYERS):
        c[:, C_LAM + i] = 0.8 - 0.6 * math.exp(-0.3 * i)
        c[:, C_OML + i] = 1.0 - (0.8 - 0.6 * math.exp(-0.3 * i))
    return c


def encoder(nc, consts, x, mem, positions, norm_mix_g, w_in, conv_dw, conv_db, conv_ln_g, conv_ln_b, w_conv_out,
            lam_q1, lam_k1, lam_q2, lam_k2, subln_g, w_attn_out, w_out, norm_mem_g, norm_x_g, w_xq, w_xkv, w_xo,
            norm_ffn_g, w_group, b_group, w_router, b_router, w1, w3, w2, final_norm_g, out):
    mem_t_dram = nc.dram_tensor("mem_t_scratch", (LAYERS, P, DC * T), F32, kind="Internal").ap()

    with ExitStack() as ctx:
        def sb(name, shape, dt=F32):
            return ctx.enter_context(nc.sbuf_tensor(name, shape, dt))

        def sem(name):
            return ctx.enter_context(nc.semaphore(name))

        ring = sb("ring", [P, RING, DC * SLAB])
        ring_at = nc.sbuf_base - RING * DC * SLAB * 4
        h = sb("h", [P, TT, D])
        uT = sb("uT", [P, DC, T])
        uT_at = nc.sbuf_base - DC * T * 4
        glu_pad = sb("glu_pad", [P, DC, T + 2 * PAD + 2])
        big = sb("big", [P, 7, DC * T])
        big_at = nc.sbuf_base - 7 * DC * T * 4
        memT = sb("memT", [P, DC, T])
        cst = sb("cst", [P, NCON])
        pk = sb("pk", [P, LAYERS, NPK])
        cur = sb("cur", [P, NPK])
        rope_cs = sb("rope_cs", [P, 2, T])
        work = sb("work", [P, 2304])
        small = sb("small", [P, 224])
        rs_ln = sb("rs_ln", [P, T])
        npass_i = sb("npass_i", [P, 1], I32)
        ps = ctx.enter_context(nc.psum_tensor("ps", [P, 8, SLAB], F32))

        quarter_bytes = 2 * DC * P * 4
        operand_bytes = DC * T * 4
        wsplit = nc.alloc_sbuf_tensor_at("weight_split", [P, SPLITS, 2, DC * P], F32R,
                                         offset=ring_at + LAND * DC * SLAB * 4).ap()
        xsplit = nc.alloc_sbuf_tensor_at("operand_split", [P, 4, DC, T], F32R,
                                         offset=ring_at + LAND * DC * SLAB * 4 + SPLITS * quarter_bytes).ap()
        conv_hi = nc.alloc_sbuf_tensor_at("conv_high", [P, DC, T], F32R, offset=big_at + operand_bytes).ap()
        conv_lo = nc.alloc_sbuf_tensor_at("conv_low", [P, DC, T], F32R, offset=uT_at).ap()
        assert LAND * DC * SLAB * 4 + SPLITS * quarter_bytes + 4 * operand_bytes <= RING * DC * SLAB * 4

        u_s = o_s = m_s = x_s = (xsplit[:, 0], xsplit[:, 1])
        mem_s = xo_s = (xsplit[:, 2], xsplit[:, 3])
        conv_s = (conv_hi, conv_lo)

        def chunks(i):
            return big[:, i, :].rearrange("p (c t) -> p c t", c=DC)

        def rows(i):
            return big[:, i, :].rearrange("p (s d) -> p s d", s=TT)

        glu = glu_pad[:, :, PAD:PAD + T]
        sq = glu
        xkT = glu
        conv = chunks(0)
        qT = chunks(1)
        kT = chunks(2)
        merged = chunks(2)
        v = rows(3)
        xv = rows(3)
        gate_c = chunks(4)
        xqT = chunks(4)
        gate_a = chunks(5)
        o_all = big[:, 6, :].rearrange("p (s e) -> p s e", s=ATTN_STEPS)
        uN = rows(6)
        memN = rows(3)

        ident = cst[:, C_ID:C_ID + P]
        rot = cst[:, C_ROT:C_ROT + P]
        tri = cst[:, C_TRI:C_TRI + P]
        mean_m = cst[:, C_MEAN:C_MEAN + P]
        iota = cst[:, C_IOTA:C_IOTA + CAP]
        par = cur[:, 0:K_WR].rearrange("p (c r) -> p c r", c=DC)
        wr = cur[:, K_WR:K_RB].rearrange("p (c n) -> p c n", c=DC)
        rb = cur[:, K_RB:K_SUB]
        sub_col = cur[:, K_SUB:K_SUB + 1]
        neglam = cur[:, K_LAM:K_LAM + 1]

        def wk(at, *shape):
            n = int(np.prod(shape))
            a = work[:, at:at + n]
            if len(shape) == 1:
                return a
            names = "abcd"[:len(shape)]
            return a.rearrange(f"p ({' '.join(names)}) -> p {' '.join(names)}",
                               **{k: s for k, s in zip(names[:-1], shape[:-1])})

        sg = wk(0, 2, 2, T)
        qraw = wk(0, 2, 2, T)
        rt1 = wk(1024, 2, T)
        rt2 = wk(1536, 2, T)
        E = wk(0, 2, 2, T)
        amix = wk(1024, 2, T)
        aTs = wk(1536, 2, T)
        etmp = wk(2048, T)
        pT = wk(1024, 2, 2 * T)
        nmx = small[:, 0:32].rearrange("p (s c) -> p s c", s=ATTN_STEPS)
        sm = small[:, 32:64].rearrange("p (s c) -> p s c", s=ATTN_STEPS)
        ssq = small[:, 66:82]
        ss = small[:, 82:84]
        xnm = small[:, 84:92].rearrange("p (s c) -> p s c", s=XHEADS)
        xsm = small[:, 92:100].rearrange("p (s c) -> p s c", s=XHEADS)
        cnt1 = small[:, 100:101]
        thr7 = small[:, 101:108]
        mss = small[:, 112:114]

        rbuf = big[:, 2, :]
        roff = [0]

        def rt(*shape):
            n = int(np.prod(shape))
            a = rbuf[:, roff[0]:roff[0] + n]
            roff[0] += n
            if len(shape) == 1:
                return a
            names = "abcd"[:len(shape)]
            return a.rearrange(f"p ({' '.join(names)}) -> p {' '.join(names)}",
                               **{k: s for k, s in zip(names[:-1], shape[:-1])})

        logit = rt(TT, NR)
        m_g = rt(TT)
        d_g = rt(TT, GROUPS)
        e_g = rt(TT, GROUPS)
        g_w = rt(TT)
        eq_g = rt(TT, GROUPS)
        oh_g = rt(TT, GROUPS)
        mx_g = rt(TT)
        masked = rt(TT, EXPERTS)
        top1 = rt(TT)
        top2 = rt(TT)
        first = rt(TT, EXPERTS)
        mx_e = rt(TT)
        oh1 = rt(TT, EXPERTS)
        oh2 = rt(TT, EXPERTS)
        gap = rt(TT)
        e_gap = rt(TT)
        w_1 = rt(TT)
        w_2 = rt(TT)
        tok_w = rt(TT, EXPERTS)
        tok_w2 = rt(TT, EXPERTS)
        picked = rt(TT, EXPERTS)
        rank = rt(TT, EXPERTS)
        roff[0] = 0
        rbuf = big[:, 3, :]
        sel = rt(TT, 2, CAP)
        spread = rt(TT, 2, 2, CAP)
        xe = rt(DC, 2 * CAP)
        up_t = rt(FC, 2, CAP)
        rbuf = big[:, 4, :]
        roff[0] = 0
        y_sb = rt(SLAB)
        scat = rt(2, T)
        up_sb = rt(SLAB)
        silu_t = rt(FC, 2, CAP)

        landed = [sem(f"slab_landed_{i}") for i in range(RING)]
        slab_in = [sem(f"dense_slab_landed_{i}") for i in range(LAND)]
        split_out = sem("dense_slab_split")
        freed = sem("slot_freed")
        cst_in, x_in, par_in, pos_in, mem_in, lam_in, sub_in, router_in = (sem(n) for n in (
            "consts_in", "x_in", "params_in", "pos_in", "mem_in", "lambdas_in", "subln_in", "router_params_in"))
        st_rows, st_pk, st_mss, st_mvar, st_msq, st_mn, st_mt, st_mg, st_msto = (sem("setup_" + n) for n in (
            "rows_turned", "params_packed", "mem_squares", "mem_variance", "mem_root", "mem_normed", "mem_turned",
            "mem_scaled", "mem_stored"))
        st_ang, st_cs, st_dot, st_exp, st_ch = (sem("setup_" + n) for n in (
            "angles", "sincos", "lambda_dots", "lambda_exps", "vector_chain"))
        mt_in = sem("mem_t_in")
        layer_end, layer_go = sem("layer_end"), sem("layer_go")
        np_ready, np_seen = sem("passes_ready"), sem("passes_seen")
        layer_clear = sem("layer_clear")
        sel_ready, spread_ready, xg_done, gt_done, xe_ready, scat_ready, up_done, up_out, upt_done, silu_ready, \
            upt_ready, y_done, y_out, added = (sem("moe_" + n) for n in (
                "select_ready", "spread_ready", "gathered", "spread_turned", "tokens_ready", "scatter_ready",
                "up_done", "up_out", "up_turned", "silu_ready", "hidden_ready", "down_done", "down_out", "added"))
        h_back = sem("moe_residual_back")
        fin_g, fin_ss, fin_var, fin_sq, fin_ch, fin_out, out_done = (sem("final_" + n) for n in (
            "gain_in", "squares", "variance", "root", "chain", "rows_ready", "stored"))

        first_sem = sem("bank_full_0")
        full = [first_sem] + [sem(f"bank_full_{b}") for b in range(1, TURN)]
        free = [sem(f"bank_free_{b}") for b in range(TURN)]
        dch, ach = sem("vector_chain"), sem("scalar_chain")
        cur_ready = sem("layer_params_ready")
        w_hi, w_lo, w_used = sem("weights_high"), sem("weights_low"), sem("weights_used")
        hi_ready, lo_ready, mem_hi, mem_lo, conv_hi_ready, conv_lo_ready, m_hi, xo_hi = (sem(n) for n in (
            "operand_high_ready", "operand_low_ready", "memory_high", "memory_low", "conv_high_ready",
            "conv_low_ready", "merged_high", "cross_high"))
        n_ss, n_var, n_root, n_ready, n_turned = (sem("norm_" + n) for n in (
            "squares", "variance", "root", "rows_ready", "columns_ready"))
        sig_ready, glu_ready = sem("glu_sigmoid_ready"), sem("glu_ready")
        conv_ready, ln_xc, ln_sq, ln_var, ln_root, ln_y, ln_out = (sem(n) for n in (
            "conv_ready", "ln_centred", "ln_squared", "ln_variance", "ln_root", "ln_scaled", "ln_silu_ready"))
        qraw_ready, rope_full, rope_ready = sem("rope_raw_ready"), sem("rope_turned"), sem("rope_ready")
        v_ready = sem("v_ready")
        s_full, nm_ready, exp_ready, a_ready, at_full, at_ready, pv_full, o_ready = (sem("attn_" + n) for n in (
            "scores", "max_ready", "exp_ready", "mix_ready", "mix_turned", "mix_columns", "values", "rows_out"))
        gate_raw, gate_ready, o_var, o_root, o_norm, oT_ready = (sem(n) for n in (
            "gates_raw", "gates_ready", "subln_variance", "subln_root", "subln_ready", "attn_columns_ready"))
        xk_ready, xv_ready, merged_ready, h_ready, xq_ready = (sem(n) for n in (
            "xk_ready", "xv_ready", "merged_ready", "h_ready", "xq_ready"))
        xs_full, xnm_ready, xexp_ready, xp_ready, xt_full, xt_ready, xo_ready = (sem("cross_" + n) for n in (
            "scores", "max_ready", "exp_ready", "probs_ready", "probs_turned", "probs_columns", "columns_ready"))
        r_diff, r_exp, r_gap, r_gexp, r_mask, rank_ready = (sem("router_" + n) for n in (
            "group_diff", "group_exp", "gap", "gap_exp", "picked", "rank_ready"))
        last_sem = rank_ready
        cleared = range(first_sem.num, last_sem.num + 1)

        block = ctx.enter_context(nc.Block())

        def slab_source(name, L):
            kind, half = name[:-1], int(name[-1])
            c = {"a": 0, "g": D, "q": 2 * D, "k": 3 * D, "v": 4 * D, "gc": 5 * D, "ga": 6 * D}
            if kind in c:
                w, c0 = w_in, c[kind]
            elif kind in ("xk", "xv"):
                w, c0 = w_xkv, D * (kind == "xv")
            else:
                w, c0 = {"co": w_conv_out, "ao": w_attn_out, "wo": w_out, "xq": w_xq, "xo": w_xo}[kind], 0
            c0 += half * SLAB
            return w[L, :, c0:c0 + SLAB].rearrange("(c p) n -> p c n", p=P)

        def slot(j):
            return ring[:, j, :].rearrange("p (c n) -> p c n", c=DC)

        def by_rows(name):
            return name[:-1] in ("v", "xv", "wo", "xo")

        def landed_quarter(q):
            n, c = q // QUARTERS, q % QUARTERS
            w = slot(n % LAND)
            return w[:, 2 * c:2 * c + 2, :] if by_rows(SLABS[n]) else w[:, :, c * P:(c + 1) * P]

        def split_quarter(q, part):
            c = 2 if by_rows(SLABS[q // QUARTERS]) else DC
            return wsplit[:, q % SPLITS, part, :].rearrange("p (c n) -> p c n", c=c)

        @block.sync
        def _(sp):
            sp.dma_start(memN, mem[0].rearrange("(s p) d -> p s d", p=P)).then_inc(mem_in, 16)
            sp.dma_start(h[:], x[0].rearrange("(s p) d -> p s d", p=P)).then_inc(x_in, 16)
            sp.wait_ge(cst_in, 16)
            sp.wait_ge(par_in, 16 * 8)
            m = sp.alloc_register("sp_unit")
            sp.reg_mov(m, 0)

            def experts(L, i):
                n = sp.snap(m)
                srcs = [w1[L, 2 * i], w3[L, 2 * i], w1[L, 2 * i + 1], w3[L, 2 * i + 1], w2[L, 2 * i], w2[L, 2 * i + 1]]
                for j, s in enumerate(srcs):
                    sp.wait_ge(freed, (n + L) * RING + (RING + j + 1))
                    sp.dma_start(ring[:, j, :].rearrange("p (c n) -> p c n", c=DC if j < 4 else FC),
                                 s.rearrange("(c p) n -> p c n", p=P)).then_inc(landed[j], 16)
                sp.reg_add(m, m, 1)

            with sp.Fori(0, LAYERS) as L:
                n_pair = sp.snap(m)
                for n, name in enumerate(SLABS):
                    if n < LAND:
                        sp.wait_ge(freed, (n_pair + L) * RING + (n + 1))
                    else:
                        sp.wait_ge(split_out, L * len(SLABS) + (n - 1))
                    sp.dma_start(slot(n % LAND), slab_source(name, L)).then_inc(slab_in[n % LAND], 16)
                with sp.Fori(0, PAIRS) as i:
                    experts(L, i)
                sp.wait_ge(np_ready, L + 1)
                sp.sem_inc(np_seen, 1)
                passes = sp.value_load(npass_i[0:1, 0:1], min_val=1, max_val=MAX_PASSES)
                with sp.If(passes > 1):
                    with sp.Fori(1, passes) as _p:
                        with sp.Fori(0, PAIRS) as i:
                            experts(L, i)
                    sp.nop()
                sp.nop()
            for s in range(TT):
                sp.wait_ge(fin_out, s + 1)
                sp.dma_start(out[0, s * P:(s + 1) * P, :], uN[:, s, :]).then_inc(out_done, 16)
            sp.wait_ge(out_done, 16 * TT)

        @block.gpsimd
        def _(pool):
            for i in range(LAYERS):
                wrl = pk[:, i, K_WR:K_RB].rearrange("p (c n) -> p c n", c=DC)
                pool.dma_start(wrl[:, :, 0:GROUPS], w_group[i].rearrange("(c p) n -> p c n", p=P)).then_inc(router_in, 16)
                pool.dma_start(wrl[:, :, GROUPS:NR],
                               w_router[i].rearrange("(c p) n -> p c n", p=P)).then_inc(router_in, 16)
                pool.dma_start(pk[:, i, K_RB:K_RB + GROUPS], b_group[i].partition_broadcast(P)).then_inc(router_in, 16)
                pool.dma_start(pk[:, i, K_RB + GROUPS:K_SUB], b_router[i].partition_broadcast(P)).then_inc(router_in, 16)
            pool.wait_ge(st_mg, 4)
            pool.dma_start(mem_t_dram.rearrange("l p f -> p l f"), big[:, 1:3, :]).then_inc(st_msto, 16)
            with pool.Fori(0, LAYERS) as L:
                pool.wait_ge(st_msto, 16)
                pool.dma_start(memT[:], mem_t_dram[L].rearrange("p (c t) -> p c t", c=DC)).then_inc(mt_in, 16)
                for k in range(NQ):
                    pool.wait_ge(w_hi, k + 1)
                    pool.tensor_tensor(split_quarter(k, 1), landed_quarter(k), split_quarter(k, 0).bitcast(F32),
                                       ALU.subtract).then_inc(w_lo, 1)
                    if k % QUARTERS == QUARTERS - 1:
                        pool.wait_ge(w_lo, k + 1)
                        pool.sem_inc(split_out, 1)
                pool.wait_ge(mt_in, L * 16 + 16)
                pool.sem_inc(layer_end, 1)
                pool.wait_ge(layer_go, L + 1)
            pool.dma_start(memT[:, 0:FC, :].rearrange("p c t -> p (c t)"),
                           final_norm_g.partition_broadcast(P)).then_inc(fin_g, 16)
            pool.wait_ge(fin_g, 16)

        @block.scalar
        def _(act):
            act.dma_start(work[:, 0:T].bitcast(I32), positions[0].partition_broadcast(P)).then_inc(pos_in, 16)
            act.dma_start(cst[:], consts).then_inc(cst_in, 16)
            prow = big[:, 0, :].rearrange("p (l d) -> p l d", l=LAYERS)
            for s, r0, r1 in ((conv_dw.rearrange("l k d -> k l d"), 0, KERN), (conv_db, R_DB, R_DB + 1),
                              (conv_ln_g, R_LNG, R_LNG + 1), (conv_ln_b, R_LNB, R_LNB + 1),
                              (norm_mix_g, R_MIX, R_MIX + 1), (norm_mem_g, R_MEM, R_MEM + 1),
                              (norm_x_g, R_X, R_X + 1), (norm_ffn_g, R_FFN, R_FFN + 1)):
                s = s if r1 - r0 > 1 else s.rearrange("(o l) d -> o l d", o=1)
                act.dma_start(prow[r0:r1], s).then_inc(par_in, 16)
            for j, lv in enumerate((lam_q1, lam_k1, lam_q2, lam_k2)):
                for i in range(LAYERS):
                    act.dma_start(work[:, 1024 + (i * 4 + j) * 64:1024 + (i * 4 + j + 1) * 64],
                                  lv[i].partition_broadcast(P)).then_inc(lam_in, 16)
            for i in range(LAYERS):
                act.dma_start(pk[:, i, K_SUB:K_SUB + 1], subln_g[i].rearrange("(p o) -> p o", o=1)).then_inc(sub_in, 16)
            act.wait_ge(mem_in, 16)
            for s in range(TT):
                act.activation(uT[:, s * FC:(s + 1) * FC, :].rearrange("p c t -> p (c t)"), memN[:, s, :], ACT.Square,
                               accum_out=mss[:, s:s + 1]).then_inc(st_mss, 1)
            act.wait_ge(st_mvar, 1)
            act.activation(mss, mss, ACT.Sqrt).then_inc(st_msq, 1)
            act.wait_ge(st_ang, 1)
            act.activation(rope_cs[:], wk(512, 2, T), ACT.Sin).then_inc(st_cs, 1)
            act.wait_ge(st_dot, 1)
            act.activation(small[:, 108:112], small[:, 104:108], ACT.Exp).then_inc(st_exp, 1)

            q = act.alloc_register("act_pass")
            act.reg_mov(q, 0)
            u = act.alloc_register("act_unit")
            act.reg_mov(u, 0)

            def evac(job, dst, func=ACT.Copy, scale=1.0):
                b = bank(job)
                act.wait_ge(full[b], turn(job))
                src = ps[:, b, :]
                if len(dst.shape) == 3:
                    src = src.rearrange("p (c t) -> p c t", c=2)
                return act.activation(dst, src, func, scale=scale)

            act.wait_ge(x_in, 16)
            with act.Fori(0, LAYERS) as L:
                ch = Chain(act, ach)
                split = [0]

                def split_to(q):
                    for k in range(split[0], min(q, NQ)):
                        n = k // QUARTERS
                        if k % QUARTERS == 0:
                            act.wait_ge(slab_in[n % LAND], L * (16 * len(SLABS) // LAND) + 16 * (n // LAND + 1))
                        if k >= SPLITS:
                            act.wait_ge(w_used, k - SPLITS + 1)
                        act.activation(split_quarter(k, 0), landed_quarter(k), ACT.Copy).then_inc(w_hi, 1)
                    split[0] = max(split[0], q)

                def ahead(job):
                    split_to(LAST_QUARTER[job] + SPLITS)

                def squares(n):
                    for s in range(TT):
                        if n > 0:
                            act.wait_ge(h_ready, 4 * (n - 1) + 3 + s)
                        act.activation(uN[:, s, :], h[:, s, :], ACT.Square,
                                       accum_out=ss[:, s:s + 1]).then_inc(n_ss, 1)
                    act.wait_ge(n_var, n + 1)
                    act.activation(ss, ss, ACT.Sqrt).then_inc(n_root, 1)

                def turned(kind, dst, row):
                    for j in (1, 3):
                        b = bank(f"{kind}{j}")
                        act.wait_ge(full[b], turn(f"{kind}{j}"))
                        for c in range(2):
                            ins = act.activation(dst[:, 2 * j + c, :], ps[:, b, c * T:(c + 1) * T], ACT.Copy,
                                                 scale=par[:, 2 * j + c, row:row + 1])
                            if c == 0:
                                ins.then_inc(n_turned, 1)
                            else:
                                ins.then_inc(free[b], 1)

                def turned_high(kind, dst, row):
                    for j in range(4):
                        b = bank(f"{kind}{j}")
                        act.wait_ge(full[b], turn(f"{kind}{j}"))
                        for c in range(2):
                            act.activation(dst[0][:, 2 * j + c, :], ps[:, b, c * T:(c + 1) * T], ACT.Copy,
                                           scale=par[:, 2 * j + c, row:row + 1]).then_inc(hi_ready, 1)

                def out(job, dst, ready, n, func=ACT.Copy, scale=1.0):
                    if job in LAST_QUARTER:
                        ahead(job)
                    evac(job, dst, func, scale).then_inc(ready, 1)
                    act.wait_ge(ready, n)
                    act.sem_inc(free[bank(job)], 1)

                squares(0)
                act.wait_ge(cur_ready, 1)
                split_to(2)
                turned_high("nm", u_s, R_MIX)
                split_to(SPLITS)
                act.wait_ge(mt_in, L * 16 + 16)
                act.activation(mem_s[0], memT[:], ACT.Copy).then_inc(mem_hi, 1)
                for j in range(4):
                    if j >= 2:
                        act.wait_ge(glu_ready, j - 1)
                    out(f"g.{j}", sg[:, j % 2].rearrange("p c t -> p (c t)"), sig_ready, j + 1, ACT.Sigmoid)
                for j in range(8):
                    if j >= 2:
                        act.wait_ge(rope_ready, j - 1)
                    else:
                        act.wait_ge(glu_ready, 4)
                    job = f"q.{j}" if j < 4 else f"k.{j - 4}"
                    out(job, qraw[:, j % 2].rearrange("p c t -> p (c t)"), qraw_ready, j + 1,
                        scale=0.125 if j < 4 else 1.0)
                for j in range(4):
                    out(f"v.{j}", v[:, j % 2, (j // 2) * SLAB:(j // 2 + 1) * SLAB], v_ready, j + 1)
                act.wait_ge(rope_ready, 8)
                for s in range(ATTN_STEPS + 1):
                    if s < ATTN_STEPS:
                        split_to(QUARTERS * SLABS.index("gc0") + s + 3)
                        act.wait_ge(nm_ready, s + 1)
                        if s >= 2:
                            act.wait_ge(a_ready, s - 1)
                        for c in range(2):
                            ins = act.activation(E[:, s % 2, c, :], ps[:, score_banks(s) + c, 0:T], ACT.Exp,
                                                 bias=nmx[:, s, c:c + 1], accum_out=sm[:, s, c:c + 1])
                            ins.then_inc(exp_ready, 1)
                    if s >= 1:
                        act.wait_ge(at_full, s)
                        act.activation(aTs[:, (s - 1) % 2, :], ps[:, MIX_BANK, 0:T], ACT.Copy).then_inc(at_ready, 1)
                    if s >= 5 and s % 4 == 1 or s == ATTN_STEPS:
                        if s == ATTN_STEPS:
                            g = ATTN_STEPS // 4 - 1
                        else:
                            g = (s - 5) // 4
                        act.wait_ge(pv_full, g + 1)
                        act.activation(o_all[:, 4 * g:4 * g + 4, :].rearrange("p s e -> p (s e)"), ps[:, VALUE_BANK, :],
                                       ACT.Copy).then_inc(o_ready, 1)
                    if s == 6:
                        act.wait_ge(ln_xc, 1)
                        act.activation(sq, conv, ACT.Square).then_inc(ln_sq, 1)
                split_to(QUARTERS * SLABS.index("xk0") + 3)
                act.wait_ge(ln_var, 1)
                act.activation(rs_ln[:], rs_ln[:], ACT.Sqrt).then_inc(ln_root, 1)
                act.wait_ge(o_var, 1)
                act.activation(ssq, ssq, ACT.Sqrt).then_inc(o_root, 1)
                for j, g in enumerate((gate_c, gate_a)):
                    act.wait_ge(gate_raw, 4 * (j + 1))
                    act.activation(g, g, ACT.Sigmoid).then_inc(gate_ready, 1)
                for j in range(2):
                    out(f"xk.{j}", xkT[:, 2 * j:2 * j + 2, :], xk_ready, j + 1)
                for j in range(4):
                    act.wait_ge(full[bank(f"oT{j}")], turn(f"oT{j}"))
                    act.activation(o_s[0][:, 2 * j:2 * j + 2, :], ps[:, bank(f"oT{j}"), :].rearrange("p (c t) -> p c t", c=2),
                                   ACT.Copy, scale=sub_col).then_inc(hi_ready, 1)
                split_to(QUARTERS * SLABS.index("xk1") + 4)
                act.wait_ge(ln_y, 1)
                for c in range(DC):
                    act.activation(conv[:, c, :], conv[:, c, :], ACT.Silu, bias=par[:, c, R_LNB:R_LNB + 1],
                                   scale=par[:, c, R_LNG:R_LNG + 1]).then_inc(ln_out, 1)
                act.wait_ge(ln_out, DC)
                act.activation(conv_s[0], conv, ACT.Copy).then_inc(conv_hi_ready, 1)
                for j in range(2, 4):
                    out(f"xk.{j}", xkT[:, 2 * j:2 * j + 2, :], xk_ready, j + 1)
                for j in range(2):
                    out(f"xv.{j}", xv[:, j % 2, 0:SLAB], xv_ready, j + 1)
                ahead("wo.3")
                squares(1)
                for j in range(2, 4):
                    out(f"xv.{j}", xv[:, j % 2, SLAB:2 * SLAB], xv_ready, j + 1)
                turned_high("nx", x_s, R_X)

                def xexp(hd):
                    act.wait_ge(xnm_ready, hd + 1)
                    for s in range(TT):
                        act.activation(E[:, hd % 2, s, :], ps[:, 4 + hd % 2, s * T:(s + 1) * T], ACT.Exp,
                                       bias=xnm[:, hd, s:s + 1], accum_out=xsm[:, hd, s:s + 1]).then_inc(xexp_ready, 1)

                def xturn(hd):
                    act.wait_ge(xt_full, hd + 1)
                    act.activation(pT[:, hd % 2, :], ps[:, 6 + hd % 2, :], ACT.Copy).then_inc(xt_ready, 1)

                def xq_out(j):
                    out(f"xq.{j}", xqT[:, 2 * j:2 * j + 2, :].rearrange("p c t -> p (c t)"), xq_ready, j + 1,
                        scale=1.0 / 16)

                xq_out(0)
                xq_out(1)
                xq_out(2)
                xexp(0)
                xq_out(3)
                xexp(1)
                xturn(0)
                xexp(2)
                xturn(1)
                xexp(3)
                xturn(2)
                xturn(3)
                split_to(NQ)
                squares(2)
                turned("nf", uT, R_FFN)
                act.wait_ge(r_diff, 1)
                act.activation(e_g, d_g, ACT.Exp).then_inc(r_exp, 1)
                act.wait_ge(r_gap, 1)
                act.activation(e_gap, gap, ACT.Exp).then_inc(r_gexp, 1)

                act.wait_ge(rank_ready, 1)
                passes = act.value_load(npass_i[0:1, 0:1], min_val=1, max_val=MAX_PASSES)
                with act.Fori(0, passes) as _p:
                    with act.Fori(0, PAIRS) as _i:
                        n = act.snap(u)
                        act.wait_ge(gt_done, n + 1)
                        act.activation(scat[:, 0, :], ps[:, 2, 0:T], ACT.Copy, scale=cst[:, C_MLO:C_MLO + 1])
                        act.activation(scat[:, 1, :], ps[:, 2, 0:T], ACT.Copy,
                                       scale=cst[:, C_MHI:C_MHI + 1]).then_inc(scat_ready, 1)
                        act.wait_ge(up_done, n + 1)
                        act.activation(up_sb, ps[:, 1, :], ACT.Copy).then_inc(up_out, 1)
                        act.wait_ge(upt_done, n + 1)
                        a4 = ps[:, 2, :].rearrange("p (f e w s) -> p f e w s", f=FC, e=2, w=2)
                        act.activation(silu_t, a4[:, :, :, 0, :], ACT.Silu).then_inc(silu_ready, 1)
                        act.reg_add(u, u, 1)
                    n = act.snap(u)
                    k = act.snap(q)
                    act.wait_ge(added, n)
                    act.activation(h[:, 1, :], ps[:, 6:8, :].rearrange("p b n -> p (b n)"), ACT.Copy).then_inc(h_back, 1)
                    act.wait_ge(h_back, k * 2 + 2)
                    act.reg_add(q, q, 1)
                act.drain().then_inc(layer_end, 1)
                act.wait_ge(layer_go, L + 1)
            for s in range(TT):
                act.activation(uT[:, s * FC:(s + 1) * FC, :].rearrange("p c t -> p (c t)"), h[:, s, :], ACT.Square,
                               accum_out=ss[:, s:s + 1]).then_inc(fin_ss, 1)
            act.wait_ge(fin_var, 1)
            act.activation(ss, ss, ACT.Sqrt).then_inc(fin_sq, 1)

        @block.vector
        def _(dve):
            sc = Chain(dve, st_ch)
            dve.memset(glu_pad[:], 0.0)
            dve.wait_ge(pos_in, 16)
            dve.wait_ge(cst_in, 16)
            posf = wk(256, T)
            ang, turns, red = posf, wk(512, 2, T), wk(512, 2, T)
            sc.link(dve.tensor_copy(posf, work[:, 0:T].bitcast(I32)))
            sc.link(dve.tensor_scalar(ang, posf, cst[:, C_INVF:C_INVF + 1], None, ALU.mult))
            kk = rt2
            sc.link(dve.tensor_scalar(kk[:, 1, :], ang, 1.0 / (2 * math.pi), 0.0, ALU.mult, ALU.add))
            sc.link(dve.tensor_scalar(kk[:, 0, :], ang, 1.0 / (2 * math.pi), 0.25, ALU.mult, ALU.add))
            sc.link(dve.tensor_scalar(kk, kk, MAGIC, None, ALU.add))
            sc.link(dve.tensor_scalar(kk, kk, MAGIC, None, ALU.subtract))
            prev = ang.unsqueeze(1).to_broadcast([P, 2, T])
            for part in TWO_PI:
                sc.link(dve.scalar_tensor_tensor(red, kk, -part, prev, ALU.mult, ALU.add))
                prev = red
            sc.link(dve.tensor_scalar(red[:, 0, :], red[:, 0, :], math.pi / 2, None, ALU.add))
            ins = dve.tensor_scalar(red, red, SIN_MAX, -SIN_MAX, ALU.min, ALU.max)
            ins.then_inc(st_ang, 1)
            dve.wait_ge(st_mss, TT)
            dve.tensor_scalar(mss, mss, 1.0 / D, RMS_EPS, ALU.mult, ALU.add).then_inc(st_mvar, 1)
            dve.wait_ge(st_msq, 1)
            sc.link(dve.reciprocal(mss, mss))
            for s in range(TT):
                dve.tensor_scalar(memN[:, s, :], memN[:, s, :], mss[:, s:s + 1], None, ALU.mult).then_inc(st_mn, 1)
            dve.wait_ge(st_rows, 1)
            for i in range(LAYERS):
                sc.link(dve.tensor_copy(pk[:, i, 0:K_WR], ps[:, 4 + i, 0:K_WR]))
            dve.wait_ge(st_mt, 1)
            for j in range(4):
                for i in range(LAYERS):
                    gain = pk[:, i, 0:K_WR].rearrange("p (c r) -> p c r", c=DC)[:, 2 * j:2 * j + 2, R_MEM]
                    ins = dve.tensor_tensor(chunks(1 + i)[:, 2 * j:2 * j + 2, :],
                                            ps[:, j, :].rearrange("p (c t) -> p c t", c=2),
                                            gain.unsqueeze(2).to_broadcast([P, 2, T]), ALU.mult)
                ins.then_inc(st_mg, 1)

            q = dve.alloc_register("dve_pass")
            dve.reg_mov(q, 0)
            u = dve.alloc_register("dve_unit")
            dve.reg_mov(u, 0)
            dve.wait_ge(lam_in, 16 * 4 * LAYERS)
            dve.wait_ge(st_cs, 1)
            lv = work[:, 1024:1024 + LAYERS * 256].rearrange("p (l w d) -> p l w d", l=2 * LAYERS, w=2)
            lp = wk(1024 + LAYERS * 256, 2 * LAYERS, 64)
            sc.link(dve.tensor_tensor(lp, lv[:, :, 0, :], lv[:, :, 1, :], ALU.mult))
            dve.tensor_reduce(small[:, 104:108], lp, AX.X, ALU.add).then_inc(st_dot, 1)
            dve.wait_ge(st_exp, 1)
            for i in range(LAYERS):
                lam = pk[:, i, K_LAM:K_LAM + 1]
                sc.link(dve.tensor_tensor(lam, small[:, 109 + 2 * i:110 + 2 * i], small[:, 108 + 2 * i:109 + 2 * i],
                                          ALU.subtract))
                sc.link(dve.tensor_tensor(lam, lam, cst[:, C_LAM + i:C_LAM + i + 1], ALU.subtract))
            dve.wait_ge(sub_in, 16 * LAYERS)
            for i in range(LAYERS):
                sc.link(dve.tensor_scalar(pk[:, i, K_SUB:K_SUB + 1], pk[:, i, K_SUB:K_SUB + 1],
                                          cst[:, C_OML + i:C_OML + i + 1], None, ALU.mult))

            with dve.Fori(0, LAYERS) as L:
                ch = Chain(dve, dch)

                def both(job):
                    return ps[:, bank(job), :].rearrange("p (c t) -> p c t", c=2)

                def bcast(job, n, row):
                    return par[:, n:n + 2, row].unsqueeze(2).to_broadcast([P, 2, T])

                def norm(n):
                    dve.wait_ge(n_ss, TT * (n + 1))
                    dve.tensor_scalar(ss, ss, 1.0 / D, RMS_EPS, ALU.mult, ALU.add).then_inc(n_var, 1)
                    dve.wait_ge(n_root, n + 1)
                    ch.link(dve.reciprocal(ss, ss))
                    for s in range(TT):
                        dve.tensor_scalar(uN[:, s, :], h[:, s, :], ss[:, s:s + 1], None, ALU.mult).then_inc(n_ready, 1)

                def turned(kind, dst, row):
                    for j in (0, 2):
                        job = f"{kind}{j}"
                        dve.wait_ge(full[bank(job)], turn(job))
                        dve.tensor_tensor(dst[:, 2 * j:2 * j + 2, :], both(job), bcast(job, 2 * j, row),
                                          ALU.mult).then_inc(free[bank(job)], 1)

                def low(job, dst, c, n, have, scale, ready):
                    hi, lo = (d[:, c:c + n, :] for d in dst)
                    at = c % 2
                    dve.wait_ge(*have)
                    dve.scalar_tensor_tensor(lo, both(job)[:, at:at + n, :], scale, hi.bitcast(F32), ALU.mult,
                                             ALU.subtract).then_inc(ready, 1)

                def turned_low(kind, dst, row, n):
                    for c in range(DC):
                        low(f"{kind}{c // 2}", dst, c, 1, (hi_ready, n + 2 * (c // 2) + 2), par[:, c, row:row + 1], lo_ready)
                        if c % 2:
                            dve.wait_ge(lo_ready, n + c + 1)
                            dve.sem_inc(free[bank(f"{kind}{c // 2}")], 1)

                dve.tensor_copy(cur[:, 0:K_WR], pk[:, L, 0:K_WR]).then_inc(cur_ready, 1)
                dve.wait_ge(cur_ready, 1)
                norm(0)
                turned_low("nm", u_s, R_MIX, 0)
                dve.wait_ge(mem_hi, 1)
                dve.tensor_tensor(mem_s[1], memT[:], mem_s[0].bitcast(F32), ALU.subtract).then_inc(mem_lo, 1)

                conv_last = {}
                taps = [(c0, t) for c0 in range(0, DC, 2) for t in range(KERN)]

                def conv_taps(n, have):
                    for _ in range(n):
                        if not taps or taps[0][0] // 2 >= have:
                            return
                        c0, t = taps.pop(0)
                        for c in (c0, c0 + 1):
                            src, wt = glu_pad[:, c, t:t + T], par[:, c, t:t + 1]
                            if t == 0:
                                dve.wait_ge(glu_ready, c0 // 2 + 1)
                                ins = dve.tensor_scalar(conv[:, c, :], src, wt, par[:, c, R_DB:R_DB + 1], ALU.mult, ALU.add)
                            else:
                                ch.after(conv_last[c])
                                ins = dve.scalar_tensor_tensor(conv[:, c, :], src, wt, conv[:, c, :], ALU.mult, ALU.add)
                            if not taps and c == c0 + 1:
                                ins.then_inc(conv_ready, 1)
                            else:
                                conv_last[c] = ch.note(ins)

                for j in range(4):
                    dve.wait_ge(sig_ready, j + 1)
                    dve.wait_ge(full[bank(f"a.{j}")], turn(f"a.{j}"))
                    dve.tensor_tensor(glu[:, 2 * j:2 * j + 2, :], both(f"a.{j}"), sg[:, j % 2], ALU.mult).then_inc(glu_ready, 1)
                    dve.wait_ge(glu_ready, j + 1)
                    dve.sem_inc(free[bank(f"a.{j}")], 1)
                    conv_taps((8, 26, 8, 8)[j], j + 1)
                dve.wait_ge(router_in, 16 * 4 * LAYERS)
                dve.tensor_copy(cur[:, K_WR:NPK], pk[:, L, K_WR:NPK]).then_inc(cur_ready, 1)
                dve.wait_ge(cur_ready, 2)
                dve.wait_ge(st_msto, 16)
                cos2 = rope_cs[:, 0:1, :].to_broadcast([P, 2, T])
                sin2 = rope_cs[:, 1:2, :].to_broadcast([P, 2, T])
                for j in range(8):
                    job = f"q.{j}" if j < 4 else f"k.{j - 4}"
                    dst = (qT if j < 4 else kT)[:, 2 * (j % 4):2 * (j % 4) + 2, :]
                    dve.wait_ge(qraw_ready, j + 1)
                    k1 = ch.note(dve.tensor_tensor(rt1, qraw[:, j % 2], cos2, ALU.mult))
                    conv_taps(4, 4)
                    dve.wait_ge(rope_full, j + 1)
                    k2 = ch.note(dve.tensor_tensor(rt2, ps[:, ROPE_BANK, :].rearrange("p (c t) -> p c t", c=2), sin2, ALU.mult))
                    conv_taps(1, 4)
                    ch.after(k2)
                    dve.tensor_tensor(dst, rt1, rt2, ALU.add).then_inc(rope_ready, 1)
                    conv_taps(3, 4)
                conv_taps(len(taps), 4)

                def row_max(s):
                    dve.wait_ge(s_full, s + 1)
                    dve.tensor_reduce(nmx[:, s, :], ps[:, score_banks(s):score_banks(s) + 2, 0:T], AX.X, ALU.max,
                                      negate=True).then_inc(nm_ready, 1)

                dve.wait_ge(rope_ready, 8)
                row_max(0)
                for s in range(ATTN_STEPS):
                    if s + 1 < ATTN_STEPS:
                        row_max(s + 1)
                    dve.wait_ge(exp_ready, 2 * (s + 1))
                    rc = sm[:, s, :]
                    if s >= 1:
                        dve.wait_ge(a_ready, s)
                    ch.link(dve.reciprocal(rc, rc))
                    ch.link(dve.tensor_scalar(rc[:, 1:2], rc[:, 1:2], neglam, None, ALU.mult))
                    ch.link(dve.tensor_scalar(etmp, E[:, s % 2, 1, :], rc[:, 1:2], None, ALU.mult))
                    if s >= 2:
                        dve.wait_ge(at_full, s - 1)
                    dve.scalar_tensor_tensor(amix[:, s % 2, :], E[:, s % 2, 0, :], rc[:, 0:1], etmp, ALU.mult,
                                             ALU.add).then_inc(a_ready, 1)
                    if s % 2 == 1:
                        job = f"gate.{s // 2}"
                        g, j = ((gate_c, s // 2) if s < 8 else (gate_a, s // 2 - 4))
                        dve.wait_ge(full[bank(job)], turn(job))
                        dve.tensor_copy(g[:, 2 * j:2 * j + 2, :], both(job)).then_inc(gate_raw, 1)
                        dve.wait_ge(gate_raw, s // 2 + 1)
                        dve.sem_inc(free[bank(job)], 1)
                    if s == 3:
                        dve.wait_ge(full[bank("mean")], turn("mean"))
                        dve.wait_ge(conv_ready, 1)
                        mu = ps[:, bank("mean"), 0:T].unsqueeze(1).to_broadcast([P, DC, T])
                        dve.tensor_tensor(conv, conv, mu, ALU.subtract).then_inc(ln_xc, 1)
                        dve.wait_ge(ln_xc, 1)
                        dve.sem_inc(free[bank("mean")], 1)
                    if s == 9:
                        dve.wait_ge(full[bank("var")], turn("var"))
                        dve.tensor_scalar(rs_ln[:], ps[:, bank("var"), 0:T], LN_EPS, None, ALU.add).then_inc(ln_var, 1)
                        dve.wait_ge(ln_var, 1)
                        dve.sem_inc(free[bank("var")], 1)
                dve.wait_ge(o_ready, 4)
                sqo = uT[:].rearrange("p c t -> p (c t)").rearrange("p (s e) -> p s e", s=ATTN_STEPS)
                ch.link(dve.tensor_tensor(sqo, o_all, o_all, ALU.mult))
                ch.link(dve.tensor_reduce(ssq, sqo, AX.X, ALU.add))
                dve.tensor_scalar(ssq, ssq, 1.0 / P, LN_EPS, ALU.mult, ALU.add).then_inc(o_var, 1)
                dve.wait_ge(o_root, 1)
                ch.link(dve.reciprocal(ssq, ssq))
                dve.tensor_tensor(o_all, o_all, ssq.unsqueeze(2).to_broadcast([P, ATTN_STEPS, P]),
                                  ALU.mult).then_inc(o_norm, 1)
                dve.wait_ge(ln_root, 1)
                ch.link(dve.reciprocal(rs_ln[:], rs_ln[:]))
                dve.tensor_tensor(conv, conv, rs_ln[:].unsqueeze(1).to_broadcast([P, DC, T]), ALU.mult).then_inc(ln_y, 1)
                for j in range(4):
                    low(f"oT{j}", o_s, 2 * j, 2, (hi_ready, DC + j + 1), sub_col, lo_ready)
                    dve.wait_ge(lo_ready, DC + j + 1)
                    dve.sem_inc(free[bank(f"oT{j}")], 1)
                dve.wait_ge(conv_hi_ready, 1)
                dve.tensor_tensor(conv_s[1], conv, conv_s[0].bitcast(F32), ALU.subtract).then_inc(conv_lo_ready, 1)
                dve.wait_ge(gate_ready, 2)
                mg = {}
                for j in range(4):
                    job = f"ao.{j}"
                    dve.wait_ge(full[bank(job)], turn(job))
                    mg[j] = ch.note(dve.tensor_tensor(merged[:, 2 * j:2 * j + 2, :], both(job),
                                                      gate_a[:, 2 * j:2 * j + 2, :], ALU.mult))
                    ch.after(mg[j])
                    dve.sem_inc(free[bank(job)], 1)
                for j in range(4):
                    job = f"co.{j}"
                    dve.wait_ge(full[bank(job)], turn(job))
                    g = gate_c[:, 2 * j:2 * j + 2, :]
                    ch.link(dve.tensor_tensor(g, both(job), g, ALU.mult))
                    dve.sem_inc(free[bank(job)], 1)
                    m = merged[:, 2 * j:2 * j + 2, :]
                    hi, lo = (d[:, 2 * j:2 * j + 2, :] for d in m_s)
                    dve.tensor_tensor(hi, m, g, ALU.add).then_inc(m_hi, 1)
                    ch.link(dve.tensor_tensor(m, m, g, ALU.add))
                    dve.wait_ge(m_hi, j + 1)
                    dve.tensor_tensor(lo, m, hi.bitcast(F32), ALU.subtract).then_inc(merged_ready, 1)

                def add_to_h(kind, base):
                    for j in range(4):
                        job, s, half = f"{kind}{j}", j % 2, j // 2
                        dve.wait_ge(full[bank(job)], turn(job))
                        hs = h[:, s, half * SLAB:(half + 1) * SLAB]
                        dve.tensor_tensor(hs, hs, ps[:, bank(job), :], ALU.add).then_inc(h_ready, 1)
                        dve.wait_ge(h_ready, base + j + 1)
                        dve.sem_inc(free[bank(job)], 1)

                add_to_h("wo.", 0)
                norm(1)
                turned_low("nx", x_s, R_X, DC + 4)

                def xmax(hd):
                    dve.wait_ge(xs_full, hd + 1)
                    dve.tensor_reduce(xnm[:, hd, :], ps[:, 4 + hd % 2, :].rearrange("p (s k) -> p s k", s=TT), AX.X,
                                      ALU.max, negate=True).then_inc(xnm_ready, 1)

                def xscale(hd):
                    dve.wait_ge(xexp_ready, TT * (hd + 1))
                    ch.link(dve.reciprocal(xsm[:, hd, :], xsm[:, hd, :]))
                    for s in range(TT):
                        dve.tensor_scalar(E[:, hd % 2, s, :], E[:, hd % 2, s, :], xsm[:, hd, s:s + 1], None,
                                          ALU.mult).then_inc(xp_ready, 1)

                def px_out(hd):
                    job = f"px{hd}"
                    dve.wait_ge(full[bank(job)], turn(job))
                    hi, lo = (d[:, 2 * hd:2 * hd + 2, :] for d in xo_s)
                    dve.tensor_copy(hi, both(job)).then_inc(xo_hi, 1)
                    dve.wait_ge(xo_hi, hd + 1)
                    dve.tensor_tensor(lo, both(job), hi.bitcast(F32), ALU.subtract).then_inc(xo_ready, 1)
                    dve.wait_ge(xo_ready, hd + 1)
                    dve.sem_inc(free[bank(job)], 1)

                xmax(0)
                xscale(0)
                for hd in range(1, XHEADS):
                    xmax(hd)
                    xscale(hd)
                    if hd >= 2:
                        px_out(hd - 2)
                px_out(2)
                px_out(3)
                add_to_h("xo.", 4)
                norm(2)
                turned("nf", uT, R_FFN)

                def over(a, n):
                    return a.unsqueeze(2).to_broadcast([P, TT, n])

                def desc(n):
                    return cst[:, C_DESC + EXPERTS - n:C_DESC + EXPERTS].unsqueeze(1).to_broadcast([P, TT, n])

                dve.wait_ge(full[bank("router")], turn("router"))
                ch.link(dve.tensor_tensor(logit, ps[:, bank("router"), 0:TT * NR].rearrange("p (s n) -> p s n", s=TT),
                                          rb.unsqueeze(1).to_broadcast([P, TT, NR]), ALU.add))
                lg = logit[:, :, 0:GROUPS]
                ch.link(dve.tensor_reduce(m_g, lg, AX.X, ALU.max))
                dve.tensor_tensor(d_g, lg, over(m_g, GROUPS), ALU.subtract).then_inc(r_diff, 1)
                ch.link(dve.tensor_tensor(eq_g, lg, over(m_g, GROUPS), ALU.is_equal))
                ch.link(dve.tensor_tensor(eq_g, eq_g, desc(GROUPS), ALU.mult))
                ch.link(dve.tensor_reduce(mx_g, eq_g, AX.X, ALU.max))
                ch.link(dve.tensor_tensor(oh_g, eq_g, over(mx_g, GROUPS), ALU.is_equal))
                ch.link(dve.tensor_scalar(oh_g, oh_g, -1.0, 1e30, ALU.add, ALU.mult))
                for s in range(TT):
                    ch.link(dve.tensor_tensor(masked[:, s, :].rearrange("p (g e) -> p g e", g=GROUPS),
                                              logit[:, s, GROUPS:NR].rearrange("p (g e) -> p g e", g=GROUPS),
                                              oh_g[:, s, :].unsqueeze(2).to_broadcast([P, GROUPS, PER_GROUP]), ALU.add))
                for top, oh in ((top1, oh1), (top2, oh2)):
                    ch.link(dve.tensor_reduce(top, masked, AX.X, ALU.max))
                    ch.link(dve.tensor_tensor(first, masked, over(top, EXPERTS), ALU.is_equal))
                    ch.link(dve.tensor_tensor(first, first, desc(EXPERTS), ALU.mult))
                    ch.link(dve.tensor_reduce(mx_e, first, AX.X, ALU.max))
                    ch.link(dve.tensor_tensor(oh, first, over(mx_e, EXPERTS), ALU.is_equal))
                    if oh is oh1:
                        ch.link(dve.scalar_tensor_tensor(masked, oh1, -3e30, masked, ALU.mult, ALU.add))
                dve.tensor_tensor(gap, top2, top1, ALU.subtract).then_inc(r_gap, 1)
                dve.tensor_tensor(picked, oh1, oh2, ALU.add).then_inc(r_mask, 1)
                dve.wait_ge(r_exp, 1)
                ch.link(dve.tensor_reduce(g_w, e_g, AX.X, ALU.add))
                ch.link(dve.reciprocal(g_w, g_w))
                dve.wait_ge(r_gexp, 1)
                ch.link(dve.tensor_scalar(w_1, e_gap, 1.0, None, ALU.add))
                ch.link(dve.reciprocal(w_1, w_1))
                ch.link(dve.tensor_tensor(w_1, w_1, g_w, ALU.mult))
                ch.link(dve.tensor_tensor(w_2, w_1, e_gap, ALU.mult))
                ch.link(dve.tensor_tensor(tok_w, oh1, over(w_1, EXPERTS), ALU.mult))
                ch.link(dve.tensor_tensor(tok_w2, oh2, over(w_2, EXPERTS), ALU.mult))
                ch.link(dve.tensor_tensor(tok_w, tok_w, tok_w2, ALU.add))
                rkb = ps[:, bank("rank"), :]
                dve.wait_ge(full[bank("rank")], turn("rank"))
                ch.link(dve.tensor_scalar(rank, rkb[:, 0:TT * EXPERTS].rearrange("p (s e) -> p s e", s=TT), float(D), 1.0,
                                          ALU.mult, ALU.add))
                ch.link(dve.tensor_tensor(rank, rank, picked, ALU.mult))
                ch.link(dve.tensor_scalar(rank, rank, -1.0, None, ALU.add))
                ch.link(dve.tensor_reduce(cnt1, rkb[:, TT * EXPERTS:(TT + 1) * EXPERTS], AX.X, ALU.max))
                ch.link(dve.tensor_scalar(cnt1, cnt1, float(D), None, ALU.mult))
                ch.link(dve.tensor_tensor(thr7, cst[:, C_THR:C_THR + MAX_PASSES - 1],
                                          cnt1.to_broadcast([P, MAX_PASSES - 1]), ALU.is_lt))
                ch.link(dve.tensor_reduce(cnt1, thr7, AX.X, ALU.add))
                dve.tensor_scalar(npass_i[:], cnt1, 1.0, None, ALU.add).then_inc(rank_ready, 1)
                dve.wait_ge(rank_ready, 1)
                dve.sem_inc(np_ready, 1)

                passes = dve.value_load(npass_i[0:1, 0:1], min_val=1, max_val=MAX_PASSES)
                with dve.Fori(0, passes) as _p:
                    with dve.Fori(0, PAIRS) as i:
                        n = dve.snap(u)
                        dve.tensor_tensor(sel, rank[:, :, bass.ds(i * 2, 2)].unsqueeze(3).to_broadcast([P, TT, 2, CAP]),
                                          iota.unsqueeze(1).unsqueeze(1).to_broadcast([P, TT, 2, CAP]),
                                          ALU.is_equal).then_inc(sel_ready, 1)
                        dve.wait_ge(sel_ready, n + 1)
                        for dup in range(2):
                            dve.tensor_tensor(spread[:, :, :, dup, :], sel,
                                              tok_w[:, :, bass.ds(i * 2, 2)].unsqueeze(3).to_broadcast([P, TT, 2, CAP]),
                                              ALU.mult).then_inc(spread_ready, 1)
                        dve.wait_ge(xg_done, n + 1)
                        dve.tensor_tensor(xe, ps[:, 0, :].rearrange("p (c s) -> p c s", c=DC),
                                          par[:, :, R_FFN].unsqueeze(2).to_broadcast([P, DC, 2 * CAP]),
                                          ALU.mult).then_inc(xe_ready, 1)
                        dve.wait_ge(silu_ready, n + 1)
                        a4 = ps[:, 2, :].rearrange("p (f e w s) -> p f e w s", f=FC, e=2, w=2)
                        dve.tensor_tensor(up_t, silu_t, a4[:, :, :, 1, :], ALU.mult).then_inc(upt_ready, 1)
                        dve.wait_ge(y_done, n + 1)
                        dve.tensor_copy(y_sb, ps[:, 3, :]).then_inc(y_out, 1)
                        dve.reg_add(u, u, 1)
                    n = dve.snap(u)
                    k = dve.snap(q)
                    dve.wait_ge(added, n)
                    dve.tensor_copy(h[:, 0, :], ps[:, 4:6, :].rearrange("p b n -> p (b n)")).then_inc(h_back, 1)
                    dve.wait_ge(h_back, k * 2 + 2)
                    dve.tensor_scalar(rank, rank, -float(CAP), None, ALU.add)
                    dve.drain()
                    dve.reg_add(q, q, 1)
                dve.drain()
                dve.wait_ge(layer_end, 3 * L + 3)
                dve.sem_inc(layer_clear, 1)
                dve.sem_clear(cleared)
                dve.sem_inc(layer_go, 1)

            fc = Chain(dve, fin_ch)
            dve.wait_ge(fin_ss, TT)
            dve.tensor_scalar(ss, ss, 1.0 / D, RMS_EPS, ALU.mult, ALU.add).then_inc(fin_var, 1)
            dve.wait_ge(fin_sq, 1)
            fc.link(dve.reciprocal(ss, ss))
            dve.wait_ge(fin_g, 16)
            for s in range(TT):
                dve.scalar_tensor_tensor(uN[:, s, :], h[:, s, :], ss[:, s:s + 1],
                                         memT[:, 0:FC, :].rearrange("p c t -> p (c t)"), ALU.mult,
                                         ALU.mult).then_inc(fin_out, 1)

        @block.tensor
        def _(pe):
            prow = big[:, 0, :].rearrange("p (l d) -> p l d", l=LAYERS)
            pe.sem_inc(freed, RING)
            pe.wait_ge(cst_in, 16)
            pe.wait_ge(par_in, 16 * 8)
            for i in range(LAYERS):
                for c in range(DC):
                    last = pe.transpose(ps[:, 4 + i, c * ROWS:(c + 1) * ROWS], prow[0:ROWS, i, c * P:(c + 1) * P],
                                        ident[0:ROWS, 0:ROWS])
            last.then_inc(st_rows, 1)

            def turn_rows(dst, src, j):
                for c in range(2):
                    for s in range(TT):
                        last = pe.transpose(dst[:, c * T + s * P:c * T + (s + 1) * P],
                                            src[:, s, (2 * j + c) * P:(2 * j + c + 1) * P], ident)
                return last

            pe.wait_ge(st_mn, TT)
            for j in range(4):
                last = turn_rows(ps[:, j, :], memN, j)
            last.then_inc(st_mt, 1)
            pe.wait_ge(st_mg, 4)

            u = pe.alloc_register("pe_unit")
            pe.reg_mov(u, 0)
            q = pe.alloc_register("pe_pass")
            pe.reg_mov(q, 0)
            with pe.Fori(0, LAYERS) as L:
                def begin(job):
                    if turn(job) > 1:
                        pe.wait_ge(free[bank(job)], turn(job) - 1)
                    return ps[:, bank(job), :]

                owed = []

                def settle():
                    for job in owed:
                        pe.wait_ge(full[bank(job)], turn(job))
                        pe.sem_inc(w_used, 1)
                    owed.clear()

                def used(last, job, more=()):
                    if job is None:
                        last.then_inc(w_used, 1)
                    else:
                        last.then_inc(full[bank(job)], 1)
                        owed.append(job)

                def columns(dst, q, xs, job=None):
                    hi, lo = split_quarter(q, 0), split_quarter(q, 1)
                    pe.wait_ge(w_hi, q + 1)
                    for k in range(DC):
                        pe.matmul(dst, hi[:, k, :], xs[0][:, k, :], start=(k == 0), stop=False)
                        pe.matmul(dst, hi[:, k, :], xs[1][:, k, :], start=False, stop=False)
                    settle()
                    pe.wait_ge(w_lo, q + 1)
                    for k in range(DC):
                        last = pe.matmul(dst, lo[:, k, :], xs[0][:, k, :], start=False, stop=(k == DC - 1))
                    used(last, job)

                def col_jobs(kind, slab, jobs, xs, after=None):
                    q = QUARTERS * SLABS.index(slab)
                    for n, j in enumerate(jobs):
                        job = f"{kind}{j}"
                        dst = begin(job)
                        for c in range(2):
                            columns(dst[:, c * T:(c + 1) * T], q + 2 * n + c, xs, job if c else None)
                        if after:
                            after(j)

                def row_jobs(kind, slab, jobs, xs, after=None):
                    q0 = QUARTERS * SLABS.index(slab)
                    dst = [begin(f"{kind}{j}") for j in jobs]
                    for c in range(QUARTERS):
                        q = q0 + c
                        hi, lo = split_quarter(q, 0), split_quarter(q, 1)
                        pe.wait_ge(w_hi, q + 1)
                        for s in range(TT):
                            for k in range(2):
                                xh, xl = (d[:, 2 * c + k, s * P:(s + 1) * P] for d in xs)
                                pe.matmul(dst[s], xh, hi[:, k, :], start=(c == 0 and k == 0), stop=False)
                                pe.matmul(dst[s], xl, hi[:, k, :], start=False, stop=False)
                        settle()
                        pe.wait_ge(w_lo, q + 1)
                        for s in range(TT):
                            for k in range(2):
                                last = pe.matmul(dst[s], xs[0][:, 2 * c + k, s * P:(s + 1) * P], lo[:, k, :],
                                                 start=False, stop=(c == QUARTERS - 1 and k == 1))
                            if c == QUARTERS - 1 and s < TT - 1:
                                last.then_inc(full[bank(f"{kind}{jobs[s]}")], 1)
                        used(last, f"{kind}{jobs[-1]}" if c == QUARTERS - 1 else None)
                        if after and c == 0:
                            after()

                def turn_norm(kind, n):
                    pe.wait_ge(n_ready, TT * (n + 1))
                    for j in range(4):
                        job = f"{kind}{j}"
                        turn_rows(begin(job), uN, j).then_inc(full[bank(job)], 1)
                    for j in range(4):
                        pe.wait_ge(free[bank(f"{kind}{j}")], turn(f"{kind}{j}"))

                turn_norm("nm", 0)
                col_jobs("a.", "a0", (0, 1), u_s)
                col_jobs("g.", "g0", (0, 1), u_s)
                col_jobs("a.", "a1", (2, 3), u_s)
                col_jobs("g.", "g1", (2, 3), u_s)

                def rotate(j):
                    pe.wait_ge(qraw_ready, j + 1)
                    if j >= 1:
                        pe.wait_ge(rope_ready, j)
                    pe.matmul(ps[:, ROPE_BANK, :], rot, qraw[:, j % 2].rearrange("p c t -> p (c t)"), start=True,
                              stop=True).then_inc(rope_full, 1)

                col_jobs("q.", "q0", (0, 1), u_s, lambda j: rotate(j - 1) if j else None)
                col_jobs("q.", "q1", (2, 3), u_s, lambda j: rotate(j - 1))
                col_jobs("k.", "k0", (0, 1), u_s, lambda j: rotate(j + 3))
                col_jobs("k.", "k1", (2, 3), u_s, lambda j: rotate(j + 3))
                row_jobs("v.", "v0", (0, 1), u_s, lambda: rotate(7))
                row_jobs("v.", "v1", (2, 3), u_s)
                settle()

                def scores(s):
                    hd, t = s // TT, s % TT
                    if s >= 2:
                        pe.wait_ge(exp_ready, 2 * (s - 1))
                    for c in range(2):
                        lo = 2 * HALF * c
                        last = pe.matmul(ps[:, score_banks(s) + c, 0:T], qT[lo:lo + 2 * HALF, hd, t * P:(t + 1) * P],
                                         kT[lo:lo + 2 * HALF, hd, :], start=True, stop=True)
                    last.then_inc(s_full, 1)

                def turn_mix(s):
                    pe.wait_ge(a_ready, s + 1)
                    if s >= 1:
                        pe.wait_ge(at_ready, s)
                    for k in range(2):
                        last = pe.transpose(ps[:, MIX_BANK, k * P:(k + 1) * P], amix[:, s % 2, k * P:(k + 1) * P], ident)
                    last.then_inc(at_full, 1)

                def values(s):
                    hd = s // TT
                    pe.wait_ge(at_ready, s + 1)
                    if s % 4 == 0 and s >= 4:
                        pe.wait_ge(o_ready, s // 4)
                    for k in range(2):
                        last = pe.matmul(ps[:, VALUE_BANK, (s % 4) * P:(s % 4 + 1) * P], aTs[:, s % 2, k * P:(k + 1) * P],
                                         v[:, k, hd * P:(hd + 1) * P], start=(k == 0), stop=(k == 1))
                    if s % 4 == 3:
                        last.then_inc(pv_full, 1)

                pe.wait_ge(rope_ready, 8)
                pe.wait_ge(v_ready, 4)
                scores(0)
                for s in range(ATTN_STEPS):
                    if s + 1 < ATTN_STEPS:
                        scores(s + 1)
                    job = f"gate.{s // 2}"
                    if s % 2 == 0:
                        gdst = begin(job)
                    columns(gdst[:, (s % 2) * T:(s % 2 + 1) * T], QUARTERS * SLABS.index("gc0") + s, u_s,
                            job if s % 2 else None)
                    if s == 1:
                        pe.wait_ge(conv_ready, 1)
                        dst = begin("mean")
                        for c in range(DC):
                            last = pe.matmul(dst[:, 0:T], mean_m, conv[:, c, :], start=(c == 0), stop=(c == DC - 1))
                        last.then_inc(full[bank("mean")], 1)
                    if s == 7:
                        pe.wait_ge(ln_sq, 1)
                        dst = begin("var")
                        for c in range(DC):
                            last = pe.matmul(dst[:, 0:T], mean_m, sq[:, c, :], start=(c == 0), stop=(c == DC - 1))
                        last.then_inc(full[bank("var")], 1)
                    if s >= 1:
                        values(s - 1)
                    turn_mix(s)
                values(ATTN_STEPS - 1)

                pe.wait_ge(mem_lo, 1)
                col_jobs("xk.", "xk0", (0, 1), mem_s)
                settle()
                pe.wait_ge(o_norm, 1)
                for j in range(4):
                    dst = begin(f"oT{j}")
                    for c in range(2):
                        for s in range(TT):
                            last = pe.transpose(dst[:, c * T + s * P:c * T + (s + 1) * P],
                                                o_all[:, (2 * j + c) * TT + s, :], ident)
                    last.then_inc(full[bank(f"oT{j}")], 1)
                col_jobs("xk.", "xk1", (2, 3), mem_s)
                pe.wait_ge(lo_ready, DC + 4)
                col_jobs("ao.", "ao0", (0, 1), o_s)
                col_jobs("ao.", "ao1", (2, 3), o_s)
                pe.wait_ge(conv_lo_ready, 1)
                col_jobs("co.", "co0", (0, 1), conv_s)
                col_jobs("co.", "co1", (2, 3), conv_s)
                row_jobs("xv.", "xv0", (0, 1), mem_s)
                settle()
                pe.wait_ge(merged_ready, 4)
                row_jobs("wo.", "wo0", (0, 1), m_s)
                row_jobs("wo.", "wo1", (2, 3), m_s)
                row_jobs("xv.", "xv1", (2, 3), mem_s)
                settle()
                turn_norm("nx", 1)

                def xscores(hd):
                    pe.wait_ge(xq_ready, hd + 1)
                    if hd == 0:
                        pe.wait_ge(xk_ready, 4)
                    if hd >= 2:
                        pe.wait_ge(xexp_ready, TT * (hd - 1))
                    for s in range(TT):
                        for c in range(2):
                            last = pe.matmul(ps[:, 4 + hd % 2, s * T:(s + 1) * T], xqT[:, 2 * hd + c, s * P:(s + 1) * P],
                                             xkT[:, 2 * hd + c, :], start=(c == 0), stop=(c == 1))
                    last.then_inc(xs_full, 1)

                def xturn(hd):
                    pe.wait_ge(xp_ready, TT * (hd + 1))
                    if hd >= 2:
                        pe.wait_ge(xt_ready, hd - 1)
                    for k in range(2):
                        for s in range(TT):
                            last = pe.transpose(ps[:, 6 + hd % 2, k * T + s * P:k * T + (s + 1) * P],
                                                E[:, hd % 2, s, k * P:(k + 1) * P], ident)
                    last.then_inc(xt_full, 1)

                def xvalues(hd):
                    pe.wait_ge(xt_ready, hd + 1)
                    if hd == 0:
                        pe.wait_ge(xv_ready, 4)
                    dst = begin(f"px{hd}")
                    for c in range(2):
                        for k in range(2):
                            last = pe.matmul(dst[:, c * T:(c + 1) * T], xv[:, k, (2 * hd + c) * P:(2 * hd + c + 1) * P],
                                             pT[:, hd % 2, k * T:(k + 1) * T], start=(k == 0), stop=(k == 1))
                    last.then_inc(full[bank(f"px{hd}")], 1)

                col_jobs("xq.", "xq0", (0, 1), x_s)

                def xq_job(j):
                    dst = begin(f"xq.{j}")
                    for c in range(2):
                        columns(dst[:, c * T:(c + 1) * T], QUARTERS * SLABS.index("xq0") + 2 * j + c, x_s,
                                f"xq.{j}" if c else None)

                xq_job(2)
                xscores(0)
                xq_job(3)
                settle()
                xscores(1)
                xturn(0)
                for hd in range(2, XHEADS + 2):
                    if hd < XHEADS:
                        xscores(hd)
                    if hd - 1 < XHEADS:
                        xturn(hd - 1)
                    xvalues(hd - 2)
                pe.wait_ge(xo_ready, 4)
                row_jobs("xo.", "xo0", (0, 1), xo_s)
                row_jobs("xo.", "xo1", (2, 3), xo_s)
                settle()
                pe.sem_inc(freed, RING)
                turn_norm("nf", 2)

                pe.wait_ge(n_turned, 2)
                pe.wait_ge(cur_ready, 2)
                dst = begin("router")
                for s in range(TT):
                    for k in range(DC):
                        last = pe.matmul(dst[:, s * NR:(s + 1) * NR], uT[:, k, s * P:(s + 1) * P], wr[:, k, :],
                                         start=(k == 0), stop=(k == DC - 1))
                last.then_inc(full[bank("router")], 1)
                pe.wait_ge(r_mask, 1)
                dst = ps[:, bank("rank"), :]
                pe.matmul(dst[:, 0:EXPERTS], tri, picked[:, 0, :], start=True, stop=True)
                pe.matmul(dst[:, EXPERTS:2 * EXPERTS], tri, picked[:, 1, :], start=True, stop=False)
                pe.matmul(dst[:, EXPERTS:2 * EXPERTS], mean_m, picked[:, 0, :], start=False, stop=True)
                pe.matmul(dst[:, 2 * EXPERTS:3 * EXPERTS], mean_m, picked[:, 0, :], start=True, stop=False)
                pe.matmul(dst[:, 2 * EXPERTS:3 * EXPERTS], mean_m, picked[:, 1, :], start=False,
                          stop=True).then_inc(full[bank("rank")], 1)

                pe.wait_ge(rank_ready, 1)
                passes = pe.value_load(npass_i[0:1, 0:1], min_val=1, max_val=MAX_PASSES)
                with pe.Fori(0, passes) as _p:
                    for s in range(TT):
                        for half in range(HALVES):
                            pe.matmul(ps[:, 4 + 2 * s + half, :], ident, h[:, s, half * SLAB:(half + 1) * SLAB],
                                      start=True, stop=True)
                    with pe.Fori(0, PAIRS) as _i:
                        n = pe.snap(u)
                        pe.wait_ge(sel_ready, n + 1)
                        for c in range(DC):
                            for s in range(TT):
                                last = pe.matmul(ps[:, 0, c * 2 * CAP:(c + 1) * 2 * CAP], uN[:, s, c * P:(c + 1) * P],
                                                 sel[:, s].rearrange("p e s -> p (e s)"), start=(s == 0), stop=(s == TT - 1))
                        last.then_inc(xg_done, 1)
                        pe.wait_ge(spread_ready, n * 2 + 2)
                        for s in range(TT):
                            last = pe.transpose(ps[:, 2, s * P:(s + 1) * P],
                                                spread[:, s].rearrange("p e w s -> p (e w s)"), ident)
                        last.then_inc(gt_done, 1)
                        pe.wait_ge(xe_ready, n + 1)
                        for j in range(4):
                            pe.wait_ge(landed[j], n * 16 + 16)
                        for k in range(DC):
                            for j in range(4):
                                e = j // 2
                                last = pe.matmul(ps[CAP * j:CAP * (j + 1), 1, :], xe[:, k, e * CAP:(e + 1) * CAP],
                                                 slot(j)[:, k, :], start=(k == 0), stop=(k == DC - 1),
                                                 skip_group_check=True)
                        last.then_inc(up_done, 1)
                        pe.wait_ge(up_done, n + 1)
                        pe.sem_inc(freed, 4)
                        pe.wait_ge(up_out, n + 1)
                        pe.wait_ge(scat_ready, n + 1)
                        for f in range(FC):
                            last = pe.transpose(ps[:, 2, f * P:(f + 1) * P], up_sb[:, f * P:(f + 1) * P], ident)
                        last.then_inc(upt_done, 1)
                        pe.wait_ge(upt_ready, n + 1)
                        for j in range(4, RING):
                            pe.wait_ge(landed[j], n * 16 + 16)
                        for f in range(FC):
                            for j in range(4):
                                e, half = j // 2, j % 2
                                w = ring[:, 4 + e, :].rearrange("p (c n) -> p c n", c=FC)
                                last = pe.matmul(ps[CAP * j:CAP * (j + 1), 3, :], up_t[:, f, e, :],
                                                 w[:, f, half * SLAB:(half + 1) * SLAB], start=(f == 0),
                                                 stop=(f == FC - 1), skip_group_check=True)
                        last.then_inc(y_done, 1)
                        pe.wait_ge(y_done, n + 1)
                        pe.sem_inc(freed, 2)
                        pe.wait_ge(y_out, n + 1)
                        for s in range(TT):
                            for half in range(HALVES):
                                last = pe.matmul(ps[:, 4 + 2 * s + half, :], scat[:, half, s * P:(s + 1) * P], y_sb,
                                                 start=False, stop=True, skip_group_check=True)
                        last.then_inc(added, 1)
                        pe.reg_add(u, u, 1)
                    k = pe.snap(q)
                    pe.wait_ge(h_back, k * 2 + 2)
                    pe.reg_add(q, q, 1)
                pe.drain().then_inc(layer_end, 1)
                pe.wait_ge(layer_go, L + 1)


_INS = ["x", "mem", "positions", "norm_mix_g", "w_in", "conv_dw", "conv_db", "conv_ln_g", "conv_ln_b", "w_conv_out",
        "lam_q1", "lam_k1", "lam_q2", "lam_k2", "subln_g", "w_attn_out", "w_out", "norm_mem_g", "norm_x_g", "w_xq",
        "w_xkv", "w_xo", "norm_ffn_g", "w_group", "b_group", "w_router", "b_router", "w1", "w3", "w2", "final_norm_g"]


def kernel(**inputs):
    import concourse.bacc as _bacc
    from concourse.bass_utils import run_bass_kernel_spmd as _run

    nc = _bacc.Bacc("TRN2", target_bir_lowering=False, num_devices=1)
    arrays, args = {}, []
    for name in ["consts"] + _INS:
        a = constants() if name == "consts" else np.ascontiguousarray(inputs[name])
        arrays[f"in_{name}_dram"] = a
        args.append(nc.dram_tensor(f"in_{name}_dram", a.shape, mybir.dt.from_np(a.dtype), kind="ExternalInput").ap())
    o = nc.dram_tensor("out_0_dram", (1, T, D), F32, kind="ExternalOutput").ap()
    encoder(nc, *args, o)
    r = _run(nc, [arrays], core_ids=[0])
    return r.results[0]["out_0_dram"]
```

```python
import math
from contextlib import ExitStack

import numpy as np

import concourse.bass as bass
from concourse import mybir

P = 128
F32 = mybir.dt.float32
F32R = mybir.dt.float32r
I32 = mybir.dt.int32
ALU = mybir.AluOpType
ACT = mybir.ActivationFunctionType
AX = mybir.AxisListType

LAYERS = 2
T = 256
TT = T // P
D = 1024
DC = D // P
KERN = 31
PAD = KERN // 2
HEADS = 8
HALF = 32
XHEADS = 4
GROUPS = 4
PER_GROUP = 8
EXPERTS = GROUPS * PER_GROUP
FF = D // 2
FC = FF // P
SLAB = 512
RING = 6
PAIRS = EXPERTS // 2
CAP = 32
MAX_PASSES = T // CAP
HALVES = D // SLAB

R_DB, R_LNG, R_LNB, R_MIX, R_MEM, R_X, R_FFN = range(KERN, KERN + 7)
ROWS = KERN + 7
NR = GROUPS + EXPERTS
K_WR = DC * ROWS
K_RB = K_WR + DC * NR
K_SUB = K_RB + NR
K_LAM = K_SUB + 1
NPK = K_LAM + 1

C_ID = 0
C_ROT = C_ID + P
C_TRI = C_ROT + P
C_MEAN = C_TRI + P
C_IOTA = C_MEAN + P
C_THR = C_IOTA + CAP
C_DESC = C_THR + MAX_PASSES - 1
C_INVF = C_DESC + EXPERTS
C_MLO = C_INVF + 1
C_MHI = C_MLO + 1
C_LAM = C_MHI + 1
C_OML = C_LAM + LAYERS
NCON = C_OML + LAYERS

RMS_EPS = 1e-6
LN_EPS = 1e-5
TWO_PI = (6.28125, 0.0019350051879882812, 3.019916e-07)
MAGIC = 12582912.0
SIN_MAX = 3.1415925

SLABS = ["xk0", "a0", "g0", "a1", "g1", "q0", "q1", "k0", "k1", "v0", "v1", "gc0", "gc1", "ga0", "ga1",
         "xk1", "ao0", "ao1", "co0", "co1", "wo0", "wo1", "xv0", "xv1", "xq0", "xq1", "xo0", "xo1"]

TAPS = ((7, 22, 5, 2), (3, 2, 14), 2)

PAIR_SLOTS = [4, 0, 1, 2, 3, 5]
EARLY = 3
EARLY_STEPS = 2 * EARLY
LATE_STEPS = 2 * (4 - EARLY) + 2

LAND = 2
QUARTERS = 4
SPLITS = 4
NQ = QUARTERS * len(SLABS)

TURN = 4


def pairs(name):
    return [f"{name}{j}" for j in range(4)]


ATTN_STEPS = HEADS * TT
JOBS = (["xk.0", "xk.1"] + pairs("nm") + ["a.0", "a.1", "g.0", "g.1", "a.2", "a.3", "g.2", "g.3"] + pairs("q.") + pairs("k.")
        + pairs("v."))
for _j in range(ATTN_STEPS // 2):
    JOBS += [f"gate.{_j}"]
JOBS += ["xk.2", "mean"] + pairs("oT") + ["xk.3", "var"] + pairs("ao.") + pairs("co.") + pairs("wo.")
JOBS += ["xv.0", "xv.1"] + pairs("nx") + ["xv.2", "xv.3"] + pairs("xq.") + pairs("px") + pairs("xo.") + pairs("nf")
JOBS += ["router", "rank"]


def banks_of_jobs():
    where, used, last = {}, [0] * TURN, -1
    for job in JOBS:
        n = TURN // 2 if job.startswith("gate") else TURN
        last = (last + 1) % n
        used[last] += 1
        where[job] = (last, used[last])
    return where


WHERE = banks_of_jobs()


def last_quarters():
    at = {}
    for kind in ("a", "g", "q", "k", "xk", "ao", "co", "xq"):
        for j in range(4):
            at[f"{kind}.{j}"] = QUARTERS * SLABS.index(f"{kind}{j // 2}") + (1, 3)[j % 2]
    for kind in ("v", "xv", "wo", "xo"):
        for j in range(4):
            at[f"{kind}.{j}"] = QUARTERS * SLABS.index(f"{kind}{j // 2}") + 3
    return at


LAST_QUARTER = last_quarters()


def bank(job):
    return WHERE[job][0]


def turn(job):
    return WHERE[job][1]


def score_banks(s):
    return 2 + 2 * (s % 2)


ROPE_BANK = 5
VALUE_BANK = 6
MIX_BANK = 7


class Chain:

    def __init__(self, eng, sem):
        self.eng, self.sem, self.n = eng, sem, 0

    def note(self, ins):
        ins.then_inc(self.sem, 1)
        self.n += 1
        return self.n

    def after(self, n):
        self.eng.wait_ge(self.sem, n)

    def link(self, ins):
        self.after(self.note(ins))


def constants():
    c = np.zeros((P, NCON), np.float32)
    p = np.arange(P)
    c[:, C_ID:C_ID + P] = np.eye(P)
    for b in range(0, P, 2 * HALF):
        for d in range(HALF):
            c[b + HALF + d, C_ROT + b + d] = -1.0
            c[b + d, C_ROT + b + HALF + d] = 1.0
    c[:, C_TRI:C_TRI + P] = (p[:, None] < p[None, :]) / D
    c[:, C_MEAN:C_MEAN + P] = 1.0 / D
    c[:, C_IOTA:C_IOTA + CAP] = np.arange(CAP)
    c[:, C_THR:C_THR + MAX_PASSES - 1] = CAP * np.arange(1, MAX_PASSES)
    c[:, C_DESC:C_DESC + EXPERTS] = EXPERTS - np.arange(EXPERTS)
    step = np.float32(-math.log(10000.0))
    c[:, C_INVF] = np.exp(step * (p % HALF).astype(np.float32) / np.float32(HALF))
    c[:, C_MLO] = (p // CAP) % 2 == 0
    c[:, C_MHI] = (p // CAP) % 2 == 1
    for i in range(LAYERS):
        c[:, C_LAM + i] = 0.8 - 0.6 * math.exp(-0.3 * i)
        c[:, C_OML + i] = 1.0 - (0.8 - 0.6 * math.exp(-0.3 * i))
    return c


def encoder(nc, consts, x, mem, positions, norm_mix_g, w_in, conv_dw, conv_db, conv_ln_g, conv_ln_b, w_conv_out,
            lam_q1, lam_k1, lam_q2, lam_k2, subln_g, w_attn_out, w_out, norm_mem_g, norm_x_g, w_xq, w_xkv, w_xo,
            norm_ffn_g, w_group, b_group, w_router, b_router, w1, w3, w2, final_norm_g, out):
    mem_t_dram = nc.dram_tensor("mem_t_scratch", (LAYERS, P, DC * T), F32, kind="Internal").ap()

    with ExitStack() as ctx:
        def sb(name, shape, dt=F32):
            return ctx.enter_context(nc.sbuf_tensor(name, shape, dt))

        def sem(name):
            return ctx.enter_context(nc.semaphore(name))

        ring = sb("ring", [P, RING, DC * SLAB])
        ring_at = nc.sbuf_base - RING * DC * SLAB * 4
        h = sb("h", [P, TT, D])
        uT = sb("uT", [P, DC, T])
        glu_pad = sb("glu_pad", [P, DC, T + 2 * PAD + 2])
        big = sb("big", [P, 7, DC * T])
        big_at = nc.sbuf_base - 7 * DC * T * 4
        memT = sb("memT", [P, DC, T])
        cst = sb("cst", [P, NCON])
        pk = sb("pk", [P, LAYERS, NPK])
        cur = sb("cur", [P, NPK])
        rope_cs = sb("rope_cs", [P, 2, T])
        work = sb("work", [P, 2304])
        small = sb("small", [P, 224])
        rs_ln = sb("rs_ln", [P, T])
        npass_i = sb("npass_i", [P, 1], I32)
        ps = ctx.enter_context(nc.psum_tensor("ps", [P, 8, SLAB], F32))

        quarter_bytes = 2 * DC * P * 4
        operand_bytes = DC * T * 4
        wsplit = nc.alloc_sbuf_tensor_at("weight_split", [P, SPLITS, 2, DC * P], F32R,
                                         offset=ring_at + LAND * DC * SLAB * 4).ap()
        xsplit = nc.alloc_sbuf_tensor_at("operand_split", [P, 4, DC, T], F32R,
                                         offset=ring_at + LAND * DC * SLAB * 4 + SPLITS * quarter_bytes).ap()
        conv_hi = nc.alloc_sbuf_tensor_at("conv_high", [P, DC, T], F32R, offset=big_at + operand_bytes).ap()
        conv_lo = nc.alloc_sbuf_tensor_at("conv_low", [P, DC, T], F32R, offset=big_at + 3 * operand_bytes).ap()
        assert LAND * DC * SLAB * 4 + SPLITS * quarter_bytes + 4 * operand_bytes <= RING * DC * SLAB * 4

        u_s = o_s = m_s = x_s = (xsplit[:, 0], xsplit[:, 1])
        mem_s = xo_s = (xsplit[:, 2], xsplit[:, 3])
        conv_s = (conv_hi, conv_lo)

        def chunks(i):
            return big[:, i, :].rearrange("p (c t) -> p c t", c=DC)

        def rows(i):
            return big[:, i, :].rearrange("p (s d) -> p s d", s=TT)

        glu = glu_pad[:, :, PAD:PAD + T]
        sq = chunks(1)
        xkT = uT
        conv = chunks(0)
        qT = chunks(1)
        kT = chunks(2)
        merged = chunks(2)
        v = rows(3)
        xv = rows(3)
        gate_c = chunks(4)
        xqT = chunks(4)
        gate_a = chunks(5)
        o_all = big[:, 6, :].rearrange("p (s e) -> p s e", s=ATTN_STEPS)
        uN = rows(6)
        memN = rows(3)

        ident = cst[:, C_ID:C_ID + P]
        rot = cst[:, C_ROT:C_ROT + P]
        tri = cst[:, C_TRI:C_TRI + P]
        mean_m = cst[:, C_MEAN:C_MEAN + P]
        iota = cst[:, C_IOTA:C_IOTA + CAP]
        par = cur[:, 0:K_WR].rearrange("p (c r) -> p c r", c=DC)
        wr = cur[:, K_WR:K_RB].rearrange("p (c n) -> p c n", c=DC)
        rb = cur[:, K_RB:K_SUB]
        sub_col = cur[:, K_SUB:K_SUB + 1]
        neglam = cur[:, K_LAM:K_LAM + 1]

        def wk(at, *shape):
            n = int(np.prod(shape))
            a = work[:, at:at + n]
            if len(shape) == 1:
                return a
            names = "abcd"[:len(shape)]
            return a.rearrange(f"p ({' '.join(names)}) -> p {' '.join(names)}",
                               **{k: s for k, s in zip(names[:-1], shape[:-1])})

        sg = wk(0, 2, 2, T)
        qraw = wk(0, 2, 2, T)
        rt1 = wk(1024, 2, T)
        rt2 = wk(1536, 2, T)
        E = wk(0, 2, 2, T)
        amix = wk(1024, 2, T)
        aTs = wk(1536, 2, T)
        etmp = wk(2048, T)
        pT = wk(1024, 2, 2 * T)
        nmx = small[:, 0:32].rearrange("p (s c) -> p s c", s=ATTN_STEPS)
        sm = small[:, 32:64].rearrange("p (s c) -> p s c", s=ATTN_STEPS)
        ssq = small[:, 66:82]
        ss = small[:, 82:84]
        xnm = small[:, 84:92].rearrange("p (s c) -> p s c", s=XHEADS)
        xsm = small[:, 92:100].rearrange("p (s c) -> p s c", s=XHEADS)
        cnt1 = small[:, 100:101]
        thr7 = small[:, 101:108]
        mss = small[:, 112:114]

        ahead_buf = [[big[:, b, :].rearrange("p (c n) -> p c n", c=DC // 2) for b in half] for half in ((0, 5), (1, 2))]

        rbuf = work
        roff = [0]

        def rt(*shape):
            n = int(np.prod(shape))
            a = rbuf[:, roff[0]:roff[0] + n]
            roff[0] += n
            if len(shape) == 1:
                return a
            names = "abcd"[:len(shape)]
            return a.rearrange(f"p ({' '.join(names)}) -> p {' '.join(names)}",
                               **{k: s for k, s in zip(names[:-1], shape[:-1])})

        logit = rt(TT, NR)
        m_g = rt(TT)
        d_g = rt(TT, GROUPS)
        e_g = rt(TT, GROUPS)
        g_w = rt(TT)
        eq_g = rt(TT, GROUPS)
        oh_g = rt(TT, GROUPS)
        mx_g = rt(TT)
        masked = rt(TT, EXPERTS)
        top1 = rt(TT)
        top2 = rt(TT)
        first = rt(TT, EXPERTS)
        mx_e = rt(TT)
        oh1 = rt(TT, EXPERTS)
        oh2 = rt(TT, EXPERTS)
        gap = rt(TT)
        e_gap = rt(TT)
        w_1 = rt(TT)
        w_2 = rt(TT)
        tok_w = rt(TT, EXPERTS)
        tok_w2 = rt(TT, EXPERTS)
        picked = rt(TT, EXPERTS)
        rank = rt(TT, EXPERTS)
        roff[0] = 0
        rbuf = big[:, 3, :]
        sel = rt(TT, 2, CAP)
        spread = rt(TT, 2, 2, CAP)
        xe = rt(DC, 2 * CAP)
        up_t = rt(FC, 2, CAP)
        rbuf = big[:, 4, :]
        roff[0] = 0
        y_sb = rt(SLAB)
        scat = rt(2, T)
        up_sb = rt(SLAB)
        silu_t = rt(FC, 2, CAP)

        up_in = [[sem(f"up_slab_{j}_half_{k}_landed") for j in range(4)] for k in range(2)]
        ahead_free = sem("ahead_buffers_free")
        ahead_in = [[sem(f"ahead_slab_{j}_half_{k}_landed") for j in range(2)] for k in range(2)]
        down_in = [sem(f"down_slab_{e}_landed") for e in range(2)]
        slab_in = [sem(f"dense_slab_landed_{i}") for i in range(LAND)]
        split_out = sem("dense_slab_split")
        freed = [sem("early_slot_freed"), sem("late_slot_freed")]
        cst_in, x_in, par_in, pos_in, mem_in, lam_in, sub_in, router_in = (sem(n) for n in (
            "consts_in", "x_in", "params_in", "pos_in", "mem_in", "lambdas_in", "subln_in", "router_params_in"))
        st_rows, st_mss, st_mvar, st_msq, st_mn, st_mt, st_mg, st_msto = (sem("setup_" + n) for n in (
            "rows_turned", "mem_squares", "mem_variance", "mem_root", "mem_normed", "mem_turned",
            "mem_scaled", "mem_stored"))
        st_ang, st_cs, st_dot, st_exp, st_ch = (sem("setup_" + n) for n in (
            "angles", "sincos", "lambda_dots", "lambda_exps", "vector_chain"))
        mt_in, mem_ready = sem("mem_t_in"), sem("layer_mem_ready")
        layer_end, layer_go = sem("layer_end"), sem("layer_go")
        first_slot_seen = sem("first_slot_seen")
        np_ready, np_seen = sem("passes_ready"), sem("passes_seen")
        layer_clear = sem("layer_clear")
        sel_ready, spread_ready, xg_done, gt_done, xe_ready, scat_ready, up_half, up_done, up_out, upt_done, silu_ready, \
            upt_ready, y_done, y_out, added = (sem("moe_" + n) for n in (
                "select_ready", "spread_ready", "gathered", "spread_turned", "tokens_ready", "scatter_ready",
                "up_first_half", "up_done", "up_out", "up_turned", "silu_ready", "hidden_ready", "down_done", "down_out", "added"))
        fin_g, fin_ss, fin_var, fin_sq, fin_ch, fin_out, out_done = (sem("final_" + n) for n in (
            "gain_in", "squares", "variance", "root", "chain", "rows_ready", "stored"))

        first_sem = sem("bank_full_0")
        full = [first_sem] + [sem(f"bank_full_{b}") for b in range(1, TURN)]
        free = [sem(f"bank_free_{b}") for b in range(TURN)]
        dch, ach = sem("vector_chain"), sem("scalar_chain")
        cur_ready = sem("layer_params_ready")
        ups_used = sem("layer_up_halves_used")
        w_hi, w_lo, w_used = sem("weights_high"), sem("weights_low"), sem("weights_used")
        hi_ready, lo_ready, mem_hi, mem_lo, conv_hi_ready, conv_lo_ready, m_hi, xo_hi = (sem(n) for n in (
            "operand_high_ready", "operand_low_ready", "memory_high", "memory_low", "conv_high_ready",
            "conv_low_ready", "merged_high", "cross_high"))
        n_ss, n_var, n_root, n_inv, n_ready, n_turned = (sem("norm_" + n) for n in (
            "squares", "variance", "root", "root_inverse", "first_rows_ready", "columns_ready"))
        n_ready_act = sem("norm_other_rows_ready")
        sig_ready, glu_ready = sem("glu_sigmoid_ready"), sem("glu_ready")
        conv_ready, ln_xc, ln_sq, ln_var, ln_root, ln_y, ln_out = (sem(n) for n in (
            "conv_ready", "ln_centred", "ln_squared", "ln_variance", "ln_root", "ln_scaled", "ln_silu_ready"))
        qraw_ready, rope_full, rope_ready = sem("rope_raw_ready"), sem("rope_turned"), sem("rope_ready")
        v_ready = sem("v_ready")
        s_full, nm_ready, exp_ready, a_ready, at_full, at_ready, pv_full, o_ready = (sem("attn_" + n) for n in (
            "scores", "max_ready", "exp_ready", "mix_ready", "mix_turned", "mix_columns", "values", "rows_out"))
        gate_raw, gate_ready, o_var, o_root, o_norm = (sem(n) for n in (
            "gates_raw", "gates_ready", "subln_variance", "subln_root", "subln_ready"))
        xk_ready, xv_ready, merged_ready, h_ready, xq_ready = (sem(n) for n in (
            "xk_ready", "xv_ready", "merged_ready", "h_ready", "xq_ready"))
        xs_full, xnm_ready, xexp_ready, xp_ready, xt_full, xt_ready, xo_ready = (sem("cross_" + n) for n in (
            "scores", "max_ready", "exp_ready", "probs_ready", "probs_turned", "probs_columns", "columns_ready"))
        r_diff, r_exp, r_gap, r_gexp, r_mask, rank_ready = (sem("router_" + n) for n in (
            "group_diff", "group_exp", "gap", "gap_exp", "picked", "rank_ready"))
        last_sem = rank_ready
        cleared = range(first_sem.num, last_sem.num + 1)

        block = ctx.enter_context(nc.Block())

        def slab_source(name, L):
            kind, half = name[:-1], int(name[-1])
            c = {"a": 0, "g": D, "q": 2 * D, "k": 3 * D, "v": 4 * D, "gc": 5 * D, "ga": 6 * D}
            if kind in c:
                w, c0 = w_in, c[kind]
            elif kind in ("xk", "xv"):
                w, c0 = w_xkv, D * (kind == "xv")
            else:
                w, c0 = {"co": w_conv_out, "ao": w_attn_out, "wo": w_out, "xq": w_xq, "xo": w_xo}[kind], 0
            c0 += half * SLAB
            return w[L, :, c0:c0 + SLAB].rearrange("(c p) n -> p c n", p=P)

        def slot(j):
            return ring[:, j, :].rearrange("p (c n) -> p c n", c=DC)

        def pair_slot(j):
            return slot(PAIR_SLOTS[j])

        def down_slot(j):
            return ring[:, PAIR_SLOTS[j], :].rearrange("p (c n) -> p c n", c=FC)

        def by_rows(name):
            return name[:-1] in ("v", "xv", "wo", "xo")

        def landed_quarter(q):
            n, c = q // QUARTERS, q % QUARTERS
            w = slot(n % LAND)
            return w[:, 2 * c:2 * c + 2, :] if by_rows(SLABS[n]) else w[:, :, c * P:(c + 1) * P]

        def split_quarter(q, part):
            c = 2 if by_rows(SLABS[q // QUARTERS]) else DC
            return wsplit[:, q % SPLITS, part, :].rearrange("p (c n) -> p c n", c=c)

        @block.sync
        def _(sp):
            sp.dma_start(memN, mem[0].rearrange("(s p) d -> p s d", p=P)).then_inc(mem_in, 16)
            sp.dma_start(h[:], x[0].rearrange("(s p) d -> p s d", p=P)).then_inc(x_in, 16)
            sp.wait_ge(cst_in, 16)
            sp.wait_ge(par_in, 16 * 8)
            m = sp.alloc_register("sp_unit")
            sp.reg_mov(m, 0)

            def up_half_source(w, L, e, k):
                return w[L, e, k * D // 2:(k + 1) * D // 2, :].rearrange("(c p) n -> p c n", p=P)

            def experts(L, i, skip=0, waited=False):
                n = sp.snap(m)
                ups = [(w1, 2 * i), (w3, 2 * i), (w1, 2 * i + 1), (w3, 2 * i + 1)]

                def left(early, step):
                    steps = EARLY_STEPS if early else LATE_STEPS
                    sp.wait_ge(freed[0 if early else 1], (n + L) * steps + (steps + step + 1))

                for k in range(2):
                    for j, (w, e) in enumerate(ups):
                        if j < skip:
                            continue
                        if not waited or k or j:
                            left(j < EARLY, k * EARLY + j if j < EARLY else k)
                        sp.dma_start(pair_slot(j)[:, k * DC // 2:(k + 1) * DC // 2, :],
                                     up_half_source(w, L, e, k)).then_inc(up_in[k][j], 16)
                for e in range(2):
                    left(False, 2 + e)
                    sp.dma_start(down_slot(4 + e),
                                 w2[L, 2 * i + e].rearrange("(c p) n -> p c n", p=P)).then_inc(down_in[e], 16)
                sp.reg_add(m, m, 1)

            with sp.Fori(0, LAYERS) as L:
                n_pair = sp.snap(m)
                for n, name in enumerate(SLABS):
                    if n < LAND:
                        sp.wait_ge(freed[0], (n_pair + L) * EARLY_STEPS + (EARLY + PAIR_SLOTS.index(n) + 1))
                    else:
                        sp.wait_ge(split_out, L * len(SLABS) + (n - 1))
                    sp.dma_start(slot(n % LAND), slab_source(name, L)).then_inc(slab_in[n % LAND], 16)
                    if name == "xv1":
                        sp.wait_ge(ahead_free, L + 1)
                        for k in range(2):
                            for j, w in enumerate((w1, w3)):
                                sp.dma_start(ahead_buf[k][j], up_half_source(w, L, 2, k)).then_inc(ahead_in[k][j], 16)
                sp.wait_ge(freed[0], (sp.snap(m) + L) * EARLY_STEPS + (EARLY_STEPS + 1))
                sp.sem_inc(first_slot_seen, 1)
                experts(L, 0, waited=True)
                experts(L, 1, skip=2)
                with sp.Fori(2, PAIRS) as i:
                    experts(L, i)
                sp.wait_ge(np_ready, L + 1)
                sp.sem_inc(np_seen, 1)
                passes = sp.value_load(npass_i[0:1, 0:1], min_val=1, max_val=MAX_PASSES)
                with sp.If(passes > 1):
                    with sp.Fori(1, passes) as _p:
                        with sp.Fori(0, PAIRS) as i:
                            experts(L, i)
                    sp.nop()
                sp.nop()
            for s in range(TT):
                sp.wait_ge(fin_out, s + 1)
                sp.dma_start(out[0, s * P:(s + 1) * P, :], uN[:, s, :]).then_inc(out_done, 16)
            sp.wait_ge(out_done, 16 * TT)

        @block.gpsimd
        def _(pool):
            for i in range(LAYERS):
                wrl = pk[:, i, K_WR:K_RB].rearrange("p (c n) -> p c n", c=DC)
                pool.dma_start(wrl[:, :, 0:GROUPS], w_group[i].rearrange("(c p) n -> p c n", p=P)).then_inc(router_in, 16)
                pool.dma_start(wrl[:, :, GROUPS:NR],
                               w_router[i].rearrange("(c p) n -> p c n", p=P)).then_inc(router_in, 16)
                pool.dma_start(pk[:, i, K_RB:K_RB + GROUPS], b_group[i].partition_broadcast(P)).then_inc(router_in, 16)
                pool.dma_start(pk[:, i, K_RB + GROUPS:K_SUB], b_router[i].partition_broadcast(P)).then_inc(router_in, 16)
            pool.wait_ge(st_mg, 4)
            for i in range(LAYERS):
                src = memT[:].rearrange("p c t -> p (c t)") if i == 0 else big[:, 1 + i, :]
                pool.dma_start(mem_t_dram[(i - 1) % LAYERS], src).then_inc(st_msto, 16)
            pool.sem_inc(mem_ready, 1)
            with pool.Fori(0, LAYERS) as L:
                for k in range(NQ):
                    pool.wait_ge(w_hi, k + 1)
                    pool.tensor_tensor(split_quarter(k, 1), landed_quarter(k), split_quarter(k, 0).bitcast(F32),
                                       ALU.subtract).then_inc(w_lo, 1)
                    if k == SPLITS - 1:
                        pool.wait_ge(mem_lo, 4)
                        pool.wait_ge(st_msto, 16 * LAYERS)
                        pool.dma_start(memT[:], mem_t_dram[L].rearrange("p (c t) -> p c t", c=DC)).then_inc(mt_in, 16)
                    if k % QUARTERS == QUARTERS - 1:
                        pool.wait_ge(w_lo, k + 1)
                        pool.sem_inc(split_out, 1)
                    if k == QUARTERS * (len(SLABS) - 1) - 1:
                        pool.sem_inc(freed[0], 2)
                    if k == NQ - 1:
                        pool.sem_inc(freed[0], EARLY_STEPS - 2)
                pool.wait_ge(ups_used, 1)
                for j in range(2):
                    pool.wait_ge(ahead_in[0][j], L * 16 + 16)
                    pool.tensor_copy(pair_slot(j)[:, 0:DC // 2, :], ahead_buf[0][j]).then_inc(up_in[0][j], 16)
                pool.wait_ge(mt_in, L * 16 + 16)
                pool.sem_inc(mem_ready, 1)
                pool.sem_inc(layer_end, 1)
                pool.wait_ge(layer_go, L + 1)
            pool.dma_start(memT[:, 0:FC, :].rearrange("p c t -> p (c t)"),
                           final_norm_g.partition_broadcast(P)).then_inc(fin_g, 16)
            pool.wait_ge(fin_g, 16)

        @block.scalar
        def _(act):
            act.dma_start(work[:, 0:T].bitcast(I32), positions[0].partition_broadcast(P)).then_inc(pos_in, 16)
            act.dma_start(cst[:], consts).then_inc(cst_in, 16)
            prow = big[:, 0, :].rearrange("p (l d) -> p l d", l=LAYERS)
            for s, r0, r1 in ((conv_dw.rearrange("l k d -> k l d"), 0, KERN), (conv_db, R_DB, R_DB + 1),
                              (conv_ln_g, R_LNG, R_LNG + 1), (conv_ln_b, R_LNB, R_LNB + 1),
                              (norm_mix_g, R_MIX, R_MIX + 1), (norm_mem_g, R_MEM, R_MEM + 1),
                              (norm_x_g, R_X, R_X + 1), (norm_ffn_g, R_FFN, R_FFN + 1)):
                s = s if r1 - r0 > 1 else s.rearrange("(o l) d -> o l d", o=1)
                act.dma_start(prow[r0:r1], s).then_inc(par_in, 16)
            for j, lv in enumerate((lam_q1, lam_k1, lam_q2, lam_k2)):
                for i in range(LAYERS):
                    act.dma_start(work[:, 1024 + (i * 4 + j) * 64:1024 + (i * 4 + j + 1) * 64],
                                  lv[i].partition_broadcast(P)).then_inc(lam_in, 16)
            for i in range(LAYERS):
                act.dma_start(pk[:, i, K_SUB:K_SUB + 1], subln_g[i].rearrange("(p o) -> p o", o=1)).then_inc(sub_in, 16)
            act.wait_ge(mem_in, 16)
            for s in range(TT):
                act.activation(uT[:, s * FC:(s + 1) * FC, :].rearrange("p c t -> p (c t)"), memN[:, s, :], ACT.Square,
                               accum_out=mss[:, s:s + 1]).then_inc(st_mss, 1)
            act.wait_ge(st_mvar, 1)
            act.activation(mss, mss, ACT.Sqrt).then_inc(st_msq, 1)
            act.wait_ge(st_ang, 1)
            act.activation(rope_cs[:], wk(512, 2, T), ACT.Sin).then_inc(st_cs, 1)
            act.wait_ge(st_dot, 1)
            act.activation(small[:, 108:112], small[:, 104:108], ACT.Exp).then_inc(st_exp, 1)

            u = act.alloc_register("act_unit")
            act.reg_mov(u, 0)

            def evac(job, dst, func=ACT.Copy, scale=1.0):
                b = bank(job)
                act.wait_ge(full[b], turn(job))
                src = ps[:, b, :]
                if len(dst.shape) == 3:
                    src = src.rearrange("p (c t) -> p c t", c=2)
                return act.activation(dst, src, func, scale=scale)

            act.wait_ge(x_in, 16)
            with act.Fori(0, LAYERS) as L:
                ch = Chain(act, ach)
                split = [0]

                def split_to(q):
                    for k in range(split[0], min(q, NQ)):
                        n = k // QUARTERS
                        if k % QUARTERS == 0:
                            act.wait_ge(slab_in[n % LAND], L * (16 * len(SLABS) // LAND) + 16 * (n // LAND + 1))
                        if k >= SPLITS:
                            act.wait_ge(w_used, k - SPLITS + 1)
                        act.activation(split_quarter(k, 0), landed_quarter(k), ACT.Copy).then_inc(w_hi, 1)
                    split[0] = max(split[0], q)

                def ahead(job):
                    split_to(LAST_QUARTER[job] + SPLITS)

                def squares(n):
                    for s in range(TT):
                        if n > 0:
                            act.wait_ge(h_ready, 4 * (n - 1) + 3 + s)
                        act.activation(uN[:, s, :], h[:, s, :], ACT.Square,
                                       accum_out=ss[:, s:s + 1]).then_inc(n_ss, 1)
                    act.wait_ge(n_var, n + 1)
                    act.activation(ss, ss, ACT.Sqrt).then_inc(n_root, 1)

                def scale_rows(n, tiles):
                    act.wait_ge(n_inv, n + 1)
                    for s in tiles:
                        act.activation(uN[:, s, :], h[:, s, :], ACT.Copy,
                                       scale=ss[:, s:s + 1]).then_inc(n_ready_act, 1)

                def turned(kind, dst, row):
                    for j in (1, 3):
                        b = bank(f"{kind}{j}")
                        act.wait_ge(full[b], turn(f"{kind}{j}"))
                        for c in range(2):
                            ins = act.activation(dst[:, 2 * j + c, :], ps[:, b, c * T:(c + 1) * T], ACT.Copy,
                                                 scale=par[:, 2 * j + c, row:row + 1])
                            if c == 0:
                                ins.then_inc(n_turned, 1)
                            else:
                                ins.then_inc(free[b], 1)

                def turned_high(kind, dst, row):
                    for j in range(4):
                        b = bank(f"{kind}{j}")
                        act.wait_ge(full[b], turn(f"{kind}{j}"))
                        for c in range(2):
                            act.activation(dst[0][:, 2 * j + c, :], ps[:, b, c * T:(c + 1) * T], ACT.Copy,
                                           scale=par[:, 2 * j + c, row:row + 1]).then_inc(hi_ready, 1)

                def out(job, dst, ready, n, func=ACT.Copy, scale=1.0):
                    if job in LAST_QUARTER:
                        ahead(job)
                    evac(job, dst, func, scale).then_inc(ready, 1)
                    act.wait_ge(ready, n)
                    act.sem_inc(free[bank(job)], 1)

                split_to(1)
                act.wait_ge(mem_ready, L + 1)
                for j in range(4):
                    act.activation(mem_s[0][:, 2 * j:2 * j + 2, :], memT[:, 2 * j:2 * j + 2, :],
                                   ACT.Copy).then_inc(mem_hi, 1)
                split_to(2)
                squares(0)
                split_to(SPLITS)
                scale_rows(0, [1])
                for j in range(2):
                    out(f"xk.{j}", xkT[:, 2 * j:2 * j + 2, :], xk_ready, j + 1)
                act.wait_ge(cur_ready, 1)
                turned_high("nm", u_s, R_MIX)
                for j in range(4):
                    if j >= 2:
                        act.wait_ge(glu_ready, j - 1)
                    out(f"g.{j}", sg[:, j % 2].rearrange("p c t -> p (c t)"), sig_ready, j + 1, ACT.Sigmoid)
                for j in range(8):
                    if j >= 2:
                        act.wait_ge(rope_ready, j - 1)
                    else:
                        act.wait_ge(glu_ready, 4)
                    job = f"q.{j}" if j < 4 else f"k.{j - 4}"
                    out(job, qraw[:, j % 2].rearrange("p c t -> p (c t)"), qraw_ready, j + 1,
                        scale=0.125 if j < 4 else 1.0)
                for j in range(4):
                    out(f"v.{j}", v[:, j % 2, (j // 2) * SLAB:(j // 2 + 1) * SLAB], v_ready, j + 1)
                act.wait_ge(rope_ready, 8)
                for s in range(ATTN_STEPS + 1):
                    if s < ATTN_STEPS:
                        split_to(QUARTERS * SLABS.index("gc0") + s + 3)
                        act.wait_ge(nm_ready, s + 1)
                        if s >= 2:
                            act.wait_ge(a_ready, s - 1)
                        for c in range(2):
                            ins = act.activation(E[:, s % 2, c, :], ps[:, score_banks(s) + c, 0:T], ACT.Exp,
                                                 bias=nmx[:, s, c:c + 1], accum_out=sm[:, s, c:c + 1])
                            ins.then_inc(exp_ready, 1)
                    if s >= 1:
                        act.wait_ge(at_full, s)
                        act.activation(aTs[:, (s - 1) % 2, :], ps[:, MIX_BANK, 0:T], ACT.Copy).then_inc(at_ready, 1)
                    if s >= 5 and s % 4 == 1 or s == ATTN_STEPS:
                        if s == ATTN_STEPS:
                            g = ATTN_STEPS // 4 - 1
                        else:
                            g = (s - 5) // 4
                        act.wait_ge(pv_full, g + 1)
                        act.activation(o_all[:, 4 * g:4 * g + 4, :].rearrange("p s e -> p (s e)"), ps[:, VALUE_BANK, :],
                                       ACT.Copy).then_inc(o_ready, 1)
                split_to(QUARTERS * SLABS.index("xk1") + 4)
                act.wait_ge(o_var, 1)
                act.activation(ssq, ssq, ACT.Sqrt).then_inc(o_root, 1)
                out("xk.2", xkT[:, 4:6, :], xk_ready, 3)
                for j in range(4):
                    act.wait_ge(full[bank(f"oT{j}")], turn(f"oT{j}"))
                    act.activation(o_s[0][:, 2 * j:2 * j + 2, :], ps[:, bank(f"oT{j}"), :].rearrange("p (c t) -> p c t", c=2),
                                   ACT.Copy, scale=sub_col).then_inc(hi_ready, 1)
                act.wait_ge(ln_xc, 1)
                act.activation(sq, conv, ACT.Square).then_inc(ln_sq, 1)
                out("xk.3", xkT[:, 6:8, :], xk_ready, 4)
                for j, g in enumerate((gate_c, gate_a)):
                    act.wait_ge(gate_raw, 4 * (j + 1))
                    act.activation(g, g, ACT.Sigmoid).then_inc(gate_ready, 1)
                act.wait_ge(ln_var, 1)
                act.activation(rs_ln[:], rs_ln[:], ACT.Sqrt).then_inc(ln_root, 1)
                ahead("ao.0")
                act.wait_ge(ln_y, 1)
                for c in range(DC):
                    act.activation(conv[:, c, :], conv[:, c, :], ACT.Silu, bias=par[:, c, R_LNB:R_LNB + 1],
                                   scale=par[:, c, R_LNG:R_LNG + 1]).then_inc(ln_out, 1)
                ahead("ao.1")
                act.wait_ge(ln_out, DC)
                act.activation(conv_s[0], conv, ACT.Copy).then_inc(conv_hi_ready, 1)
                ahead("wo.3")
                squares(1)
                scale_rows(1, [1])
                for j in range(2):
                    out(f"xv.{j}", xv[:, j % 2, 0:SLAB], xv_ready, j + 1)
                turned_high("nx", x_s, R_X)
                for j in range(2, 4):
                    out(f"xv.{j}", xv[:, j % 2, SLAB:2 * SLAB], xv_ready, j + 1)

                def xexp(hd):
                    act.wait_ge(xnm_ready, hd + 1)
                    for s in range(TT):
                        act.activation(E[:, hd % 2, s, :], ps[:, 4 + hd % 2, s * T:(s + 1) * T], ACT.Exp,
                                       bias=xnm[:, hd, s:s + 1], accum_out=xsm[:, hd, s:s + 1]).then_inc(xexp_ready, 1)

                def xturn(hd):
                    act.wait_ge(xt_full, hd + 1)
                    act.activation(pT[:, hd % 2, :], ps[:, 6 + hd % 2, :], ACT.Copy).then_inc(xt_ready, 1)

                def xq_out(j):
                    out(f"xq.{j}", xqT[:, 2 * j:2 * j + 2, :].rearrange("p c t -> p (c t)"), xq_ready, j + 1,
                        scale=1.0 / 16)

                xq_out(0)
                xq_out(1)
                xq_out(2)
                xexp(0)
                xq_out(3)
                split_to(QUARTERS * (len(SLABS) - 1))
                xexp(1)
                xturn(0)
                xexp(2)
                xturn(1)
                xexp(3)
                xturn(2)
                xturn(3)
                split_to(NQ)
                squares(2)
                turned("nf", uT, R_FFN)
                scale_rows(2, range(TT))
                act.wait_ge(r_diff, 1)
                act.activation(e_g, d_g, ACT.Exp).then_inc(r_exp, 1)
                act.wait_ge(r_gap, 1)
                act.activation(e_gap, gap, ACT.Exp).then_inc(r_gexp, 1)

                act.wait_ge(rank_ready, 1)
                passes = act.value_load(npass_i[0:1, 0:1], min_val=1, max_val=MAX_PASSES)
                def pair():
                    n = act.snap(u)
                    act.wait_ge(gt_done, n + 1)
                    act.activation(scat[:, 0, :], ps[:, 2, 0:T], ACT.Copy, scale=cst[:, C_MLO:C_MLO + 1])
                    act.activation(scat[:, 1, :], ps[:, 2, 0:T], ACT.Copy,
                                   scale=cst[:, C_MHI:C_MHI + 1]).then_inc(scat_ready, 1)
                    act.wait_ge(up_done, n + 1)
                    act.activation(up_sb, ps[:, 1, :], ACT.Copy).then_inc(up_out, 1)
                    act.wait_ge(upt_done, n + 1)
                    a4 = ps[:, 2, :].rearrange("p (f e w s) -> p f e w s", f=FC, e=2, w=2)
                    act.activation(silu_t, a4[:, :, :, 0, :], ACT.Silu).then_inc(silu_ready, 1)
                    act.reg_add(u, u, 1)

                pair()
                act.wait_ge(ups_used, 2)
                for j in range(2):
                    act.wait_ge(ahead_in[1][j], L * 16 + 16)
                    act.activation(pair_slot(j)[:, DC // 2:DC, :], ahead_buf[1][j], ACT.Copy).then_inc(up_in[1][j], 16)
                with act.Fori(1, PAIRS) as _i:
                    pair()
                with act.If(passes > 1):
                    with act.Fori(1, passes) as _p:
                        with act.Fori(0, PAIRS) as _i:
                            pair()
                    act.nop()
                act.nop()
                n = act.snap(u)
                act.wait_ge(added, n)
                act.activation(h[:, 1, :], ps[:, 6:8, :].rearrange("p b n -> p (b n)"), ACT.Copy)
                act.drain().then_inc(layer_end, 1)
                act.wait_ge(layer_go, L + 1)
            for s in range(TT):
                act.activation(uT[:, s * FC:(s + 1) * FC, :].rearrange("p c t -> p (c t)"), h[:, s, :], ACT.Square,
                               accum_out=ss[:, s:s + 1]).then_inc(fin_ss, 1)
            act.wait_ge(fin_var, 1)
            act.activation(ss, ss, ACT.Sqrt).then_inc(fin_sq, 1)

        @block.vector
        def _(dve):
            sc = Chain(dve, st_ch)
            dve.memset(glu_pad[:], 0.0)
            dve.wait_ge(pos_in, 16)
            dve.wait_ge(cst_in, 16)
            posf = wk(256, T)
            ang, turns, red = posf, wk(512, 2, T), wk(512, 2, T)
            sc.link(dve.tensor_copy(posf, work[:, 0:T].bitcast(I32)))
            sc.link(dve.tensor_scalar(ang, posf, cst[:, C_INVF:C_INVF + 1], None, ALU.mult))
            kk = rt2
            sc.link(dve.tensor_scalar(kk[:, 1, :], ang, 1.0 / (2 * math.pi), 0.0, ALU.mult, ALU.add))
            sc.link(dve.tensor_scalar(kk[:, 0, :], ang, 1.0 / (2 * math.pi), 0.25, ALU.mult, ALU.add))
            sc.link(dve.tensor_scalar(kk, kk, MAGIC, None, ALU.add))
            sc.link(dve.tensor_scalar(kk, kk, MAGIC, None, ALU.subtract))
            prev = ang.unsqueeze(1).to_broadcast([P, 2, T])
            for part in TWO_PI:
                sc.link(dve.scalar_tensor_tensor(red, kk, -part, prev, ALU.mult, ALU.add))
                prev = red
            sc.link(dve.tensor_scalar(red[:, 0, :], red[:, 0, :], math.pi / 2, None, ALU.add))
            ins = dve.tensor_scalar(red, red, SIN_MAX, -SIN_MAX, ALU.min, ALU.max)
            ins.then_inc(st_ang, 1)
            dve.wait_ge(st_mss, TT)
            dve.tensor_scalar(mss, mss, 1.0 / D, RMS_EPS, ALU.mult, ALU.add).then_inc(st_mvar, 1)
            dve.wait_ge(st_msq, 1)
            sc.link(dve.reciprocal(mss, mss))
            for s in range(TT):
                dve.tensor_scalar(memN[:, s, :], memN[:, s, :], mss[:, s:s + 1], None, ALU.mult).then_inc(st_mn, 1)
            dve.wait_ge(st_rows, 1)
            for i in range(LAYERS):
                sc.link(dve.tensor_copy(pk[:, i, 0:K_WR], ps[:, 4 + i, 0:K_WR]))
            dve.wait_ge(lam_in, 16 * 4 * LAYERS)
            dve.wait_ge(st_cs, 1)
            lv = work[:, 1024:1024 + LAYERS * 256].rearrange("p (l w d) -> p l w d", l=2 * LAYERS, w=2)
            lp = wk(1024 + LAYERS * 256, 2 * LAYERS, 64)
            sc.link(dve.tensor_tensor(lp, lv[:, :, 0, :], lv[:, :, 1, :], ALU.mult))
            dve.tensor_reduce(small[:, 104:108], lp, AX.X, ALU.add).then_inc(st_dot, 1)
            dve.wait_ge(st_exp, 1)
            for i in range(LAYERS):
                lam = pk[:, i, K_LAM:K_LAM + 1]
                sc.link(dve.tensor_tensor(lam, small[:, 109 + 2 * i:110 + 2 * i], small[:, 108 + 2 * i:109 + 2 * i],
                                          ALU.subtract))
                sc.link(dve.tensor_tensor(lam, lam, cst[:, C_LAM + i:C_LAM + i + 1], ALU.subtract))
            dve.wait_ge(sub_in, 16 * LAYERS)
            for i in range(LAYERS):
                sc.link(dve.tensor_scalar(pk[:, i, K_SUB:K_SUB + 1], pk[:, i, K_SUB:K_SUB + 1],
                                          cst[:, C_OML + i:C_OML + i + 1], None, ALU.mult))
            dve.wait_ge(st_mt, 1)
            for j in range(4):
                for i in range(LAYERS):
                    gain = pk[:, i, 0:K_WR].rearrange("p (c r) -> p c r", c=DC)[:, 2 * j:2 * j + 2, R_MEM]
                    dst = memT if i == 0 else chunks(1 + i)
                    ins = dve.tensor_tensor(dst[:, 2 * j:2 * j + 2, :],
                                            ps[:, j, :].rearrange("p (c t) -> p c t", c=2),
                                            gain.unsqueeze(2).to_broadcast([P, 2, T]), ALU.mult)
                ins.then_inc(st_mg, 1)

            u = dve.alloc_register("dve_unit")
            dve.reg_mov(u, 0)
            with dve.Fori(0, LAYERS) as L:
                ch = Chain(dve, dch)

                def both(job):
                    return ps[:, bank(job), :].rearrange("p (c t) -> p c t", c=2)

                def bcast(job, n, row):
                    return par[:, n:n + 2, row].unsqueeze(2).to_broadcast([P, 2, T])

                def variance(n):
                    dve.wait_ge(n_ss, TT * (n + 1))
                    dve.tensor_scalar(ss, ss, 1.0 / D, RMS_EPS, ALU.mult, ALU.add).then_inc(n_var, 1)

                def inverse(n):
                    dve.wait_ge(n_root, n + 1)
                    dve.reciprocal(ss, ss).then_inc(n_inv, 1)
                    dve.wait_ge(n_inv, n + 1)

                def norm(n):
                    variance(n)
                    inverse(n)
                    dve.tensor_scalar(uN[:, 0, :], h[:, 0, :], ss[:, 0:1], None, ALU.mult).then_inc(n_ready, 1)

                def turned(kind, dst, row):
                    for j in (0, 2):
                        job = f"{kind}{j}"
                        dve.wait_ge(full[bank(job)], turn(job))
                        dve.tensor_tensor(dst[:, 2 * j:2 * j + 2, :], both(job), bcast(job, 2 * j, row),
                                          ALU.mult).then_inc(free[bank(job)], 1)

                def low(job, dst, c, n, have, scale, ready):
                    hi, lo = (d[:, c:c + n, :] for d in dst)
                    at = c % 2
                    dve.wait_ge(*have)
                    dve.scalar_tensor_tensor(lo, both(job)[:, at:at + n, :], scale, hi.bitcast(F32), ALU.mult,
                                             ALU.subtract).then_inc(ready, 1)

                def turned_low(kind, dst, row, n):
                    for c in range(DC):
                        low(f"{kind}{c // 2}", dst, c, 1, (hi_ready, n + 2 * (c // 2) + 2), par[:, c, row:row + 1], lo_ready)
                        if c % 2:
                            dve.wait_ge(lo_ready, n + c + 1)
                            dve.sem_inc(free[bank(f"{kind}{c // 2}")], 1)

                for j in range(4):
                    dve.wait_ge(mem_hi, j + 1)
                    dve.tensor_tensor(mem_s[1][:, 2 * j:2 * j + 2, :], memT[:, 2 * j:2 * j + 2, :],
                                      mem_s[0][:, 2 * j:2 * j + 2, :].bitcast(F32), ALU.subtract).then_inc(mem_lo, 1)
                dve.tensor_copy(cur[:, 0:K_WR], pk[:, L, 0:K_WR]).then_inc(cur_ready, 1)
                dve.wait_ge(cur_ready, 1)
                norm(0)
                turned_low("nm", u_s, R_MIX, 0)

                conv_last = {}
                taps = [(c0, t) for c0 in range(0, DC, 2) for t in range(KERN)]

                def conv_taps(n, have):
                    for _ in range(n):
                        if not taps or taps[0][0] // 2 >= have:
                            return
                        c0, t = taps.pop(0)
                        for c in (c0, c0 + 1):
                            src, wt = glu_pad[:, c, t:t + T], par[:, c, t:t + 1]
                            if t == 0:
                                dve.wait_ge(glu_ready, c0 // 2 + 1)
                                ins = dve.tensor_scalar(conv[:, c, :], src, wt, par[:, c, R_DB:R_DB + 1], ALU.mult, ALU.add)
                            else:
                                ch.after(conv_last[c])
                                ins = dve.scalar_tensor_tensor(conv[:, c, :], src, wt, conv[:, c, :], ALU.mult, ALU.add)
                            if not taps and c == c0 + 1:
                                ins.then_inc(conv_ready, 1)
                            else:
                                conv_last[c] = ch.note(ins)

                for j in range(4):
                    dve.wait_ge(sig_ready, j + 1)
                    dve.wait_ge(full[bank(f"a.{j}")], turn(f"a.{j}"))
                    dve.tensor_tensor(glu[:, 2 * j:2 * j + 2, :], both(f"a.{j}"), sg[:, j % 2], ALU.mult).then_inc(glu_ready, 1)
                    dve.wait_ge(glu_ready, j + 1)
                    dve.sem_inc(free[bank(f"a.{j}")], 1)
                    conv_taps(TAPS[0][j], j + 1)
                dve.wait_ge(router_in, 16 * 4 * LAYERS)
                dve.tensor_copy(cur[:, K_WR:NPK], pk[:, L, K_WR:NPK]).then_inc(cur_ready, 1)
                dve.wait_ge(cur_ready, 2)
                dve.wait_ge(st_msto, 16 * LAYERS)
                cos2 = rope_cs[:, 0:1, :].to_broadcast([P, 2, T])
                sin2 = rope_cs[:, 1:2, :].to_broadcast([P, 2, T])
                for j in range(8):
                    job = f"q.{j}" if j < 4 else f"k.{j - 4}"
                    dst = (qT if j < 4 else kT)[:, 2 * (j % 4):2 * (j % 4) + 2, :]
                    dve.wait_ge(qraw_ready, j + 1)
                    k1 = ch.note(dve.tensor_tensor(rt1, qraw[:, j % 2], cos2, ALU.mult))
                    conv_taps(TAPS[1][0], 4)
                    dve.wait_ge(rope_full, j + 1)
                    k2 = ch.note(dve.tensor_tensor(rt2, ps[:, ROPE_BANK, :].rearrange("p (c t) -> p c t", c=2), sin2, ALU.mult))
                    ch.after(k2)
                    dve.tensor_tensor(dst, rt1, rt2, ALU.add).then_inc(rope_ready, 1)
                    conv_taps(TAPS[1][1], 4)
                conv_taps(TAPS[1][2], 4)

                def row_max(s):
                    dve.wait_ge(s_full, s + 1)
                    dve.tensor_reduce(nmx[:, s, :], ps[:, score_banks(s):score_banks(s) + 2, 0:T], AX.X, ALU.max,
                                      negate=True).then_inc(nm_ready, 1)

                dve.wait_ge(rope_ready, 8)
                row_max(0)
                for s in range(ATTN_STEPS):
                    if s + 1 < ATTN_STEPS:
                        row_max(s + 1)
                    dve.wait_ge(exp_ready, 2 * (s + 1))
                    rc = sm[:, s, :]
                    if s >= 1:
                        dve.wait_ge(a_ready, s)
                    ch.link(dve.reciprocal(rc, rc))
                    ch.link(dve.tensor_scalar(rc[:, 1:2], rc[:, 1:2], neglam, None, ALU.mult))
                    ch.link(dve.tensor_scalar(etmp, E[:, s % 2, 1, :], rc[:, 1:2], None, ALU.mult))
                    if s >= 2:
                        dve.wait_ge(at_full, s - 1)
                    dve.scalar_tensor_tensor(amix[:, s % 2, :], E[:, s % 2, 0, :], rc[:, 0:1], etmp, ALU.mult,
                                             ALU.add).then_inc(a_ready, 1)
                    if s % 2 == 1:
                        job = f"gate.{s // 2}"
                        g, j = ((gate_c, s // 2) if s < 8 else (gate_a, s // 2 - 4))
                        dve.wait_ge(full[bank(job)], turn(job))
                        dve.tensor_copy(g[:, 2 * j:2 * j + 2, :], both(job)).then_inc(gate_raw, 1)
                        dve.wait_ge(gate_raw, s // 2 + 1)
                        dve.sem_inc(free[bank(job)], 1)
                    conv_taps(TAPS[2], 4)
                conv_taps(len(taps), 4)
                dve.wait_ge(o_ready, 4)
                sqo = big[:, 1, :].rearrange("p (s e) -> p s e", s=ATTN_STEPS)
                ch.link(dve.tensor_tensor(sqo, o_all, o_all, ALU.mult))
                ch.link(dve.tensor_reduce(ssq, sqo, AX.X, ALU.add))
                dve.tensor_scalar(ssq, ssq, 1.0 / P, LN_EPS, ALU.mult, ALU.add).then_inc(o_var, 1)
                dve.wait_ge(o_root, 1)
                ch.link(dve.reciprocal(ssq, ssq))
                dve.tensor_tensor(o_all, o_all, ssq.unsqueeze(2).to_broadcast([P, ATTN_STEPS, P]),
                                  ALU.mult).then_inc(o_norm, 1)
                dve.wait_ge(full[bank("mean")], turn("mean"))
                dve.wait_ge(conv_ready, 1)
                mu = ps[:, bank("mean"), 0:T].unsqueeze(1).to_broadcast([P, DC, T])
                dve.tensor_tensor(conv, conv, mu, ALU.subtract).then_inc(ln_xc, 1)
                dve.wait_ge(ln_xc, 1)
                dve.sem_inc(free[bank("mean")], 1)
                for j in range(4):
                    low(f"oT{j}", o_s, 2 * j, 2, (hi_ready, DC + j + 1), sub_col, lo_ready)
                    dve.wait_ge(lo_ready, DC + j + 1)
                    dve.sem_inc(free[bank(f"oT{j}")], 1)
                dve.wait_ge(full[bank("var")], turn("var"))
                dve.tensor_scalar(rs_ln[:], ps[:, bank("var"), 0:T], LN_EPS, None, ALU.add).then_inc(ln_var, 1)
                dve.wait_ge(ln_var, 1)
                dve.sem_inc(free[bank("var")], 1)
                dve.wait_ge(ln_root, 1)
                ch.link(dve.reciprocal(rs_ln[:], rs_ln[:]))
                dve.tensor_tensor(conv, conv, rs_ln[:].unsqueeze(1).to_broadcast([P, DC, T]), ALU.mult).then_inc(ln_y, 1)
                dve.wait_ge(conv_hi_ready, 1)
                dve.tensor_tensor(conv_s[1], conv, conv_s[0].bitcast(F32), ALU.subtract).then_inc(conv_lo_ready, 1)
                dve.wait_ge(gate_ready, 2)
                mg = {}
                for j in range(4):
                    job = f"ao.{j}"
                    dve.wait_ge(full[bank(job)], turn(job))
                    mg[j] = ch.note(dve.tensor_tensor(merged[:, 2 * j:2 * j + 2, :], both(job),
                                                      gate_a[:, 2 * j:2 * j + 2, :], ALU.mult))
                    ch.after(mg[j])
                    dve.sem_inc(free[bank(job)], 1)
                for j in range(4):
                    job = f"co.{j}"
                    dve.wait_ge(full[bank(job)], turn(job))
                    g = gate_c[:, 2 * j:2 * j + 2, :]
                    ch.link(dve.tensor_tensor(g, both(job), g, ALU.mult))
                    dve.sem_inc(free[bank(job)], 1)
                    m = merged[:, 2 * j:2 * j + 2, :]
                    hi, lo = (d[:, 2 * j:2 * j + 2, :] for d in m_s)
                    dve.tensor_tensor(hi, m, g, ALU.add).then_inc(m_hi, 1)
                    ch.link(dve.tensor_tensor(m, m, g, ALU.add))
                    dve.wait_ge(m_hi, j + 1)
                    dve.tensor_tensor(lo, m, hi.bitcast(F32), ALU.subtract).then_inc(merged_ready, 1)

                def add_to_h(kind, base):
                    for j in range(4):
                        job, s, half = f"{kind}{j}", j % 2, j // 2
                        dve.wait_ge(full[bank(job)], turn(job))
                        hs = h[:, s, half * SLAB:(half + 1) * SLAB]
                        dve.tensor_tensor(hs, hs, ps[:, bank(job), :], ALU.add).then_inc(h_ready, 1)
                        dve.wait_ge(h_ready, base + j + 1)
                        dve.sem_inc(free[bank(job)], 1)

                dve.wait_ge(merged_ready, 4)
                dve.sem_inc(ahead_free, 1)
                add_to_h("wo.", 0)
                norm(1)
                turned_low("nx", x_s, R_X, DC + 4)

                def xmax(hd):
                    dve.wait_ge(xs_full, hd + 1)
                    dve.tensor_reduce(xnm[:, hd, :], ps[:, 4 + hd % 2, :].rearrange("p (s k) -> p s k", s=TT), AX.X,
                                      ALU.max, negate=True).then_inc(xnm_ready, 1)

                def xscale(hd):
                    dve.wait_ge(xexp_ready, TT * (hd + 1))
                    ch.link(dve.reciprocal(xsm[:, hd, :], xsm[:, hd, :]))
                    for s in range(TT):
                        dve.tensor_scalar(E[:, hd % 2, s, :], E[:, hd % 2, s, :], xsm[:, hd, s:s + 1], None,
                                          ALU.mult).then_inc(xp_ready, 1)

                def px_out(hd):
                    job = f"px{hd}"
                    dve.wait_ge(full[bank(job)], turn(job))
                    hi, lo = (d[:, 2 * hd:2 * hd + 2, :] for d in xo_s)
                    dve.tensor_copy(hi, both(job)).then_inc(xo_hi, 1)
                    dve.wait_ge(xo_hi, hd + 1)
                    dve.tensor_tensor(lo, both(job), hi.bitcast(F32), ALU.subtract).then_inc(xo_ready, 1)
                    dve.wait_ge(xo_ready, hd + 1)
                    dve.sem_inc(free[bank(job)], 1)

                xmax(0)
                xscale(0)
                for hd in range(1, XHEADS):
                    xmax(hd)
                    xscale(hd)
                    if hd >= 2:
                        px_out(hd - 2)
                px_out(2)
                px_out(3)
                add_to_h("xo.", 4)
                variance(2)
                turned("nf", uT, R_FFN)
                inverse(2)

                def over(a, n):
                    return a.unsqueeze(2).to_broadcast([P, TT, n])

                def desc(n):
                    return cst[:, C_DESC + EXPERTS - n:C_DESC + EXPERTS].unsqueeze(1).to_broadcast([P, TT, n])

                dve.wait_ge(full[bank("router")], turn("router"))
                for s in range(TT):
                    ch.link(dve.scalar_tensor_tensor(logit[:, s, :], ps[:, bank("router"), s * NR:(s + 1) * NR],
                                                     ss[:, s:s + 1], rb, ALU.mult, ALU.add))
                lg = logit[:, :, 0:GROUPS]
                ch.link(dve.tensor_reduce(m_g, lg, AX.X, ALU.max))
                dve.tensor_tensor(d_g, lg, over(m_g, GROUPS), ALU.subtract).then_inc(r_diff, 1)
                ch.link(dve.tensor_tensor(eq_g, lg, over(m_g, GROUPS), ALU.is_equal))
                ch.link(dve.tensor_tensor(eq_g, eq_g, desc(GROUPS), ALU.mult))
                ch.link(dve.tensor_reduce(mx_g, eq_g, AX.X, ALU.max))
                ch.link(dve.tensor_tensor(oh_g, eq_g, over(mx_g, GROUPS), ALU.is_equal))
                ch.link(dve.tensor_scalar(oh_g, oh_g, -1.0, 1e30, ALU.add, ALU.mult))
                for s in range(TT):
                    ch.link(dve.tensor_tensor(masked[:, s, :].rearrange("p (g e) -> p g e", g=GROUPS),
                                              logit[:, s, GROUPS:NR].rearrange("p (g e) -> p g e", g=GROUPS),
                                              oh_g[:, s, :].unsqueeze(2).to_broadcast([P, GROUPS, PER_GROUP]), ALU.add))
                for top, oh in ((top1, oh1), (top2, oh2)):
                    ch.link(dve.tensor_reduce(top, masked, AX.X, ALU.max))
                    ch.link(dve.tensor_tensor(first, masked, over(top, EXPERTS), ALU.is_equal))
                    ch.link(dve.tensor_tensor(first, first, desc(EXPERTS), ALU.mult))
                    ch.link(dve.tensor_reduce(mx_e, first, AX.X, ALU.max))
                    ch.link(dve.tensor_tensor(oh, first, over(mx_e, EXPERTS), ALU.is_equal))
                    if oh is oh1:
                        ch.link(dve.scalar_tensor_tensor(masked, oh1, -3e30, masked, ALU.mult, ALU.add))
                dve.tensor_tensor(gap, top2, top1, ALU.subtract).then_inc(r_gap, 1)
                dve.tensor_tensor(picked, oh1, oh2, ALU.add).then_inc(r_mask, 1)
                dve.wait_ge(r_exp, 1)
                ch.link(dve.tensor_reduce(g_w, e_g, AX.X, ALU.add))
                ch.link(dve.reciprocal(g_w, g_w))
                dve.wait_ge(r_gexp, 1)
                ch.link(dve.tensor_scalar(w_1, e_gap, 1.0, None, ALU.add))
                ch.link(dve.reciprocal(w_1, w_1))
                ch.link(dve.tensor_tensor(w_1, w_1, g_w, ALU.mult))
                ch.link(dve.tensor_tensor(w_2, w_1, e_gap, ALU.mult))
                ch.link(dve.tensor_tensor(tok_w, oh1, over(w_1, EXPERTS), ALU.mult))
                ch.link(dve.tensor_tensor(tok_w2, oh2, over(w_2, EXPERTS), ALU.mult))
                ch.link(dve.tensor_tensor(tok_w, tok_w, tok_w2, ALU.add))
                rkb = ps[:, bank("rank"), :]
                dve.wait_ge(full[bank("rank")], turn("rank"))
                ch.link(dve.tensor_scalar(rank, rkb[:, 0:TT * EXPERTS].rearrange("p (s e) -> p s e", s=TT), float(D), 1.0,
                                          ALU.mult, ALU.add))
                ch.link(dve.tensor_tensor(rank, rank, picked, ALU.mult))
                ch.link(dve.tensor_scalar(rank, rank, -1.0, None, ALU.add))
                ch.link(dve.tensor_reduce(cnt1, rkb[:, TT * EXPERTS:(TT + 1) * EXPERTS], AX.X, ALU.max))
                ch.link(dve.tensor_scalar(cnt1, cnt1, float(D), None, ALU.mult))
                ch.link(dve.tensor_tensor(thr7, cst[:, C_THR:C_THR + MAX_PASSES - 1],
                                          cnt1.to_broadcast([P, MAX_PASSES - 1]), ALU.is_lt))
                ch.link(dve.tensor_reduce(cnt1, thr7, AX.X, ALU.add))
                dve.tensor_scalar(npass_i[:], cnt1, 1.0, None, ALU.add).then_inc(rank_ready, 1)
                dve.wait_ge(rank_ready, 1)
                dve.sem_inc(np_ready, 1)

                passes = dve.value_load(npass_i[0:1, 0:1], min_val=1, max_val=MAX_PASSES)
                with dve.Fori(0, passes) as _p:
                    with dve.Fori(0, PAIRS) as i:
                        n = dve.snap(u)
                        dve.tensor_tensor(sel, rank[:, :, bass.ds(i * 2, 2)].unsqueeze(3).to_broadcast([P, TT, 2, CAP]),
                                          iota.unsqueeze(1).unsqueeze(1).to_broadcast([P, TT, 2, CAP]),
                                          ALU.is_equal).then_inc(sel_ready, 1)
                        dve.wait_ge(sel_ready, n + 1)
                        for dup in range(2):
                            dve.tensor_tensor(spread[:, :, :, dup, :], sel,
                                              tok_w[:, :, bass.ds(i * 2, 2)].unsqueeze(3).to_broadcast([P, TT, 2, CAP]),
                                              ALU.mult).then_inc(spread_ready, 1)
                        dve.wait_ge(xg_done, n + 1)
                        dve.tensor_tensor(xe, ps[:, 0, :].rearrange("p (c s) -> p c s", c=DC),
                                          par[:, :, R_FFN].unsqueeze(2).to_broadcast([P, DC, 2 * CAP]),
                                          ALU.mult).then_inc(xe_ready, 1)
                        dve.wait_ge(silu_ready, n + 1)
                        a4 = ps[:, 2, :].rearrange("p (f e w s) -> p f e w s", f=FC, e=2, w=2)
                        dve.tensor_tensor(up_t, silu_t, a4[:, :, :, 1, :], ALU.mult).then_inc(upt_ready, 1)
                        dve.wait_ge(y_done, n + 1)
                        dve.tensor_copy(y_sb, ps[:, 3, :]).then_inc(y_out, 1)
                        dve.reg_add(u, u, 1)
                    dve.drain()
                    dve.tensor_scalar(rank, rank, -float(CAP), None, ALU.add)
                    dve.drain()
                n = dve.snap(u)
                dve.wait_ge(added, n)
                dve.tensor_copy(h[:, 0, :], ps[:, 4:6, :].rearrange("p b n -> p (b n)"))
                dve.drain()
                dve.wait_ge(layer_end, 3 * L + 3)
                dve.sem_inc(layer_clear, 1)
                dve.sem_clear(cleared)
                dve.sem_inc(layer_go, 1)

            fc = Chain(dve, fin_ch)
            dve.wait_ge(fin_ss, TT)
            dve.tensor_scalar(ss, ss, 1.0 / D, RMS_EPS, ALU.mult, ALU.add).then_inc(fin_var, 1)
            dve.wait_ge(fin_sq, 1)
            fc.link(dve.reciprocal(ss, ss))
            dve.wait_ge(fin_g, 16)
            for s in range(TT):
                dve.scalar_tensor_tensor(uN[:, s, :], h[:, s, :], ss[:, s:s + 1],
                                         memT[:, 0:FC, :].rearrange("p c t -> p (c t)"), ALU.mult,
                                         ALU.mult).then_inc(fin_out, 1)

        @block.tensor
        def _(pe):
            prow = big[:, 0, :].rearrange("p (l d) -> p l d", l=LAYERS)
            pe.sem_inc(freed[0], EARLY_STEPS)
            pe.sem_inc(freed[1], LATE_STEPS)
            pe.wait_ge(cst_in, 16)
            pe.wait_ge(par_in, 16 * 8)
            for i in range(LAYERS):
                for c in range(DC):
                    last = pe.transpose(ps[:, 4 + i, c * ROWS:(c + 1) * ROWS], prow[0:ROWS, i, c * P:(c + 1) * P],
                                        ident[0:ROWS, 0:ROWS])
            last.then_inc(st_rows, 1)

            def turn_rows(dst, src, j):
                for c in range(2):
                    for s in range(TT):
                        last = pe.transpose(dst[:, c * T + s * P:c * T + (s + 1) * P],
                                            src[:, s, (2 * j + c) * P:(2 * j + c + 1) * P], ident)
                return last

            pe.wait_ge(st_mn, TT)
            for j in range(4):
                last = turn_rows(ps[:, j, :], memN, j)
            last.then_inc(st_mt, 1)
            pe.wait_ge(st_mg, 4)

            u = pe.alloc_register("pe_unit")
            pe.reg_mov(u, 0)
            with pe.Fori(0, LAYERS) as L:
                def begin(job):
                    if turn(job) > 1:
                        pe.wait_ge(free[bank(job)], turn(job) - 1)
                    return ps[:, bank(job), :]

                owed = []

                def settle():
                    for job in owed:
                        pe.wait_ge(full[bank(job)], turn(job))
                        pe.sem_inc(w_used, 1)
                    owed.clear()

                def used(last, job, more=()):
                    if job is None:
                        last.then_inc(w_used, 1)
                    else:
                        last.then_inc(full[bank(job)], 1)
                        owed.append(job)

                def columns(dst, q, xs, job=None, have=None):
                    hi, lo = split_quarter(q, 0), split_quarter(q, 1)
                    pe.wait_ge(w_hi, q + 1)
                    for k in range(DC):
                        if have is not None and k % have[2] == 0:
                            pe.wait_ge(have[0], have[1] + k // have[2] + 1)
                        pe.matmul(dst, hi[:, k, :], xs[0][:, k, :], start=(k == 0), stop=False)
                        pe.matmul(dst, hi[:, k, :], xs[1][:, k, :], start=False, stop=False)
                    settle()
                    pe.wait_ge(w_lo, q + 1)
                    for k in range(DC):
                        last = pe.matmul(dst, lo[:, k, :], xs[0][:, k, :], start=False, stop=(k == DC - 1))
                    used(last, job)

                def col_jobs(kind, slab, jobs, xs, after=None, have=None):
                    q = QUARTERS * SLABS.index(slab)
                    for n, j in enumerate(jobs):
                        job = f"{kind}{j}"
                        dst = begin(job)
                        for c in range(2):
                            columns(dst[:, c * T:(c + 1) * T], q + 2 * n + c, xs, job if c else None,
                                    have if n == c == 0 else None)
                        if after:
                            after(j)

                def row_jobs(kind, slab, jobs, xs, after=None, have=None):
                    q0 = QUARTERS * SLABS.index(slab)
                    dst = [begin(f"{kind}{j}") for j in jobs]
                    for c in range(QUARTERS):
                        q = q0 + c
                        hi, lo = split_quarter(q, 0), split_quarter(q, 1)
                        pe.wait_ge(w_hi, q + 1)
                        if have is not None:
                            pe.wait_ge(have, c + 1)
                        for s in range(TT):
                            for k in range(2):
                                xh, xl = (d[:, 2 * c + k, s * P:(s + 1) * P] for d in xs)
                                pe.matmul(dst[s], xh, hi[:, k, :], start=(c == 0 and k == 0), stop=False)
                                pe.matmul(dst[s], xl, hi[:, k, :], start=False, stop=False)
                        settle()
                        pe.wait_ge(w_lo, q + 1)
                        for s in range(TT):
                            for k in range(2):
                                last = pe.matmul(dst[s], xs[0][:, 2 * c + k, s * P:(s + 1) * P], lo[:, k, :],
                                                 start=False, stop=(c == QUARTERS - 1 and k == 1))
                            if c == QUARTERS - 1 and s < TT - 1:
                                last.then_inc(full[bank(f"{kind}{jobs[s]}")], 1)
                        used(last, f"{kind}{jobs[-1]}" if c == QUARTERS - 1 else None)
                        if after and c == 0:
                            after()

                def turn_norm(kind, src):
                    for j in range(4):
                        job = f"{kind}{j}"
                        turn_rows(begin(job), src, j).then_inc(full[bank(job)], 1)

                col_jobs("xk.", "xk0", (0, 1), mem_s, have=(mem_lo, 0, 2))
                settle()
                pe.wait_ge(n_ready, 1)
                pe.wait_ge(n_ready_act, 1)
                turn_norm("nm", uN)
                col_jobs("a.", "a0", (0, 1), u_s, have=(lo_ready, 0, 1))
                col_jobs("g.", "g0", (0, 1), u_s)
                col_jobs("a.", "a1", (2, 3), u_s)
                col_jobs("g.", "g1", (2, 3), u_s)

                def rotate(j):
                    pe.wait_ge(qraw_ready, j + 1)
                    if j >= 1:
                        pe.wait_ge(rope_ready, j)
                    pe.matmul(ps[:, ROPE_BANK, :], rot, qraw[:, j % 2].rearrange("p c t -> p (c t)"), start=True,
                              stop=True).then_inc(rope_full, 1)

                col_jobs("q.", "q0", (0, 1), u_s, lambda j: rotate(j - 1) if j else None)
                col_jobs("q.", "q1", (2, 3), u_s, lambda j: rotate(j - 1))
                col_jobs("k.", "k0", (0, 1), u_s, lambda j: rotate(j + 3))
                col_jobs("k.", "k1", (2, 3), u_s, lambda j: rotate(j + 3))
                row_jobs("v.", "v0", (0, 1), u_s, lambda: rotate(7))
                row_jobs("v.", "v1", (2, 3), u_s)
                settle()

                def scores(s):
                    hd, t = s // TT, s % TT
                    if s >= 2:
                        pe.wait_ge(exp_ready, 2 * (s - 1))
                    for c in range(2):
                        lo = 2 * HALF * c
                        last = pe.matmul(ps[:, score_banks(s) + c, 0:T], qT[lo:lo + 2 * HALF, hd, t * P:(t + 1) * P],
                                         kT[lo:lo + 2 * HALF, hd, :], start=True, stop=True)
                    last.then_inc(s_full, 1)

                def turn_mix(s):
                    pe.wait_ge(a_ready, s + 1)
                    if s >= 1:
                        pe.wait_ge(at_ready, s)
                    for k in range(2):
                        last = pe.transpose(ps[:, MIX_BANK, k * P:(k + 1) * P], amix[:, s % 2, k * P:(k + 1) * P], ident)
                    last.then_inc(at_full, 1)

                def values(s):
                    hd = s // TT
                    pe.wait_ge(at_ready, s + 1)
                    if s % 4 == 0 and s >= 4:
                        pe.wait_ge(o_ready, s // 4)
                    for k in range(2):
                        last = pe.matmul(ps[:, VALUE_BANK, (s % 4) * P:(s % 4 + 1) * P], aTs[:, s % 2, k * P:(k + 1) * P],
                                         v[:, k, hd * P:(hd + 1) * P], start=(k == 0), stop=(k == 1))
                    if s % 4 == 3:
                        last.then_inc(pv_full, 1)

                pe.wait_ge(rope_ready, 8)
                pe.wait_ge(v_ready, 4)
                scores(0)
                for s in range(ATTN_STEPS):
                    if s + 1 < ATTN_STEPS:
                        scores(s + 1)
                    job = f"gate.{s // 2}"
                    if s % 2 == 0:
                        gdst = begin(job)
                    columns(gdst[:, (s % 2) * T:(s % 2 + 1) * T], QUARTERS * SLABS.index("gc0") + s, u_s,
                            job if s % 2 else None)
                    if s >= 1:
                        values(s - 1)
                    turn_mix(s)
                values(ATTN_STEPS - 1)

                def xk_job(j):
                    dst = begin(f"xk.{j}")
                    for c in range(2):
                        columns(dst[:, c * T:(c + 1) * T], QUARTERS * SLABS.index("xk1") + 2 * (j - 2) + c, mem_s,
                                f"xk.{j}" if c else None)
                    settle()

                xk_job(2)

                def channel_mean(job, src):
                    dst = begin(job)
                    for c in range(DC):
                        last = pe.matmul(dst[:, 0:T], mean_m, src[:, c, :], start=(c == 0), stop=(c == DC - 1))
                    last.then_inc(full[bank(job)], 1)

                pe.wait_ge(conv_ready, 1)
                channel_mean("mean", conv)
                pe.wait_ge(o_norm, 1)
                for j in range(4):
                    dst = begin(f"oT{j}")
                    for c in range(2):
                        for s in range(TT):
                            last = pe.transpose(dst[:, c * T + s * P:c * T + (s + 1) * P],
                                                o_all[:, (2 * j + c) * TT + s, :], ident)
                    last.then_inc(full[bank(f"oT{j}")], 1)
                xk_job(3)
                pe.wait_ge(ln_sq, 1)
                channel_mean("var", sq)
                pe.wait_ge(lo_ready, DC + 4)
                col_jobs("ao.", "ao0", (0, 1), o_s)
                col_jobs("ao.", "ao1", (2, 3), o_s)
                pe.wait_ge(conv_lo_ready, 1)
                col_jobs("co.", "co0", (0, 1), conv_s)
                col_jobs("co.", "co1", (2, 3), conv_s)
                row_jobs("wo.", "wo0", (0, 1), m_s, have=merged_ready)
                row_jobs("wo.", "wo1", (2, 3), m_s)
                row_jobs("xv.", "xv0", (0, 1), mem_s)
                settle()
                pe.wait_ge(n_ready, 2)
                pe.wait_ge(n_ready_act, 2)
                turn_norm("nx", uN)
                row_jobs("xv.", "xv1", (2, 3), mem_s)

                def xscores(hd):
                    pe.wait_ge(xq_ready, hd + 1)
                    if hd == 0:
                        pe.wait_ge(xk_ready, 4)
                    if hd >= 2:
                        pe.wait_ge(xexp_ready, TT * (hd - 1))
                    for s in range(TT):
                        for c in range(2):
                            last = pe.matmul(ps[:, 4 + hd % 2, s * T:(s + 1) * T], xqT[:, 2 * hd + c, s * P:(s + 1) * P],
                                             xkT[:, 2 * hd + c, :], start=(c == 0), stop=(c == 1))
                    last.then_inc(xs_full, 1)

                def xturn(hd):
                    pe.wait_ge(xp_ready, TT * (hd + 1))
                    if hd >= 2:
                        pe.wait_ge(xt_ready, hd - 1)
                    for k in range(2):
                        for s in range(TT):
                            last = pe.transpose(ps[:, 6 + hd % 2, k * T + s * P:k * T + (s + 1) * P],
                                                E[:, hd % 2, s, k * P:(k + 1) * P], ident)
                    last.then_inc(xt_full, 1)

                def xvalues(hd):
                    pe.wait_ge(xt_ready, hd + 1)
                    if hd == 0:
                        pe.wait_ge(xv_ready, 4)
                    dst = begin(f"px{hd}")
                    for c in range(2):
                        for k in range(2):
                            last = pe.matmul(dst[:, c * T:(c + 1) * T], xv[:, k, (2 * hd + c) * P:(2 * hd + c + 1) * P],
                                             pT[:, hd % 2, k * T:(k + 1) * T], start=(k == 0), stop=(k == 1))
                    last.then_inc(full[bank(f"px{hd}")], 1)

                col_jobs("xq.", "xq0", (0, 1), x_s, have=(lo_ready, DC + 4, 1))

                def xq_job(j):
                    dst = begin(f"xq.{j}")
                    for c in range(2):
                        columns(dst[:, c * T:(c + 1) * T], QUARTERS * SLABS.index("xq0") + 2 * j + c, x_s,
                                f"xq.{j}" if c else None)

                xq_job(2)
                xscores(0)
                xq_job(3)
                settle()
                xscores(1)
                xturn(0)
                for hd in range(2, XHEADS + 2):
                    if hd < XHEADS:
                        xscores(hd)
                    if hd - 1 < XHEADS:
                        xturn(hd - 1)
                    xvalues(hd - 2)
                row_jobs("xo.", "xo0", (0, 1), xo_s, have=xo_ready)
                row_jobs("xo.", "xo1", (2, 3), xo_s)
                settle()
                pe.sem_inc(freed[1], LATE_STEPS)
                pe.wait_ge(h_ready, 8)
                turn_norm("nf", h)
                pe.wait_ge(cur_ready, 2)
                dst = begin("router")
                for s in range(TT):
                    for k in range(DC):
                        if s == 0 and k % 2 == 0:
                            pe.wait_ge(free[bank(f"nf{k // 2}")], turn(f"nf{k // 2}"))
                            if k % 4 == 2:
                                pe.wait_ge(n_turned, k // 4 + 1)
                        last = pe.matmul(dst[:, s * NR:(s + 1) * NR], uT[:, k, s * P:(s + 1) * P], wr[:, k, :],
                                         start=(k == 0), stop=(k == DC - 1))
                last.then_inc(full[bank("router")], 1)
                for s in range(TT):
                    for half in range(HALVES):
                        pe.matmul(ps[:, 4 + 2 * s + half, :], ident, h[:, s, half * SLAB:(half + 1) * SLAB],
                                  start=True, stop=True)
                pe.wait_ge(r_mask, 1)
                dst = ps[:, bank("rank"), :]
                pe.matmul(dst[:, 0:EXPERTS], tri, picked[:, 0, :], start=True, stop=True)
                pe.matmul(dst[:, EXPERTS:2 * EXPERTS], tri, picked[:, 1, :], start=True, stop=False)
                pe.matmul(dst[:, EXPERTS:2 * EXPERTS], mean_m, picked[:, 0, :], start=False, stop=True)
                pe.matmul(dst[:, 2 * EXPERTS:3 * EXPERTS], mean_m, picked[:, 0, :], start=True, stop=False)
                pe.matmul(dst[:, 2 * EXPERTS:3 * EXPERTS], mean_m, picked[:, 1, :], start=False,
                          stop=True).then_inc(full[bank("rank")], 1)

                pe.wait_ge(n_ready_act, 4)
                pe.wait_ge(rank_ready, 1)
                passes = pe.value_load(npass_i[0:1, 0:1], min_val=1, max_val=MAX_PASSES)
                with pe.Fori(0, passes) as _p:
                    with pe.Fori(0, PAIRS) as _i:
                        n = pe.snap(u)
                        pe.wait_ge(sel_ready, n + 1)
                        for c in range(DC):
                            for s in range(TT):
                                last = pe.matmul(ps[:, 0, c * 2 * CAP:(c + 1) * 2 * CAP], uN[:, s, c * P:(c + 1) * P],
                                                 sel[:, s].rearrange("p e s -> p (e s)"), start=(s == 0), stop=(s == TT - 1))
                        last.then_inc(xg_done, 1)
                        pe.wait_ge(spread_ready, n * 2 + 2)
                        for s in range(TT):
                            last = pe.transpose(ps[:, 2, s * P:(s + 1) * P],
                                                spread[:, s].rearrange("p e w s -> p (e w s)"), ident)
                        last.then_inc(gt_done, 1)
                        pe.wait_ge(xe_ready, n + 1)
                        for k in range(DC):
                            if k % (DC // 2) == 0:
                                for j in range(4):
                                    pe.wait_ge(up_in[k // (DC // 2)][j], n * 16 + 16)
                            for j in range(4):
                                e = j // 2
                                last = pe.matmul(ps[CAP * j:CAP * (j + 1), 1, :], xe[:, k, e * CAP:(e + 1) * CAP],
                                                 pair_slot(j)[:, k, :], start=(k == 0), stop=(k == DC - 1),
                                                 skip_group_check=True)
                            if k == DC // 2 - 1:
                                last.then_inc(up_half, 1)
                            if k == DC // 2:
                                pe.wait_ge(up_half, n + 1)
                                pe.sem_inc(ups_used, 1)
                                pe.sem_inc(freed[0], EARLY)
                                pe.sem_inc(freed[1], 4 - EARLY)
                        last.then_inc(up_done, 1)
                        pe.wait_ge(up_done, n + 1)
                        pe.sem_inc(ups_used, 1)
                        pe.sem_inc(freed[0], EARLY)
                        pe.sem_inc(freed[1], 4 - EARLY)
                        pe.wait_ge(up_out, n + 1)
                        pe.wait_ge(scat_ready, n + 1)
                        for f in range(FC):
                            last = pe.transpose(ps[:, 2, f * P:(f + 1) * P], up_sb[:, f * P:(f + 1) * P], ident)
                        last.then_inc(upt_done, 1)
                        pe.wait_ge(upt_ready, n + 1)
                        for e in range(2):
                            pe.wait_ge(down_in[e], n * 16 + 16)
                        for f in range(FC):
                            for j in range(4):
                                e, half = j // 2, j % 2
                                w = down_slot(4 + e)
                                last = pe.matmul(ps[CAP * j:CAP * (j + 1), 3, :], up_t[:, f, e, :],
                                                 w[:, f, half * SLAB:(half + 1) * SLAB], start=(f == 0),
                                                 stop=(f == FC - 1), skip_group_check=True)
                        last.then_inc(y_done, 1)
                        pe.wait_ge(y_done, n + 1)
                        pe.sem_inc(freed[1], 2)
                        pe.wait_ge(y_out, n + 1)
                        for s in range(TT):
                            for half in range(HALVES):
                                last = pe.matmul(ps[:, 4 + 2 * s + half, :], scat[:, half, s * P:(s + 1) * P], y_sb,
                                                 start=False, stop=True, skip_group_check=True)
                        last.then_inc(added, 1)
                        pe.reg_add(u, u, 1)
                pe.drain().then_inc(layer_end, 1)
                pe.wait_ge(layer_go, L + 1)


_INS = ["x", "mem", "positions", "norm_mix_g", "w_in", "conv_dw", "conv_db", "conv_ln_g", "conv_ln_b", "w_conv_out",
        "lam_q1", "lam_k1", "lam_q2", "lam_k2", "subln_g", "w_attn_out", "w_out", "norm_mem_g", "norm_x_g", "w_xq",
        "w_xkv", "w_xo", "norm_ffn_g", "w_group", "b_group", "w_router", "b_router", "w1", "w3", "w2", "final_norm_g"]


def kernel(**inputs):
    import concourse.bacc as _bacc
    from concourse.bass_utils import run_bass_kernel_spmd as _run

    nc = _bacc.Bacc("TRN2", target_bir_lowering=False, num_devices=1)
    arrays, args = {}, []
    for name in ["consts"] + _INS:
        a = constants() if name == "consts" else np.ascontiguousarray(inputs[name])
        arrays[f"in_{name}_dram"] = a
        args.append(nc.dram_tensor(f"in_{name}_dram", a.shape, mybir.dt.from_np(a.dtype), kind="ExternalInput").ap())
    o = nc.dram_tensor("out_0_dram", (1, T, D), F32, kind="ExternalOutput").ap()
    encoder(nc, *args, o)
    r = _run(nc, [arrays], core_ids=[0])
    return r.results[0]["out_0_dram"]
```
